# Optimizing a Trainium2 kernel written in Bass

```python
import math
import jax, jax.numpy as jnp
from jax import lax
import numpy as np

D_MODEL = 1024
BATCH = 1
SEQ = 512
DEPTH = 1

CHUNK = 64
Q_BLOCK = 128
HEAD_DIM = 64
N_RET_HEADS = 8
N_FOX_HEADS = 8
RET_WIDTH = N_RET_HEADS * HEAD_DIM
FOX_WIDTH = N_FOX_HEADS * HEAD_DIM
MIX_WIDTH = RET_WIDTH + FOX_WIDTH
N_MEM = 256
N_XATTN_HEADS = 4
XATTN_HEAD_DIM = D_MODEL // N_XATTN_HEADS
D_FF = -(-8 * D_MODEL // (3 * 256)) * 256
ROPE_BASE = 10000.0
EPS = 1e-6
NEG_INF = -1e30
IN_SIZES = (RET_WIDTH, RET_WIDTH, RET_WIDTH, RET_WIDTH, FOX_WIDTH, FOX_WIDTH, FOX_WIDTH, N_FOX_HEADS)
IN_WIDTH = sum(IN_SIZES)


def _split_points(sizes):
    pts, acc = [], 0
    for s in sizes[:-1]:
        acc += s
        pts.append(acc)
    return pts

def rmsnorm(x, g):
    xf = x.astype(jnp.float32)
    y = xf * lax.rsqrt(jnp.mean(xf * xf, axis=-1, keepdims=True) + EPS)
    return (y * g.astype(jnp.float32)).astype(x.dtype)

def head_group_norm(x, g):
    xf = x.astype(jnp.float32)
    mu = jnp.mean(xf, axis=-1, keepdims=True)
    xc = xf - mu
    var = jnp.mean(xc * xc, axis=-1, keepdims=True)
    return (xc * lax.rsqrt(var + EPS) * g.astype(jnp.float32)).astype(x.dtype)

def rotary(x, pos):
    d = x.shape[-1]
    inv_freq = ROPE_BASE ** (-jnp.arange(0, d, 2, dtype=jnp.float32) / d)
    ang = pos[:, None] * inv_freq[None, :]
    cos = jnp.cos(ang)[:, None, :].astype(x.dtype)
    sin = jnp.sin(ang)[:, None, :].astype(x.dtype)
    x1, x2 = x[..., : d // 2], x[..., d // 2:]
    return jnp.concatenate([x1 * cos - x2 * sin, x1 * sin + x2 * cos], axis=-1)

def chunk_retention(q, k, v):
    B, T, H, d = q.shape
    dv = v.shape[-1]
    nc = T // CHUNK
    dt = q.dtype
    log_g = jnp.log(1.0 - 2.0 ** (-5.0 - jnp.arange(H, dtype=jnp.float32)))
    idx = jnp.arange(CHUNK, dtype=jnp.float32)
    intra_decay = jnp.exp(log_g[:, None, None] * jnp.abs(idx[:, None] - idx[None, :])).astype(dt)
    q_decay = jnp.exp(log_g[None, :] * (idx[:, None] + 1.0)).astype(dt)
    k_decay = jnp.exp(log_g[None, :] * (CHUNK - 1.0 - idx[:, None])).astype(dt)
    chunk_decay = jnp.exp(log_g * CHUNK).astype(dt)[:, None, None]

    qc = (q * (d ** -0.5)).reshape(B, nc, CHUNK, H, d)
    kc = k.reshape(B, nc, CHUNK, H, d)
    vc = v.reshape(B, nc, CHUNK, H, dv)

    scores = jnp.einsum('bnihd,bnjhd->bnhij', qc, kc) * intra_decay
    intra = jnp.einsum('bnhij,bnjhe->bnihe', scores, vc)

    kv = jnp.einsum('bnjhd,bnjhe->nbhde', kc * k_decay[:, :, None], vc)

    def step(state, kv_c):
        return state * chunk_decay + kv_c, state

    _, s_prev = lax.scan(step, jnp.zeros((B, H, d, dv), kv.dtype), kv)
    inter = jnp.einsum('bnihd,nbhde->bnihe', qc * q_decay[:, :, None], s_prev)
    return (intra + inter).reshape(B, T, H, dv)

def forgetting_attention(q, k, v, log_f):
    B, T, H, d = q.shape
    F = jnp.cumsum(log_f, axis=1).transpose(0, 2, 1)
    qh = (q * (d ** -0.5)).transpose(0, 2, 1, 3)
    kh = k.transpose(0, 2, 1, 3)
    vh = v.transpose(0, 2, 1, 3)
    qpos = jnp.arange(Q_BLOCK)
    outs = []
    for blk in range(T // Q_BLOCK):
        q0 = blk * Q_BLOCK
        kend = q0 + Q_BLOCK
        logits = jnp.einsum('bhqd,bhkd->bhqk', qh[:, :, q0:kend], kh[:, :, :kend]).astype(jnp.float32)
        logits = logits + F[:, :, q0:kend, None] - F[:, :, None, :kend]
        causal = (q0 + qpos)[:, None] >= jnp.arange(kend)[None, :]
        logits = jnp.where(causal, logits, NEG_INF)
        p = jax.nn.softmax(logits, axis=-1).astype(v.dtype)
        outs.append(jnp.einsum('bhqk,bhkd->bhqd', p, vh[:, :, :kend]))
    return jnp.concatenate(outs, axis=2).transpose(0, 2, 1, 3)

def memory_cross_attention(hn, mem, w_xq, w_xkv, g_mem, g_xq, g_xk, w_xo):
    B, T, _ = hn.shape
    M = mem.shape[1]
    q = (hn @ w_xq).reshape(B, T, N_XATTN_HEADS, XATTN_HEAD_DIM)
    q = rmsnorm(q, g_xq)
    kv = rmsnorm(mem, g_mem) @ w_xkv
    k, v = jnp.split(kv, 2, axis=-1)
    k = rmsnorm(k.reshape(B, M, N_XATTN_HEADS, XATTN_HEAD_DIM), g_xk)
    v = v.reshape(B, M, N_XATTN_HEADS, XATTN_HEAD_DIM)
    logits = jnp.einsum('bthd,bmhd->bhtm', q, k).astype(jnp.float32) * (XATTN_HEAD_DIM ** -0.5)
    p = jax.nn.softmax(logits, axis=-1).astype(v.dtype)
    o = jnp.einsum('bhtm,bmhd->bthd', p, v).reshape(B, T, D_MODEL)
    return o @ w_xo

def first_inputs(seed: int = 0) -> dict:
    key = jax.random.key(seed)
    ks = jax.random.split(key, 24)
    f32 = jnp.float32
    D = D_MODEL

    def w(k, shape, fan_in):
        return jax.random.normal(k, shape, f32) * fan_in ** -0.5

    def gain(k, shape):
        return 1.0 + 0.02 * jax.random.normal(k, shape, f32)

    return {
        "x": jax.random.normal(ks[0], (BATCH, SEQ, D), f32),
        "mem": jax.random.normal(ks[1], (BATCH, N_MEM, D), f32),
        "g_mix": gain(ks[2], (DEPTH, D)),
        "w_in": w(ks[3], (DEPTH, D, IN_WIDTH), D),
        "b_forget": jax.random.uniform(ks[4], (DEPTH, N_FOX_HEADS), f32, 1.0, 4.0),
        "g_ret_out": gain(ks[5], (DEPTH, N_RET_HEADS, HEAD_DIM)),
        "g_fox_q": gain(ks[6], (DEPTH, HEAD_DIM)),
        "g_fox_k": gain(ks[7], (DEPTH, HEAD_DIM)),
        "w_out": w(ks[8], (DEPTH, MIX_WIDTH, D), MIX_WIDTH),
        "g_xattn": gain(ks[9], (DEPTH, D)),
        "w_xq": w(ks[10], (DEPTH, D, D), D),
        "w_xkv": w(ks[11], (DEPTH, D, 2 * D), D),
        "g_mem": gain(ks[12], (DEPTH, D)),
        "g_xq": gain(ks[13], (DEPTH, XATTN_HEAD_DIM)),
        "g_xk": gain(ks[14], (DEPTH, XATTN_HEAD_DIM)),
        "w_xo": w(ks[15], (DEPTH, D, D), D),
        "g_ffn": gain(ks[16], (DEPTH, D)),
        "w_gate": w(ks[17], (DEPTH, D, D_FF), D),
        "w_up": w(ks[18], (DEPTH, D, D_FF), D),
        "w_down": w(ks[19], (DEPTH, D_FF, D), D_FF),
    }

def first_block(x, mem, g_mix, w_in, b_forget, g_ret_out, g_fox_q, g_fox_k, w_out,
              g_xattn, w_xq, w_xkv, g_mem, g_xq, g_xk, w_xo,
              g_ffn, w_gate, w_up, w_down):
    B, T, _ = x.shape
    pos = jnp.arange(T, dtype=jnp.float32)
    splits = _split_points(IN_SIZES)
    h = x
    for l in range(DEPTH):
        hn = rmsnorm(h, g_mix[l])
        proj = hn @ w_in[l]
        rq, rk, rv, rg, fq, fk, fv, ff = jnp.split(proj, splits, axis=-1)

        rq = rotary(rq.reshape(B, T, N_RET_HEADS, HEAD_DIM), pos)
        rk = rotary(rk.reshape(B, T, N_RET_HEADS, HEAD_DIM), pos)
        ret = chunk_retention(rq, rk, rv.reshape(B, T, N_RET_HEADS, HEAD_DIM))
        ret = head_group_norm(ret, g_ret_out[l]).reshape(B, T, RET_WIDTH)
        ret = jax.nn.silu(rg) * ret

        fq = rmsnorm(fq.reshape(B, T, N_FOX_HEADS, HEAD_DIM), g_fox_q[l])
        fk = rmsnorm(fk.reshape(B, T, N_FOX_HEADS, HEAD_DIM), g_fox_k[l])
        log_f = jax.nn.log_sigmoid(ff.astype(jnp.float32) + b_forget[l].astype(jnp.float32))
        fox = forgetting_attention(fq, fk, fv.reshape(B, T, N_FOX_HEADS, HEAD_DIM), log_f)
        fox = fox.reshape(B, T, FOX_WIDTH)

        h = h + jnp.concatenate([ret, fox], axis=-1) @ w_out[l]

        h = h + memory_cross_attention(rmsnorm(h, g_xattn[l]), mem, w_xq[l], w_xkv[l],
                                       g_mem[l], g_xq[l], g_xk[l], w_xo[l])

        hn = rmsnorm(h, g_ffn[l])
        h = h + (jax.nn.silu(hn @ w_gate[l]) * (hn @ w_up[l])) @ w_down[l]
    return h


D_CONV = D_MODEL
CONV_K = 3
N_HEADS = D_MODEL // HEAD_DIM
N_KV_HEADS = 4
GROUP = N_HEADS // N_KV_HEADS
D_ATTN = N_HEADS * HEAD_DIM
D_KV = N_KV_HEADS * HEAD_DIM
WINDOW = 128
BLOCK = 128
ROPE_THETA = 10000.0
D_FF_2 = 2816
N_MOD = 9
ADA_INIT = 0.5
NEG_INF_2 = -1e30

IN_SPLITS = [D_CONV, D_CONV, D_CONV, D_ATTN, D_KV, D_KV, D_MODEL, D_MODEL]
IN_OFFSETS = [int(o) for o in np.cumsum(IN_SPLITS)[:-1]]
D_IN = int(sum(IN_SPLITS))


def rms_norm(x, g):
    xf = x.astype(jnp.float32)
    y = xf * lax.rsqrt(jnp.mean(xf * xf, axis=-1, keepdims=True) + EPS)
    return (y * g.astype(jnp.float32)).astype(x.dtype)

def modulate(h, shift, scale):
    return h * (1 + scale[:, None, :]) + shift[:, None, :]

def swiglu(h, w_gu, w_down):
    a, b = jnp.split(h @ w_gu, 2, axis=-1)
    return (jax.nn.silu(a) * b) @ w_down

def rope_tables(seq):
    inv = 1.0 / (ROPE_THETA ** (jnp.arange(0, HEAD_DIM, 2, dtype=jnp.float32) / HEAD_DIM))
    ang = jnp.arange(seq, dtype=jnp.float32)[:, None] * inv[None, :]
    return jnp.cos(ang), jnp.sin(ang)

def apply_rope(t, cos, sin):
    t1, t2 = jnp.split(t.astype(jnp.float32), 2, axis=-1)
    c = cos[None, :, None, :]
    s = sin[None, :, None, :]
    return jnp.concatenate([t1 * c - t2 * s, t2 * c + t1 * s], axis=-1).astype(t.dtype)

def short_conv(u, w):
    s = u.shape[1]
    up = jnp.pad(u, ((0, 0), (CONV_K - 1, 0), (0, 0)))
    out = up[:, 0:s] * w[0]
    for j in range(1, CONV_K):
        out = out + up[:, j:j + s] * w[j]
    return out

def sliding_window_attention(q, k, v, sinks):
    bsz, s, _, _ = q.shape
    nb = s // BLOCK
    qb = q.reshape(bsz, nb, BLOCK, N_KV_HEADS, GROUP, HEAD_DIM)

    def band(t):
        tp = jnp.pad(t, ((0, 0), (BLOCK, 0), (0, 0), (0, 0)))
        tp = tp.reshape(bsz, nb + 1, BLOCK, N_KV_HEADS, HEAD_DIM)
        return jnp.concatenate([tp[:, :-1], tp[:, 1:]], axis=2)

    kb, vb = band(k), band(v)
    scores = jnp.einsum('bnqhgd,bnkhd->bnhgqk', qb, kb,
                        preferred_element_type=jnp.float32) * (HEAD_DIM ** -0.5)
    qi = jnp.arange(BLOCK)[:, None]
    kj = jnp.arange(2 * BLOCK)[None, :]
    diff = BLOCK + qi - kj
    in_window = (diff >= 0) & (diff < WINDOW)
    k_pos = (jnp.arange(nb)[:, None] - 1) * BLOCK + jnp.arange(2 * BLOCK)[None, :]
    valid = in_window[None] & (k_pos >= 0)[:, None, :]
    scores = jnp.where(valid[None, :, None, None], scores, NEG_INF_2)
    sink = sinks.astype(jnp.float32).reshape(N_KV_HEADS, GROUP)[None, None, :, :, None, None]
    m = jnp.maximum(jnp.max(scores, axis=-1, keepdims=True), sink)
    p = jnp.exp(scores - m)
    denom = jnp.sum(p, axis=-1, keepdims=True) + jnp.exp(sink - m)
    probs = (p / denom).astype(v.dtype)
    out = jnp.einsum('bnhgqk,bnkhd->bnqhgd', probs, vb)
    return out.reshape(bsz, s, D_ATTN)

def second_inputs(seed: int = 0) -> dict:
    key = jax.random.key(seed)
    ks = jax.random.split(key, 24)
    f32 = jnp.float32

    def nrm(k, shape, fan_in, mult=1.0):
        return jax.random.normal(k, shape, f32) * (mult * fan_in ** -0.5)

    def gain(k, shape):
        return 1.0 + 0.05 * jax.random.normal(k, shape, f32)

    L = DEPTH
    return {
        "x": jax.random.normal(ks[0], (BATCH, SEQ, D_MODEL), f32),
        "c": jax.random.normal(ks[1], (BATCH, D_MODEL), f32),
        "w_ada": nrm(ks[2], (L, D_MODEL, N_MOD * D_MODEL), D_MODEL, ADA_INIT),
        "b_ada": 0.02 * jax.random.normal(ks[3], (L, N_MOD * D_MODEL), f32),
        "g_ffn1": gain(ks[4], (L, D_MODEL)),
        "w1_gu": nrm(ks[5], (L, D_MODEL, 2 * D_FF_2), D_MODEL),
        "w1_down": nrm(ks[6], (L, D_FF_2, D_MODEL), D_FF_2),
        "g_mix": gain(ks[7], (L, D_MODEL)),
        "w_in": nrm(ks[8], (L, D_MODEL, D_IN), D_MODEL),
        "conv_w": nrm(ks[9], (L, CONV_K, D_CONV), CONV_K),
        "w_conv_proj": nrm(ks[10], (L, D_CONV, D_MODEL), D_CONV),
        "w_attn_proj": nrm(ks[11], (L, D_ATTN, D_MODEL), D_ATTN),
        "sinks": jax.random.normal(ks[12], (L, N_HEADS), f32),
        "w_out": nrm(ks[13], (L, D_MODEL, D_MODEL), D_MODEL),
        "g_ffn2": gain(ks[14], (L, D_MODEL)),
        "w2_gu": nrm(ks[15], (L, D_MODEL, 2 * D_FF_2), D_MODEL),
        "w2_down": nrm(ks[16], (L, D_FF_2, D_MODEL), D_FF_2),
        "g_final": gain(ks[17], (D_MODEL,)),
    }

def second_block(x, c, w_ada, b_ada, g_ffn1, w1_gu, w1_down, g_mix, w_in, conv_w,
              w_conv_proj, w_attn_proj, sinks, w_out, g_ffn2, w2_gu, w2_down, g_final):
    bsz, s, _ = x.shape
    cos, sin = rope_tables(s)
    c_act = jax.nn.silu(c)
    for l in range(DEPTH):
        mods = jnp.split(c_act @ w_ada[l] + b_ada[l], N_MOD, axis=-1)
        sh1, sc1, gt1, sh2, sc2, gt2, sh3, sc3, gt3 = mods

        h = modulate(rms_norm(x, g_ffn1[l]), sh1, sc1)
        x = x + 0.5 * gt1[:, None, :] * swiglu(h, w1_gu[l], w1_down[l])

        h = modulate(rms_norm(x, g_mix[l]), sh2, sc2)
        proj = h @ w_in[l]
        b_g, c_g, u, q, k, v, z_conv, z_attn = jnp.split(proj, IN_OFFSETS, axis=-1)

        y_conv = (b_g * short_conv(c_g * u, conv_w[l])) @ w_conv_proj[l]

        q = apply_rope(q.reshape(bsz, s, N_HEADS, HEAD_DIM), cos, sin)
        k = apply_rope(k.reshape(bsz, s, N_KV_HEADS, HEAD_DIM), cos, sin)
        v = v.reshape(bsz, s, N_KV_HEADS, HEAD_DIM)
        y_attn = sliding_window_attention(q, k, v, sinks[l]) @ w_attn_proj[l]

        merged = jax.nn.sigmoid(z_conv) * y_conv + jax.nn.sigmoid(z_attn) * y_attn
        x = x + gt2[:, None, :] * (merged @ w_out[l])

        h = modulate(rms_norm(x, g_ffn2[l]), sh3, sc3)
        x = x + 0.5 * gt3[:, None, :] * swiglu(h, w2_gu[l], w2_down[l])

    return rms_norm(x, g_final)


def setup_inputs(seed=0):
    out = dict(first_inputs(seed))
    for name, value in second_inputs(seed + 1).items():
        if name != "x":
            out[name + "_2"] = value
    return out


def reference(
    x, mem, g_mix, w_in, b_forget, g_ret_out, g_fox_q, g_fox_k, w_out, g_xattn, w_xq, w_xkv,
    g_mem, g_xq, g_xk, w_xo, g_ffn, w_gate, w_up, w_down, c_2, w_ada_2, b_ada_2, g_ffn1_2,
    w1_gu_2, w1_down_2, g_mix_2, w_in_2, conv_w_2, w_conv_proj_2, w_attn_proj_2, sinks_2,
    w_out_2, g_ffn2_2, w2_gu_2, w2_down_2, g_final_2,
):
    x = first_block(
        x, mem, g_mix, w_in, b_forget, g_ret_out, g_fox_q, g_fox_k, w_out, g_xattn, w_xq, w_xkv,
        g_mem, g_xq, g_xk, w_xo, g_ffn, w_gate, w_up, w_down,
    )
    return second_block(
        x, c_2, w_ada_2, b_ada_2, g_ffn1_2, w1_gu_2, w1_down_2, g_mix_2, w_in_2, conv_w_2,
        w_conv_proj_2, w_attn_proj_2, sinks_2, w_out_2, g_ffn2_2, w2_gu_2, w2_down_2, g_final_2,
    )


_drawn_inputs = setup_inputs


def setup_inputs(seed=0):
    import zlib

    import numpy as np

    out = dict(_drawn_inputs(seed))
    spreads = {}
    factors = {'g_mix': 2.786,
     'g_ret_out': 6.485,
     'g_fox_q': 8.0,
     'g_fox_k': 8.0,
     'g_xattn': 8.0,
     'g_mem': 8.0,
     'g_xq': 8.0,
     'g_xk': 8.0,
     'g_ffn': 4.097,
     'b_ada_2': 3.341,
     'g_ffn1_2': 8.0,
     'g_mix_2': 3.905,
     'sinks_2': 8.0,
     'g_ffn2_2': 8.0}
    for name, (base, spread) in spreads.items():
        noise = np.random.default_rng([zlib.crc32(name.encode()), seed]).standard_normal(out[name].shape)
        drawn = base * np.exp(spread * noise) if base else spread * noise
        out[name] = __import__('jax').numpy.asarray(drawn.astype(out[name].dtype))
    for name, factor in factors.items():
        out[name] = (out[name] * factor).astype(out[name].dtype)
    return out
```

```python
from contextlib import ExitStack

import numpy as np
import concourse.bass as bass
from concourse import mybir

D = 1024
T = 512
M = 256
P = 128
C = D // P
QB = T // P
FF = 2816
FC = FF // P
HD = 64
CHUNK = 64
NRET = 8
NFOX = 8
NX = 4
NSW = 16
NKV = 4
NMOD = 9
EPS = 1e-6
NEG = -1e30
UNIT = 8 * P
ADA_G = 12
ADA_W = NMOD * D // ADA_G
ADA_B = ADA_W // P


class Layer:

    def __init__(self, name, u0, n, per):
        self.name, self.u0, self.n, self.per = name, u0, n, per
        self.groups = n // per


def plan_layers():
    shape = [("xk", 8, 1), ("xv", 8, 1), ("fq", 4, 1), ("fk", 4, 1), ("rq", 4, 1), ("rk", 4, 1), ("rv", 4, 1),
             ("rg", 4, 1), ("fv", 4, 1), ("ff", 1, 1), ("out", 8, 1), ("xq", 8, 1), ("xo", 8, 1),
             ("gu", 2 * FC, 2), ("down", FC, 1), ("gu1", 2 * FC, 2), ("down1", FC, 1),
             ("cu", 16, 2), ("qkv", 12, 1), ("b", 8, 1), ("cz", 16, 2), ("az", 16, 2), ("out2", 8, 1),
             ("gu2", 2 * FC, 2), ("down2", FC, 1)]
    layers, u = {}, 0
    for name, n, per in shape:
        layers[name] = Layer(name, u, n, per)
        u += n
    return layers, u


LAYERS, UNITS = plan_layers()


def bases(names):
    out, at = {}, 0
    for name in names:
        out[name] = at
        at += 8 if name.startswith("down") else LAYERS[name].groups
    return out


COPIED = bases(["xk", "xv", "fq", "fk", "rq", "rk", "rv", "rg", "fv", "ff", "xq", "qkv"])
RESID = bases(["out", "xo", "down", "down1", "out2", "down2"])
PROD = bases(["gu", "gu1", "cu", "b", "cz", "az", "gu2"])
ACTED = bases(["gu", "gu1", "cu", "cz", "az", "gu2"])
HALVES = bases(["gu", "gu1", "b", "az", "gu2"])
NORMS = {n: i for i, n in enumerate(["mem", "mix", "xattn", "ffn", "ffn1_2", "mix_2", "ffn2_2", "final"])}

VEC = {}
for _name, _n in [("g_mem", 8), ("g_mix", 8), ("g_xattn", 8), ("g_ffn", 8), ("g_ffn1_2", 8), ("g_mix_2", 8),
                  ("g_ffn2_2", 8), ("g_final", 8), ("g_ret_out", 4), ("g_fox_q", 1), ("g_fox_k", 1), ("g_xq", 2),
                  ("g_xk", 2), ("b_forget", 1), ("conv", 24), ("c", 8), ("b_ada", 72), ("sinks", 16), ("eps", 1),
                  ("one", 1), ("head_mask", 8)]:
    VEC[_name] = (sum(n for _, n in VEC.values()), _n)
NVEC = sum(n for _, n in VEC.values())
TAB = {}
for _name, _n in [("ident", P), ("rot", P), ("mean_d", P), ("mean_head", P), ("mean_256", P), ("window", 2 * P),
                  ("cos", T), ("sin", T)]:
    TAB[_name] = (sum(n for _, n in TAB.values()), _n)
NTAB = sum(n for _, n in TAB.values())

FOX_GROUPS = [(3, 0, 0, 512, 768), (2, 1, 0, 384, 384), (0, 1, 384, 128, 0), (1, 2, 0, 256, 128)]
XAT_GROUPS = [(q, q // 2, q % 2 * M, M, q * M) for q in range(QB)]
SWA_GROUPS = [(0, 0, 0, 128, 0), (1, 0, 128, 256, 128), (2, 1, 0, 256, 384), (3, 1, 256, 256, 640)]
CAUSAL_KEYS = [(0, 0, 0), (1, 0, 512), (2, 0, 1024), (1, 384, 896)]
SWA_PAIRS = [(0, 0), (1, 0), (1, 1), (2, 1), (2, 2), (3, 2), (3, 3)]


def two_block_kernel(nc, x_t, mem_t, units, w_ada, vectors, tables, decays, out_t):
    f32, f32r = mybir.dt.float32, mybir.dt.float32r
    ALU, ACT, AX = mybir.AluOpType, mybir.ActivationFunctionType, mybir.AxisListType
    L = LAYERS

    with ExitStack() as ctx:
        def sb(name, cols, dt=f32):
            return ctx.enter_context(nc.sbuf_tensor(name, [P, cols], dt))

        def sem(name):
            return ctx.enter_context(nc.semaphore(name))

        h = sb("h", C * T)
        xh, xl = sb("xh", C * T, f32r), sb("xl", C * T, f32r)
        raw, whi, wlo = sb("raw", 4 * UNIT), sb("whi", 2 * UNIT, f32r), sb("wlo", 2 * UNIT, f32r)
        tmp = sb("tmp", 4 * T)
        xn = sb("xn", 2 * T)
        root, rstd = sb("root", T), sb("rstd", T)
        tab = sb("tab", NTAB)
        vec = sb("vec", NVEC)
        mx, nm, sm, rs, es = (sb(n, 64) for n in ("mx", "nm", "sm", "rs", "es"))
        mods = sb("mods", NMOD * C)
        gmod = sb("gmod", 6 * C + 1 + C)
        arena_kb = 88
        side = sb("side", 12 * 256)
        arena = sb("arena", arena_kb * 256)

        end = nc.sbuf_base
        arena_at = end - arena_kb * 1024
        side_at = arena_at - 12 * 1024

        def at(name, kb, cols, dt=f32, base=arena_at):
            return nc.alloc_sbuf_tensor_at(name, [P, cols], dt, offset=base + int(kb * 1024))

        PR = {"fq": 0, "fk": 4, "rq": 8, "rk": 12, "rv": 16, "rg": 20, "fv": 24}
        proj = at("proj", 0, 28 * T)
        mem_in = at("mem_in", 0, C * M)
        vmem_f = at("vmem_f", 48, C * M)
        memh, meml = at("memh", 56, C * M, f32r), at("meml", 64, C * M, f32r)
        v_ret, v_fox = at("v_ret", 56, QB * T), at("v_fox", 64, QB * T)
        kmem, vmem = at("kmem", 72, C * M), at("vmem", 80, C * M)
        pt_a, pt_b = at("pt_a", 32, 1280), at("pt_b", 48, 1280)
        xq = at("xq", 0, C * T)
        hh, hl = at("hh", 0, FC * T, f32r), at("hl", 44, FC * T, f32r)
        yh, yl = at("yh", 0, C * T, f32r), at("yl", 16, C * T, f32r)
        conv = at("conv", 32, C * T)
        m1 = at("m1", 32, C * T)
        qkv = at("qkv", 48, 12 * T)
        kdup = at("kdup", 72, NKV * T)
        v_sw = at("v_sw", 80, QB * 256)
        p_sw = at("p_sw", 84, 896)
        mh, ml = at("mh", 48, C * T, f32r), at("ml", 64, C * T, f32r)
        lt = at("lt", 0, T, base=side_at)
        rb = at("rb", 2, T, base=side_at)
        rh = at("rh", 4, 2 * T, base=side_at)
        dec = at("dec", 8, 2 * T, base=side_at)
        ada_w = at("ada_w", 0, 4 * ADA_W, base=side_at)
        cpad = at("cpad", 0, 2 * 514, base=side_at)
        pt_sw = at("pt_sw", 5, 896, base=side_at)

        acc = xn

        banks = [ctx.enter_context(nc.psum_tensor(f"bank{i}", [P, T], f32)) for i in range(8)]

        def chunk(t, c, n=T):
            return t[:, c * n:(c + 1) * n] if isinstance(c, int) else t[:, bass.ds(c * n, n)]

        def table(name):
            o, n = TAB[name]
            return tab[:, o:o + n]

        def col(name, c=0, rows=slice(None)):
            o = VEC[name][0] + c
            return vec[rows, o:o + 1] if isinstance(o, int) else vec[rows, bass.ds(o, 1)]

        def mod(m, c):
            o = m * C + c
            return mods[:, o:o + 1] if isinstance(o, int) else mods[:, bass.ds(o, 1)]

        def gm(m, c):
            return gmod[:, m * C + c:m * C + c + 1]
        gq8 = gmod[:, 6 * C:6 * C + 1]
        csilu = gmod[:, 6 * C + 1:7 * C + 1]

        ident, mean_d, mean_head, mean_256 = (table(n) for n in ("ident", "mean_d", "mean_head", "mean_256"))

        consts_in, mem_loaded, x_loaded = sem("consts_in"), sem("mem_loaded"), sem("x_loaded")
        raw_loaded = [sem(f"raw_loaded{i}") for i in range(4)]
        hi_ready, lo_ready, unit_used = sem("hi_ready"), sem("lo_ready"), sem("unit_used")
        copied, resid = sem("copied"), sem("resid")
        prod, acted, half_hi, half_lo = sem("prod"), sem("acted"), sem("half_hi"), sem("half_lo")
        convolved, merged = sem("convolved"), sem("merged")
        norm_sq, norm_sum, norm_root, norm_rstd = (sem(n) for n in ("norm_sq", "norm_sum", "norm_root", "norm_rstd"))
        norm_xn, norm_hi, norm_lo = sem("norm_xn"), sem("norm_hi"), sem("norm_lo")
        setup_done = sem("setup_done")
        vmem_tr, vmem_copied = sem("vmem_tr"), sem("vmem_copied")
        kmem_sq, kmem_sum, kmem_root, kmem_rstd, kmem_done = (
            sem(n) for n in ("kmem_sq", "kmem_sum", "kmem_root", "kmem_rstd", "kmem_done"))
        hn_sq, hn_sum, hn_root, hn_rstd, hn_done = (sem(n) for n in ("hn_sq", "hn_sum", "hn_root", "hn_rstd", "hn_done"))
        rope_rot, rope_sin, rope_cos, rope_done = (sem(n) for n in ("rope_rot", "rope_sin", "rope_cos", "rope_done"))
        v_tr, v_copied = sem("v_tr"), sem("v_copied")
        gate_act, gate_dve, f_ready = sem("gate_act"), sem("gate_dve"), sem("f_ready")
        dec_in = [sem("dec_in0"), sem("dec_in1")]
        ret_scores, ret_weighted, ret_pv, ret_out = (sem(n) for n in ("ret_scores", "ret_weighted", "ret_pv", "ret_out"))
        gn_mean, gn_xc, gn_sq, gn_var, gn_root = (sem(n) for n in ("gn_mean", "gn_xc", "gn_sq", "gn_var", "gn_root"))
        gn_rstd, gn_t, gn_y, gn_hi, gn_lo = (sem(n) for n in ("gn_rstd", "gn_t", "gn_y", "gn_hi", "gn_lo"))
        rh_ready = sem("rh_ready")

        class Kind:

            def __init__(self, name, heads, groups, p, pt, scale, key_banks, out_hi, out_lo, out_chunk0):
                self.heads, self.groups, self.p, self.pt, self.scale = heads, groups, p, pt, scale
                self.key_banks = key_banks
                self.out_hi, self.out_lo, self.out_chunk0 = out_hi, out_lo, out_chunk0
                self.s_scores, self.s_max = sem(name + "_scores"), sem(name + "_max")
                self.s_sinkmax, self.s_negmax = sem(name + "_sinkmax"), sem(name + "_negmax")
                self.s_exp, self.s_sink = sem(name + "_exp"), sem(name + "_sink")
                self.s_sum, self.s_recip, self.s_pn = sem(name + "_sum"), sem(name + "_recip"), sem(name + "_pn")
                self.s_tr, self.s_pt_act, self.s_pt_dve = sem(name + "_tr"), sem(name + "_pt_act"), sem(name + "_pt_dve")
                self.s_pv, self.s_hi, self.s_lo = sem(name + "_pv"), sem(name + "_hi"), sem(name + "_lo")

        fox = Kind("fox", NFOX, FOX_GROUPS, pt_a, pt_b, 1.0, [(3, 512, 0), (4, 512, 512), (5, 256, 1024)], xh, xl, 4)
        xat = Kind("xat", NX, XAT_GROUPS, pt_a, pt_b, 256.0 ** -0.5, [(3, 512, 0), (4, 512, 512)], xh, xl, 0)
        swa = Kind("swa", NSW, SWA_GROUPS, p_sw, pt_sw, HD ** -0.5, [(3, 512, 0), (4, 384, 512)], yh, yl, 0)

        qn_sq, qn_sum, qn_root, qn_rstd, qn_done = (sem(n) for n in ("qn_sq", "qn_sum", "qn_root", "qn_rstd", "qn_done"))
        ada_in = [sem(f"ada_in{i}") for i in range(4)]
        csilu_done, ada_step, ada_sum, mods_done = sem("csilu_done"), sem("ada_step"), sem("ada_sum"), sem("mods_done")
        kdup_in, vsw_tr, vsw_copied = sem("kdup_in"), sem("vsw_tr"), sem("vsw_copied")
        final_done, stored = sem("final_done"), sem("stored")
        down_names = ("down", "down1", "down2")

        block = ctx.enter_context(nc.Block())

        def repeat(eng, n, body):
            if n:
                body(0, True)
            if n - 1 >= 2:
                with eng.Fori(1, n) as i:
                    body(i, False)
            elif n == 2:
                body(1, False)

        @block.sync
        def _(sp):
            def load_unit(u, slot, first=False):
                if not first:
                    sp.wait_ge(lo_ready, u - 3)
                sp.dma_start(raw[:, slot * UNIT:(slot + 1) * UNIT],
                             units[u, :, :] if isinstance(u, int) else
                             units[bass.ds(u, 1), :, :].rearrange("a p n -> (a p) n")).then_inc(raw_loaded[slot], 16)

            def load_ada(g, k, first=False):
                slot = k % 4
                if not (first and k < 4):
                    sp.wait_ge(ada_step, g * 8 + k - 3)
                if first and k == 0:
                    sp.wait_ge(fox.s_pv, NFOX)
                cols = slice(g * ADA_W, (g + 1) * ADA_W) if isinstance(g, int) else bass.ds(g * ADA_W, ADA_W)
                sp.dma_start(ada_w[:, slot * ADA_W:(slot + 1) * ADA_W],
                             w_ada[k * P:(k + 1) * P, cols]).then_inc(ada_in[slot], 16)

            for u in range(4):
                load_unit(u, u, True)
            gu0 = L["gu"].u0
            lead = gu0 // 4 * 4
            with sp.Fori(1, lead // 4) as i:
                for j in range(4):
                    load_unit(4 * i + j, j)
            u = lead
            for _ in range(4):
                load_unit(u, u % 4)
                u += 1

            def round_with_ada(i, first):
                for j in range(4):
                    load_unit(lead + 4 + 4 * i + j, j)
                    load_ada(i, 2 * j, first)
                    load_ada(i, 2 * j + 1, first)
            repeat(sp, 11, round_with_ada)
            u = lead + 4 + 44
            for j in range(4):
                load_unit(u + j, j)
                load_ada(11, 2 * j)
                load_ada(11, 2 * j + 1)
            u += 4
            rounds = (UNITS - u) // 4
            with sp.Fori(0, rounds) as i:
                for j in range(4):
                    load_unit(u + 4 * i + j, j)
            for v in range(u + 4 * rounds, UNITS):
                load_unit(v, v % 4)
            for c in range(C):
                sp.wait_ge(final_done, c + 1)
                sp.dma_start(out_t[c * P:(c + 1) * P, :], chunk(h, c)).then_inc(stored, 16)
            sp.wait_ge(stored, 16 * C)

        @block.gpsimd
        def _(pool):
            def low_part(u, j):
                pool.wait_ge(hi_ready, u + 1)
                pool.tensor_tensor(wlo[:, j % 2 * UNIT:(j % 2 + 1) * UNIT], raw[:, j * UNIT:(j + 1) * UNIT],
                                   whi[:, j % 2 * UNIT:(j % 2 + 1) * UNIT].bitcast(f32), ALU.subtract).then_inc(lo_ready, 1)

            with pool.Fori(0, UNITS // 4) as i:
                for j in range(4):
                    low_part(4 * i + j, j)
            for v in range(UNITS // 4 * 4, UNITS):
                low_part(v, v % 4)

        @block.scalar
        def _(act):
            def high_part(u0, i, j):
                v = u0 + j
                if isinstance(i, int) and v + 4 * i >= UNITS:
                    return
                slot = v % 4
                act.wait_ge(raw_loaded[slot], 16 * (v // 4 + 1) + 16 * i)
                if not (isinstance(i, int) and v + 4 * i < 2):
                    act.wait_ge(unit_used, v - 1 + 4 * i)
                act.activation(whi[:, v % 2 * UNIT:(v % 2 + 1) * UNIT], raw[:, slot * UNIT:(slot + 1) * UNIT],
                               ACT.Copy).then_inc(hi_ready, 1)

            def run_layer(name, epilogue):
                lay = L[name]

                def body(i, first):
                    for j in range(4):
                        high_part(lay.u0, i, j + 1)
                        if (j + 1) % lay.per == 0:
                            act.wait_ge(unit_used, lay.u0 + j + 1 + 4 * i)
                            g = (4 * i + j) // lay.per if isinstance(i, int) else (
                                4 * i + j if lay.per == 1 else 2 * i + j // 2)
                            epilogue(g, j)
                repeat(act, lay.n // 4, body)
                for r in range(lay.n // 4 * 4, lay.n):
                    high_part(lay.u0, 0, r + 1)
                    act.wait_ge(unit_used, lay.u0 + r + 1)
                    epilogue(r, r % 4)

            def run_split_only(name):
                lay = L[name]

                def body(i, first):
                    for j in range(4):
                        high_part(lay.u0, i, j + 1)
                repeat(act, lay.n // 4, body)
                for r in range(lay.n // 4 * 4, lay.n):
                    high_part(lay.u0, 0, r + 1)

            def copy_to(dest, c0, n, func=ACT.Copy):
                def epilogue(g, j):
                    act.activation(chunk(dest, c0 + g, n), banks[j][:, 0:n], func).then_inc(copied, 1)
                return epilogue

            def norm(name, src, dst, n, shift=None, ready=None):
                b = 8 * NORMS[name]
                for c in range(C):
                    if ready:
                        act.wait_ge(ready[0], ready[1] + (c + 1 if ready[2] else 0))
                    if c >= 4:
                        act.wait_ge(norm_sum, b + c - 3)
                    act.activation(tmp[:, c % 4 * T:c % 4 * T + n], chunk(src, c, n), ACT.Square).then_inc(norm_sq, 1)
                act.wait_ge(norm_sum, b + C)
                act.activation(root[:, 0:n], banks[7 if name != "mem" else 6][:, 0:n], ACT.Sqrt,
                               bias=col("eps")).then_inc(norm_root, 1)
                if dst is None:
                    return
                for c in range(C):
                    act.wait_ge(norm_xn, b + c + 1)
                    if shift is None:
                        act.activation(chunk(dst, c, n), xn[:, c % 2 * T:c % 2 * T + n], ACT.Copy).then_inc(norm_hi, 1)
                    else:
                        act.activation(chunk(dst, c, n), xn[:, c % 2 * T:c % 2 * T + n], ACT.Identity,
                                       bias=mod(shift, c)).then_inc(norm_hi, 1)

            def head_squares(src, c0, b, tmp_free):
                act.wait_ge(*tmp_free)
                for c in range(4):
                    act.activation(chunk(tmp, c), chunk(src, c0 + c), ACT.Square).then_inc(hn_sq, 1)

            def head_roots(b):
                for c in range(4):
                    act.wait_ge(hn_sum, b + c + 1)
                    act.activation(banks[4 + c][:, :], banks[4 + c][:, :], ACT.Sqrt, bias=col("eps")).then_inc(hn_root, 1)

            def pair_layer(name, func, split_to=None):
                member = {"gu": 0, "gu1": 0, "gu2": 0, "cu": 0, "cz": 1, "az": 1}[name]
                a0, h0, p0 = ACTED[name], HALVES.get(name, 0), PROD[name]

                def epilogue(g, j):
                    s = (j // 2) % 2
                    if not (isinstance(g, int) and g < 2 and name == "gu"):
                        act.wait_ge(prod, p0 + g - 1)
                    act.activation(chunk(tmp, s), banks[j - 1 + member][:, :], func).then_inc(acted, 1)
                    if split_to is not None:
                        act.wait_ge(merged if name == "az" else prod, (g + 1) if name == "az" else p0 + g + 1)
                        act.activation(chunk(split_to, g), chunk(tmp, 2 + s), ACT.Copy).then_inc(half_hi, 1)
                run_layer(name, epilogue)

            def attention(k, evac):
                for hd in range(k.heads + 1):
                    if hd >= 1:
                        act.wait_ge(k.s_tr, hd)
                        if hd >= 2:
                            act.wait_ge(k.s_pv, hd - 1)
                        b, w, o = k.key_banks[0]
                        act.activation(k.pt[:, o:o + w], banks[b][:, 0:w], ACT.Copy).then_inc(k.s_pt_act, 1)
                    if hd < k.heads:
                        act.wait_ge(k.s_negmax, hd + 1)
                        if hd >= 1:
                            act.wait_ge(k.s_tr, hd)
                        for q, b, o, w, po in k.groups:
                            act.activation(k.p[:, po:po + w], banks[b][:, o:o + w], ACT.Exp,
                                           bias=nm[:, 4 * hd + q:4 * hd + q + 1], scale=k.scale,
                                           accum_out=sm[:, 4 * hd + q:4 * hd + q + 1]).then_inc(k.s_exp, 1)
                        if k is swa:
                            act.activation(es[:, 4 * hd:4 * hd + 4], nm[:, 4 * hd:4 * hd + 4], ACT.Exp,
                                           bias=col("sinks", hd)).then_inc(k.s_sink, 1)
                    if hd >= 1:
                        evac(hd - 1)

            def pair_evac(k):
                def evac(hd):
                    if hd % 2:
                        act.wait_ge(k.s_pv, hd + 1)
                        act.activation(chunk(k.out_hi, k.out_chunk0 + hd // 2), banks[6 + hd // 2 % 2][:, :],
                                       ACT.Copy).then_inc(k.s_hi, 1)
                return evac

            act.dma_start(mem_in[:, :].rearrange("p (c t) -> p c t", c=C),
                          mem_t.rearrange("(c p) t -> p c t", p=P)).then_inc(mem_loaded, 16)
            act.dma_start(vec[:, :], vectors).then_inc(consts_in, 16)
            act.dma_start(tab[:, :], tables).then_inc(consts_in, 16)
            act.dma_start(h[:, :].rearrange("p (c t) -> p c t", c=C),
                          x_t.rearrange("(c p) t -> p c t", p=P)).then_inc(x_loaded, 16)
            act.wait_ge(consts_in, 32)
            act.wait_ge(mem_loaded, 16)
            high_part(0, 0, 0)
            norm("mem", mem_in, memh, M)
            act.wait_ge(norm_sum, 8)
            norm("mix", h, xh, T, ready=(x_loaded, 16, False))
            run_layer("xk", copy_to(kmem, 0, M))
            run_layer("xv", copy_to(vmem_f, 0, M))
            run_layer("fq", copy_to(proj, PR["fq"], T))
            for n in range(4):
                act.wait_ge(vmem_tr, n + 1)
                act.activation(chunk(vmem, n), banks[4 + n][:, :], ACT.Copy).then_inc(vmem_copied, 1)
            act.wait_ge(norm_sum, 16)
            for c in range(C):
                act.activation(chunk(tmp, c, M), chunk(kmem, c, M), ACT.Square).then_inc(kmem_sq, 1)
            run_layer("fk", copy_to(proj, PR["fk"], T))
            for n in range(2):
                act.wait_ge(kmem_sum, 2 * n + 2)
                act.activation(banks[4 + n][:, :], banks[4 + n][:, :], ACT.Sqrt, bias=col("eps")).then_inc(kmem_root, 1)
            head_squares(proj, PR["fq"], 0, (kmem_sum, NX))
            run_layer("rq", copy_to(proj, PR["rq"], T))
            head_roots(0)
            head_squares(proj, PR["fk"], 4, (hn_sum, 4))
            run_layer("rk", copy_to(proj, PR["rk"], T))
            head_roots(4)
            run_layer("rv", copy_to(proj, PR["rv"], T))
            run_layer("rg", copy_to(proj, PR["rg"], T, ACT.Silu))
            for n in range(2):
                act.dma_start(chunk(dec, n), decays[n, :, :]).then_inc(dec_in[n], 16)
            run_layer("fv", copy_to(proj, PR["fv"], T))
            for n in range(QB):
                act.wait_ge(v_tr, n + 1)
                act.activation(chunk(v_ret, n), banks[4 + n][:, :], ACT.Copy).then_inc(v_copied, 1)

            def forget_logits(g, j):
                act.wait_ge(hn_sum, 8)
                act.activation(tmp[0:8, 0:T], banks[0][0:8, :], ACT.Identity,
                               bias=col("b_forget", 0, slice(0, 8))).then_inc(copied, 1)
            run_layer("ff", forget_logits)
            act.wait_ge(copied, COPIED["ff"] + 1)
            act.activation(tmp[0:8, T:2 * T], tmp[0:8, 0:T], ACT.Abs).then_inc(gate_act, 1)
            act.wait_ge(gate_act, 1)
            act.activation(tmp[0:8, T:2 * T], tmp[0:8, T:2 * T], ACT.Exp, scale=-1.0).then_inc(gate_act, 1)
            act.wait_ge(gate_act, 2)
            act.activation(tmp[0:8, T:2 * T], tmp[0:8, T:2 * T], ACT.Ln, bias=col("one", 0, slice(0, 8))).then_inc(gate_act, 1)
            for n in range(QB):
                act.wait_ge(v_tr, QB + n + 1)
                act.activation(chunk(v_fox, n), banks[4 + n][:, :], ACT.Copy).then_inc(v_copied, 1)

            act.wait_ge(f_ready, 1)
            for s in range(2 * QB + 4):
                if 1 <= s < NRET - 1:
                    act.wait_ge(ret_weighted, 4 * s)
                    act.dma_start(chunk(dec, (s + 1) % 2), decays[s + 1, :, :]).then_inc(dec_in[(s + 1) % 2], 16)
                if s % 2 == 0 and 2 <= s <= NRET:
                    p = s // 2 - 1
                    act.wait_ge(ret_pv, s)
                    act.activation(chunk(proj, PR["rq"] + p), banks[3 + p % 2][:, :], ACT.Copy).then_inc(ret_out, 1)
                if s % 2 == 1 and 3 <= s <= NRET + 1:
                    p = (s - 3) // 2
                    act.wait_ge(gn_xc, p + 1)
                    act.activation(chunk(tmp, p), chunk(proj, PR["rq"] + p), ACT.Square).then_inc(gn_sq, 1)
                if s % 2 == 0 and 4 <= s <= NRET + 2:
                    p = (s - 4) // 2
                    act.wait_ge(gn_var, p + 1)
                    act.activation(banks[6][:, :], banks[6][:, :], ACT.Sqrt, bias=col("eps")).then_inc(gn_root, 1)
                if s % 2 == 1 and 5 <= s:
                    p = (s - 5) // 2
                    act.wait_ge(gn_y, p + 1)
                    act.activation(chunk(xh, p), chunk(proj, PR["rg"] + p), ACT.Copy).then_inc(gn_hi, 1)
            attention(fox, pair_evac(fox))
            run_split_only("out")
            norm("xattn", h, xh, T, ready=(resid, RESID["out"], True))

            run_layer("xq", copy_to(xq, 0, T))
            for half in range(2):
                for c in range(4):
                    if half:
                        act.wait_ge(qn_sum, c // 2 + 1)
                    act.activation(chunk(tmp, c), chunk(xq, 4 * half + c), ACT.Square).then_inc(qn_sq, 1)
                for n in range(2):
                    act.wait_ge(qn_sum, 2 * half + n + 1)
                    act.activation(banks[4 + 2 * half + n][:, :], banks[4 + 2 * half + n][:, :], ACT.Sqrt,
                                   bias=col("eps")).then_inc(qn_root, 1)

            def xat_evac(hd):
                act.wait_ge(xat.s_pv, hd + 1)
                for d in range(2):
                    act.activation(chunk(xh, 2 * hd + d), banks[6 + d][:, :], ACT.Copy).then_inc(xat.s_hi, 1)
            attention(xat, xat_evac)
            run_split_only("xo")
            norm("ffn", h, xh, T, ready=(resid, RESID["xo"], True))
            act.activation(csilu, vec[:, VEC["c"][0]:VEC["c"][0] + C], ACT.Silu).then_inc(csilu_done, 1)
            pair_layer("gu", ACT.Silu, hh)
            run_split_only("down")
            norm("ffn1_2", h, xh, T, shift=0, ready=(resid, RESID["down"], True))
            pair_layer("gu1", ACT.Silu, hh)
            run_split_only("down1")
            norm("mix_2", h, xh, T, shift=3, ready=(resid, RESID["down1"], True))
            pair_layer("cu", ACT.Copy)
            run_layer("qkv", copy_to(qkv, 0, T))

            def gated_high(g, j):
                s = j % 2
                act.wait_ge(prod, PROD["b"] + g + 1)
                act.activation(chunk(yh, g), chunk(tmp, 2 + s), ACT.Copy).then_inc(half_hi, 1)
            run_layer("b", gated_high)
            for n in range(2):
                act.wait_ge(vsw_tr, n + 1)
                act.activation(chunk(v_sw, n), banks[4 + n][:, :], ACT.Copy).then_inc(vsw_copied, 1)
            act.wait_ge(rope_done, 18)
            for g in range(NKV):
                for half in range(2):
                    act.dma_start(kdup[half * HD:(half + 1) * HD, g * T:(g + 1) * T],
                                  qkv[g % 2 * HD:(g % 2 + 1) * HD, (8 + g // 2) * T:(9 + g // 2) * T]).then_inc(kdup_in, 16)
            pair_layer("cz", ACT.Sigmoid)
            attention(swa, pair_evac(swa))
            pair_layer("az", ACT.Sigmoid, mh)
            run_split_only("out2")
            norm("ffn2_2", h, xh, T, shift=6, ready=(resid, RESID["out2"], True))
            pair_layer("gu2", ACT.Silu, hh)
            run_split_only("down2")
            norm("final", h, None, T, ready=(resid, RESID["down2"], True))

        @block.vector
        def _(dve):
            tt, ts, stt = dve.tensor_tensor, dve.tensor_scalar, dve.scalar_tensor_tensor

            def norm(name, src, dst, n, gain, shift=None, own=None):
                i = NORMS[name]
                b = 8 * i
                if own:
                    dve.wait_ge(*own)
                dve.wait_ge(norm_root, i + 1)
                dve.reciprocal(rstd[:, 0:n], root[:, 0:n]).then_inc(norm_rstd, 1)
                dve.wait_ge(norm_rstd, i + 1)

                def low(c):
                    dve.wait_ge(norm_hi, b + c + 1)
                    xc = xn[:, c % 2 * T:c % 2 * T + n]
                    if shift is None:
                        tt(chunk(dst[1], c, n), xc, chunk(dst[0], c, n).bitcast(f32), ALU.subtract).then_inc(norm_lo, 1)
                    else:
                        stt(chunk(dst[1], c, n), xc, mod(shift, c), chunk(dst[0], c, n).bitcast(f32),
                            ALU.add, ALU.subtract).then_inc(norm_lo, 1)

                for c in range(C):
                    if c >= 2:
                        dve.wait_ge(norm_lo, b + c - 1)
                    stt(xn[:, c % 2 * T:c % 2 * T + n], chunk(src, c, n), gain(c), rstd[:, 0:n],
                        ALU.mult, ALU.mult).then_inc(norm_xn, 1)
                    if c >= 1:
                        low(c - 1)
                low(C - 1)

            def head_norm(c0, b, gain, own):
                dve.wait_ge(*own)
                for c in range(4):
                    dve.wait_ge(hn_root, b + c + 1)
                    if c >= 2:
                        dve.wait_ge(hn_done, b + c - 1)
                    dve.reciprocal(chunk(xn, c % 2), banks[4 + c][:, :]).then_inc(hn_rstd, 1)
                    dve.wait_ge(hn_rstd, b + c + 1)
                    stt(chunk(proj, c0 + c), chunk(proj, c0 + c), gain, chunk(xn, c % 2),
                        ALU.mult, ALU.mult).then_inc(hn_done, 1)

            rope_n = [0]

            def rope(buf, c0, n, own=None):
                if own:
                    dve.wait_ge(*own)
                for c in range(n):
                    r = rope_n[0]
                    x = chunk(buf, c0 + c)
                    dve.wait_ge(rope_rot, r + 1)
                    if r >= 2:
                        dve.wait_ge(rope_done, r - 1)
                    tt(chunk(xn, r % 2), banks[4 + c % 4][:, :], table("sin"), ALU.mult).then_inc(rope_sin, 1)
                    tt(x, x, table("cos"), ALU.mult).then_inc(rope_cos, 1)
                    dve.wait_ge(rope_sin, r + 1)
                    dve.wait_ge(rope_cos, r + 1)
                    tt(x, x, chunk(xn, r % 2), ALU.add).then_inc(rope_done, 1)
                    rope_n[0] += 1

            def residual(name, gate=None):
                lay = L[name]
                for j in range(C):
                    if name in down_names:
                        if j % 4 == 0:
                            dve.wait_ge(unit_used, lay.u0 + FC // 2 * (j // 4 + 1))
                        bank = banks[j]
                    else:
                        dve.wait_ge(unit_used, lay.u0 + j + 1)
                        bank = banks[j % 4]
                    if gate is None:
                        tt(chunk(h, j), bank[:, :], chunk(h, j), ALU.add).then_inc(resid, 1)
                    else:
                        stt(chunk(h, j), bank[:, :], gate(j), chunk(h, j), ALU.mult, ALU.add).then_inc(resid, 1)

            def pairs(name, split_to=None, extra=None):
                lay = L[name]
                a0, h0, p0 = ACTED[name], HALVES.get(name, 0), PROD[name]

                def one(g, i, j):
                    dve.wait_ge(unit_used, lay.u0 + 2 * j + 2 + 4 * i)
                    dve.wait_ge(acted, a0 + g + 1)
                    member = 1 if name in ("gu", "gu1", "gu2", "cu") else 0
                    bank = banks[2 * j + member]
                    if name == "cu":
                        if not (isinstance(g, int) and g < 2):
                            dve.wait_ge(convolved, 3 * g - 3)
                        o = j * 514
                        tt(cpad[:, o + 2:o + 514], chunk(tmp, j), bank[:, :], ALU.mult).then_inc(prod, 1)
                        dve.wait_ge(prod, p0 + g + 1)
                        y = chunk(conv, g)
                        ts(y, cpad[:, o:o + T], col("conv", g), None, ALU.mult).then_inc(convolved, 1)
                        dve.wait_ge(convolved, 3 * g + 1)
                        stt(y, cpad[:, o + 1:o + 1 + T], col("conv", C + g), y, ALU.mult, ALU.add).then_inc(convolved, 1)
                        dve.wait_ge(convolved, 3 * g + 2)
                        stt(y, cpad[:, o + 2:o + 2 + T], col("conv", 2 * C + g), y, ALU.mult, ALU.add).then_inc(convolved, 1)
                    elif name == "cz":
                        tt(chunk(m1, g), chunk(tmp, j), bank[:, :], ALU.mult).then_inc(prod, 1)
                    else:
                        t = chunk(tmp, 2 + j)
                        if not (isinstance(g, int) and g < 2 and name == "gu"):
                            dve.wait_ge(half_lo, h0 + g - 1)
                        tt(t, chunk(tmp, j), bank[:, :], ALU.mult).then_inc(prod, 1)
                        if name == "az":
                            dve.wait_ge(prod, p0 + g + 1)
                            tt(t, t, chunk(m1, g), ALU.add).then_inc(merged, 1)
                        dve.wait_ge(half_hi, h0 + g + 1)
                        tt(chunk(split_to[1], g), t, chunk(split_to[0], g).bitcast(f32), ALU.subtract).then_inc(half_lo, 1)

                def body(i, first):
                    one(2 * i, i, 0)
                    if extra:
                        extra(i, first)
                    one(2 * i + 1, i, 1)
                repeat(dve, lay.n // 4, body)

            def ada_group(g, first):
                if first:
                    dve.wait_ge(csilu_done, 1)
                    dve.wait_ge(norm_lo, 8 * NORMS["ffn"] + C)
                else:
                    dve.wait_ge(ada_sum, g)
                for k in range(C):
                    dve.wait_ge(ada_in[k % 4], 32 * g + 16 * (k // 4) + 16)
                    w = ada_w[:, k % 4 * ADA_W:(k % 4 + 1) * ADA_W]
                    if k == 0:
                        ts(acc[:, 0:ADA_W], w, csilu[:, 0:1], None, ALU.mult).then_inc(ada_step, 1)
                    else:
                        dve.wait_ge(ada_step, 8 * g + k)
                        stt(acc[:, 0:ADA_W], w, csilu[:, k:k + 1], acc[:, 0:ADA_W], ALU.mult, ALU.add).then_inc(ada_step, 1)

            def attention(k, before_head=None, evac=None):
                for hd in range(k.heads + 1):
                    if hd < k.heads:
                        if before_head:
                            before_head(hd)
                        dve.wait_ge(k.s_scores, hd + 1)
                        for q, b, o, w, _ in k.groups:
                            dve.reduce_max(mx[:, 4 * hd + q:4 * hd + q + 1], banks[b][:, o:o + w], AX.X).then_inc(k.s_max, 1)
                        dve.wait_ge(k.s_max, 4 * hd + 4)
                        m4, n4 = mx[:, 4 * hd:4 * hd + 4], nm[:, 4 * hd:4 * hd + 4]
                        if k is swa:
                            ts(m4, m4, k.scale, col("sinks", hd), ALU.mult, ALU.max).then_inc(k.s_sinkmax, 1)
                            dve.wait_ge(k.s_sinkmax, hd + 1)
                            ts(n4, m4, -1.0, None, ALU.mult).then_inc(k.s_negmax, 1)
                        else:
                            ts(n4, m4, -k.scale, None, ALU.mult).then_inc(k.s_negmax, 1)
                    if hd >= 1:
                        dve.wait_ge(k.s_tr, hd)
                        if hd >= 2:
                            dve.wait_ge(k.s_pv, hd - 1)
                        for b, w, o in k.key_banks[1:]:
                            dve.tensor_copy(k.pt[:, o:o + w], banks[b][:, 0:w]).then_inc(k.s_pt_dve, 1)
                    if hd < k.heads:
                        s4, r4 = sm[:, 4 * hd:4 * hd + 4], rs[:, 4 * hd:4 * hd + 4]
                        dve.wait_ge(k.s_exp, 4 * hd + 4)
                        if k is swa:
                            dve.wait_ge(k.s_sink, hd + 1)
                            tt(s4, s4, es[:, 4 * hd:4 * hd + 4], ALU.add).then_inc(k.s_sum, 1)
                            dve.wait_ge(k.s_sum, hd + 1)
                        dve.reciprocal(r4, s4).then_inc(k.s_recip, 1)
                        dve.wait_ge(k.s_recip, hd + 1)
                        for q, b, o, w, po in k.groups:
                            ts(k.p[:, po:po + w], k.p[:, po:po + w], rs[:, 4 * hd + q:4 * hd + q + 1], None,
                               ALU.mult).then_inc(k.s_pn, 1)
                    if hd >= 1:
                        evac(hd - 1)

            def pair_evac(k):
                def evac(hd):
                    if hd % 2:
                        c = k.out_chunk0 + hd // 2
                        dve.wait_ge(k.s_hi, hd // 2 + 1)
                        tt(chunk(k.out_lo, c), banks[6 + hd // 2 % 2][:, :], chunk(k.out_hi, c).bitcast(f32),
                           ALU.subtract).then_inc(k.s_lo, 1)
                return evac

            dve.memset(lt[:, :], 0.0).then_inc(setup_done, 1)
            dve.memset(rb[:, :], 0.0).then_inc(setup_done, 1)
            dve.wait_ge(setup_done, 2)
            for p0 in (0, HD):
                dve.memset(lt[p0 + 32:p0 + 40, :], -1.0).then_inc(setup_done, 1)
                dve.memset(rb[p0:p0 + 8, :], 1.0).then_inc(setup_done, 1)
            dve.wait_ge(consts_in, 32)
            ts(gq8, col("g_fox_q"), HD ** -0.5, None, ALU.mult).then_inc(setup_done, 1)
            dve.wait_ge(mem_loaded, 16)
            norm("mem", mem_in, (memh, meml), M, lambda c: col("g_mem", c))
            dve.wait_ge(x_loaded, 16)
            norm("mix", h, (xh, xl), T, lambda c: col("g_mix", c), own=(norm_lo, 8))
            dve.wait_ge(norm_lo, 16)
            for n in range(2):
                dve.wait_ge(kmem_root, n + 1)
                dve.reciprocal(chunk(xn, n), banks[4 + n][:, :]).then_inc(kmem_rstd, 1)
            dve.wait_ge(kmem_rstd, 2)
            dve.wait_ge(copied, COPIED["xk"] + C)
            for c in range(C):
                stt(chunk(kmem, c, M), chunk(kmem, c, M), col("g_xk", c % 2), chunk(xn, c // 2, M),
                    ALU.mult, ALU.mult).then_inc(kmem_done, 1)
            dve.wait_ge(setup_done, 7)
            head_norm(PR["fq"], 0, gq8, (kmem_done, C))
            head_norm(PR["fk"], 4, col("g_fox_k"), (hn_done, 4))
            rope(proj, PR["rq"], 4, (hn_done, 8))
            rope(proj, PR["rk"], 4)
            dve.wait_ge(copied, COPIED["ff"] + 1)
            ts(tmp[0:8, 2 * T:3 * T], tmp[0:8, 0:T], 0.0, None, ALU.min).then_inc(gate_dve, 1)
            dve.wait_ge(gate_dve, 1)
            dve.wait_ge(gate_act, 3)
            tt(tmp[0:8, 3 * T:4 * T], tmp[0:8, 2 * T:3 * T], tmp[0:8, T:2 * T], ALU.subtract).then_inc(gate_dve, 1)
            dve.wait_ge(gate_dve, 2)
            dve.tensor_tensor_scan(lt[0:8, :], rb[0:8, :], tmp[0:8, 3 * T:4 * T], 0.0, ALU.mult, ALU.add).then_inc(gate_dve, 1)
            dve.wait_ge(gate_dve, 3)
            for n, dst in enumerate((rb[32:40, :], lt[HD:HD + 8, :], rb[HD + 32:HD + 40, :])):
                dve.tensor_copy(dst, lt[0:8, :]).then_inc(gate_dve, 1)
            dve.wait_ge(gate_dve, 6)
            ts(rh[:, 0:T], rb[:, :], col("head_mask", 0), None, ALU.mult).then_inc(f_ready, 1)

            for s in range(2 * QB + 4):
                if s < NRET:
                    dve.wait_ge(dec_in[s % 2], 16 * (s // 2 + 1))
                    dve.wait_ge(ret_scores, s + 1)
                    if s >= 2:
                        dve.wait_ge(ret_pv, s - 1)
                    pt = pt_a if s % 2 == 0 else pt_b
                    for kb in range(QB):
                        b, o, so = CAUSAL_KEYS[kb]
                        w = T - kb * P
                        tt(pt[:, so:so + w], banks[b][:, o:o + w], dec[:, s % 2 * T:s % 2 * T + w],
                           ALU.mult).then_inc(ret_weighted, 1)
                if s % 2 == 1 and 3 <= s <= NRET + 1:
                    p = (s - 3) // 2
                    ro = chunk(proj, PR["rq"] + p)
                    dve.wait_ge(gn_mean, p + 1)
                    tt(ro, ro, banks[5][:, :], ALU.subtract).then_inc(gn_xc, 1)
                if s % 2 == 0 and 4 <= s <= NRET + 2:
                    p = (s - 4) // 2
                    dve.wait_ge(gn_root, p + 1)
                    if p >= 1:
                        dve.wait_ge(gn_t, p)
                    else:
                        dve.wait_ge(rope_done, 8)
                    dve.reciprocal(chunk(xn, 0), banks[6][:, :]).then_inc(gn_rstd, 1)
                    dve.wait_ge(gn_rstd, p + 1)
                    if p >= 1:
                        dve.wait_ge(gn_y, p)
                    stt(chunk(xn, 1), chunk(proj, PR["rq"] + p), col("g_ret_out", p), chunk(xn, 0),
                        ALU.mult, ALU.mult).then_inc(gn_t, 1)
                    dve.wait_ge(gn_t, p + 1)
                    tt(chunk(proj, PR["rg"] + p), chunk(xn, 1), chunk(proj, PR["rg"] + p), ALU.mult).then_inc(gn_y, 1)
                if s % 2 == 1 and 5 <= s:
                    p = (s - 5) // 2
                    dve.wait_ge(gn_hi, p + 1)
                    tt(chunk(xl, p), chunk(proj, PR["rg"] + p), chunk(xh, p).bitcast(f32), ALU.subtract).then_inc(gn_lo, 1)

            def next_right_rows(hd):
                if hd + 1 < NFOX:
                    if hd >= 1:
                        dve.wait_ge(fox.s_scores, hd)
                    ts(chunk(rh, (hd + 1) % 2), rb[:, :], col("head_mask", hd + 1), None, ALU.mult).then_inc(f_ready, 1)
            attention(fox, next_right_rows, pair_evac(fox))
            residual("out")
            norm("xattn", h, (xh, xl), T, lambda c: col("g_xattn", c), own=(gn_y, 4))
            dve.wait_ge(norm_lo, 8 * NORMS["xattn"] + C)
            for n in range(NX):
                dve.wait_ge(qn_root, n + 1)
                if n >= 2:
                    dve.wait_ge(qn_done, 2 * (n - 1))
                dve.reciprocal(chunk(xn, n % 2), banks[4 + n][:, :]).then_inc(qn_rstd, 1)
                dve.wait_ge(qn_rstd, n + 1)
                for d in range(2):
                    x = chunk(xq, 2 * n + d)
                    stt(x, x, col("g_xq", d), chunk(xn, n % 2), ALU.mult, ALU.mult).then_inc(qn_done, 1)

            def xat_evac(hd):
                for d in range(2):
                    c = 2 * hd + d
                    dve.wait_ge(xat.s_hi, c + 1)
                    tt(chunk(xl, c), banks[6 + d][:, :], chunk(xh, c).bitcast(f32), ALU.subtract).then_inc(xat.s_lo, 1)
            attention(xat, None, xat_evac)
            residual("xo")
            norm("ffn", h, (xh, xl), T, lambda c: col("g_ffn", c), own=(qn_done, C))
            pairs("gu", (hh, hl), ada_group)
            ada_group(11, False)
            dve.wait_ge(ada_sum, ADA_G)
            o = VEC["b_ada"][0]
            tt(mods[:, :], banks[7][:, 0:NMOD * C], vec[:, o:o + NMOD * C], ALU.add).then_inc(mods_done, 1)
            dve.wait_ge(mods_done, 1)
            for m, gname in enumerate(("g_ffn1_2", "g_mix_2", "g_ffn2_2")):
                go = VEC[gname][0]
                stt(gmod[:, m * C:(m + 1) * C], mods[:, (3 * m + 1) * C:(3 * m + 2) * C], 1.0, vec[:, go:go + C],
                    ALU.add, ALU.mult).then_inc(mods_done, 1)
            for m in (0, 2):
                ts(gmod[:, (3 + m) * C:(4 + m) * C], mods[:, (3 * m + 2) * C:(3 * m + 3) * C], 0.5, None,
                   ALU.mult).then_inc(mods_done, 1)
            residual("down")
            dve.wait_ge(mods_done, 6)
            norm("ffn1_2", h, (xh, xl), T, lambda c: gm(0, c), 0, own=(ada_sum, ADA_G))
            pairs("gu1", (hh, hl))
            residual("down1", lambda j: gm(3, j))
            norm("mix_2", h, (xh, xl), T, lambda c: gm(1, c), 3, own=(norm_lo, 8 * NORMS["ffn1_2"] + C))
            dve.wait_ge(ada_step, 8 * ADA_G)
            for n in range(2):
                dve.memset(cpad[:, n * 514:n * 514 + 2], 0.0).then_inc(setup_done, 1)
            dve.wait_ge(setup_done, 9)
            pairs("cu")
            dve.wait_ge(convolved, 3 * C)
            dve.wait_ge(norm_lo, 8 * NORMS["mix_2"] + C)
            for g in range(C):
                dve.wait_ge(unit_used, L["b"].u0 + g + 1)
                dve.wait_ge(half_lo, HALVES["b"] + g - 1)
                tt(chunk(tmp, 2 + g % 2), banks[g % 4][:, :], chunk(conv, g), ALU.mult).then_inc(prod, 1)
                if g in (0, 4):
                    rope(qkv, g, 4)
                if g == 6:
                    rope(qkv, 8, 2)
                dve.wait_ge(half_hi, HALVES["b"] + g + 1)
                tt(chunk(yl, g), chunk(tmp, 2 + g % 2), chunk(yh, g).bitcast(f32), ALU.subtract).then_inc(half_lo, 1)
            pairs("cz")
            attention(swa, None, pair_evac(swa))
            pairs("az", (mh, ml))
            residual("out2", lambda j: mod(5, j))
            norm("ffn2_2", h, (xh, xl), T, lambda c: gm(2, c), 6, own=(rope_done, 18))
            pairs("gu2", (hh, hl))
            residual("down2", lambda j: gm(5, j))
            dve.wait_ge(norm_root, NORMS["final"] + 1)
            dve.wait_ge(norm_lo, 8 * NORMS["ffn2_2"] + C)
            dve.reciprocal(rstd[:, :], root[:, :]).then_inc(norm_rstd, 1)
            dve.wait_ge(norm_rstd, NORMS["final"] + 1)
            for c in range(C):
                stt(chunk(h, c), chunk(h, c), col("g_final", c), rstd[:, :], ALU.mult, ALU.mult).then_inc(final_done, 1)

        @block.tensor
        def _(pe):
            mm = nc.tensor.matmul
            bank_free = {}

            def take(b):
                if b in bank_free:
                    for s, v in bank_free.pop(b):
                        pe.wait_ge(s, v)

            def tiles(n_tiles, slot):
                for t in range(n_tiles):
                    o = slot * UNIT + t * P
                    yield t, whi[:, o:o + P], wlo[:, o:o + P]

            def unit_product(u, slot, bank, rhs, n, ready=None):
                pe.wait_ge(lo_ready, u + 1)
                for t, wh, wl in tiles(8, slot):
                    if ready:
                        pe.wait_ge(ready[0], ready[1] + (t + 1 if ready[2] else 0))
                    rh_, rl_ = chunk(rhs[0], t, n), chunk(rhs[1], t, n)
                    mm(bank[:, 0:n], wh, rh_, start=t == 0, stop=False)
                    mm(bank[:, 0:n], wh, rl_, start=False, stop=False)
                    last = mm(bank[:, 0:n], wl, rh_, start=False, stop=t == 7)
                last.then_inc(unit_used, 1)

            def dense(name, rhs, n, free, ready=None, after_first=None):
                lay = L[name]
                sem_free, base = free
                ring = 4 // lay.per

                def body(i, first):
                    for j in range(4):
                        if j % lay.per == 0:
                            if first:
                                for b in range(j, j + lay.per):
                                    take(b)
                            else:
                                g = (4 * i + j) if lay.per == 1 else 2 * i + j // 2
                                pe.wait_ge(sem_free, base + g - ring + 1)
                        unit_product(lay.u0 + j + 4 * i, (lay.u0 + j) % 2, banks[j], rhs[j % lay.per], n,
                                     ready if first and j < lay.per else None)
                        if j == 0 and after_first and not first:
                            after_first(i - 1)
                if lay.n >= 4:
                    repeat(pe, lay.n // 4, body)
                else:
                    for j in range(lay.n):
                        take(j)
                        unit_product(lay.u0 + j, (lay.u0 + j) % 2, banks[j], rhs[0], n)
                for b in range(min(4, lay.n)):
                    bank_free[b] = [(sem_free, base + lay.groups - ring + b // lay.per + 1)] if lay.n >= 4 else [
                        (sem_free, base + b + 1)]

            def down(name, ready_value, extra=None):
                lay = L[name]
                n_half = FC // 2
                for half in range(2):
                    for b in range(4):
                        take(4 * half + b)
                    if half == 0:
                        pe.wait_ge(half_lo, ready_value)

                    def unit(u, par, k0, first, last_unit):
                        pe.wait_ge(lo_ready, u + 1)
                        for t, wh, wl in tiles(8, par):
                            kk, o = t // 4, t % 4
                            rh_, rl_ = chunk(hh, k0 + kk), chunk(hl, k0 + kk)
                            bank = banks[4 * half + o]
                            mm(bank[:, :], wh, rh_, start=first and kk == 0, stop=False)
                            mm(bank[:, :], wh, rl_, start=False, stop=False)
                            done = mm(bank[:, :], wl, rh_, start=False, stop=last_unit and kk == 1)
                        done.then_inc(unit_used, 1)
                    u0 = lay.u0 + n_half * half
                    unit(u0, u0 % 2, 0, True, False)
                    with pe.Fori(0, (n_half - 3) // 2) as i:
                        for j in range(2):
                            unit(u0 + 1 + j + 2 * i, (u0 + 1 + j) % 2, 2 + 2 * j + 4 * i, False, False)
                    unit(u0 + n_half - 2, (u0 + n_half - 2) % 2, 2 * (n_half - 2), False, False)
                    unit(u0 + n_half - 1, (u0 + n_half - 1) % 2, 2 * (n_half - 1), False, True)
                    if half == 0 and extra:
                        extra()
                for b in range(8):
                    bank_free[b] = [(resid, RESID[name] + b + 1)]

            def norm_sums(name, n):
                i = NORMS[name]
                b = banks[7 if name != "mem" else 6]
                take(7 if name != "mem" else 6)
                for c in range(C):
                    pe.wait_ge(norm_sq, 8 * i + c + 1)
                    mm(b[:, 0:n], mean_d, tmp[:, c % 4 * T:c % 4 * T + n], start=c == 0, stop=c == C - 1).then_inc(norm_sum, 1)
                bank_free[7 if name != "mem" else 6] = [(norm_root, i + 1)]

            def head_sums(b):
                for c in range(4):
                    take(4 + c)
                    pe.wait_ge(hn_sq, b + c + 1)
                    mm(banks[4 + c][:, :], mean_head, chunk(tmp, c), start=True, stop=True).then_inc(hn_sum, 1)
                    bank_free[4 + c] = [(hn_rstd, b + c + 1)]

            rope_n = [0]

            def rope(buf, c0, n, ready):
                pe.wait_ge(*ready)
                for c in range(n):
                    take(4 + c)
                    mm(banks[4 + c][:, :], table("rot"), chunk(buf, c0 + c), start=True, stop=True).then_inc(rope_rot, 1)
                    rope_n[0] += 1
                    bank_free[4 + c] = [(rope_sin, rope_n[0])]

            def values_to_tokens(c0, copied_at, b):
                pe.wait_ge(copied, copied_at)
                for s in range(QB):
                    take(4 + s)
                    for c in range(4):
                        last = nc.tensor.transpose(banks[4 + s][:, c * P:(c + 1) * P],
                                                   proj[:, (c0 + c) * T + s * P:(c0 + c) * T + (s + 1) * P], ident)
                    last.then_inc(v_tr, 1)
                    bank_free[4 + s] = [(v_copied, b + s + 1)]

            def all_banks_taken():
                for b in list(bank_free):
                    take(b)

            def attention(k, scores, transposes, weighted, evacuated):
                all_banks_taken()
                for hd in range(k.heads + 1):
                    if hd < k.heads:
                        if hd >= 1:
                            pe.wait_ge(k.s_exp, 4 * hd)
                        scores(hd).then_inc(k.s_scores, 1)
                    if hd >= 1:
                        d = hd - 1
                        pe.wait_ge(k.s_pn, 4 * d + 4)
                        if d >= 1:
                            pe.wait_ge(k.s_pt_act, d)
                            pe.wait_ge(k.s_pt_dve, d * (len(k.key_banks) - 1))
                        transposes(d).then_inc(k.s_tr, 1)
                        pe.wait_ge(k.s_pt_act, d + 1)
                        pe.wait_ge(k.s_pt_dve, (d + 1) * (len(k.key_banks) - 1))
                        evacuated(d)
                        weighted(d).then_inc(k.s_pv, 1)

            def pair_out_free(k):
                def f(hd):
                    if hd % 2 == 0 and hd >= 4:
                        pe.wait_ge(k.s_lo, hd // 2 - 1)
                return f

            X = (xh, xl)
            pe.wait_ge(consts_in, 32)
            norm_sums("mem", M)
            norm_sums("mix", T)
            dense("xk", [(memh, meml)], M, (copied, COPIED["xk"]), ready=(norm_lo, 0, True))
            dense("xv", [(memh, meml)], M, (copied, COPIED["xv"]))
            dense("fq", [X], T, (copied, COPIED["fq"]), ready=(norm_lo, 8, True))
            pe.wait_ge(copied, COPIED["xv"] + C)
            for m in range(2):
                for half in range(2):
                    n = 2 * m + half
                    take(4 + n)
                    for c in range(4):
                        cc = 4 * half + c
                        last = nc.tensor.transpose(banks[4 + n][:, c * P:(c + 1) * P],
                                                   vmem_f[:, cc * M + m * P:cc * M + (m + 1) * P], ident)
                    last.then_inc(vmem_tr, 1)
                    bank_free[4 + n] = [(vmem_copied, n + 1)]
            dense("fk", [X], T, (copied, COPIED["fk"]))
            for hd in range(NX):
                if hd % 2 == 0:
                    take(4 + hd // 2)
                for d in range(2):
                    pe.wait_ge(kmem_sq, 2 * hd + d + 1)
                    last = mm(banks[4 + hd // 2][:, hd % 2 * M:(hd % 2 + 1) * M], mean_256, chunk(tmp, 2 * hd + d, M),
                              start=d == 0, stop=d == 1)
                last.then_inc(kmem_sum, 1)
            for n in range(2):
                bank_free[4 + n] = [(kmem_rstd, n + 1)]
            dense("rq", [X], T, (copied, COPIED["rq"]))
            head_sums(0)
            dense("rk", [X], T, (copied, COPIED["rk"]))
            head_sums(4)
            dense("rv", [X], T, (copied, COPIED["rv"]))
            rope(proj, PR["rq"], 4, (copied, COPIED["rq"] + 4))
            dense("rg", [X], T, (copied, COPIED["rg"]))
            rope(proj, PR["rk"], 4, (copied, COPIED["rk"] + 4))
            dense("fv", [X], T, (copied, COPIED["fv"]))
            values_to_tokens(PR["rv"], COPIED["rv"] + 4, 0)
            dense("ff", [X], T, (copied, COPIED["ff"]))
            values_to_tokens(PR["fv"], COPIED["fv"] + 4, 4)

            all_banks_taken()
            pe.wait_ge(rope_done, 8)
            pe.wait_ge(v_copied, 4)

            def causal_values(k_pt, v, hd, bank):
                r0 = hd % 2 * HD
                for kb in range(QB):
                    so, w = CAUSAL_KEYS[kb][2], T - kb * P
                    last = mm(bank[r0:r0 + HD, kb * P:T], v[:, kb * T + hd * HD:kb * T + (hd + 1) * HD],
                              k_pt[:, so:so + w], start=kb == 0, stop=kb == QB - 1)
                return last

            for s in range(NRET + 3):
                if s < NRET:
                    if s >= 1:
                        pe.wait_ge(ret_weighted, 4 * s)
                    r0, c = s % 2 * HD, s // 2
                    for kb in range(QB):
                        b, o, _ = CAUSAL_KEYS[kb]
                        w = T - kb * P
                        kk = (PR["rk"] + c) * T + kb * P
                        qq = (PR["rq"] + c) * T
                        last = mm(banks[b][:, o:o + w], proj[r0:r0 + HD, kk:kk + P], proj[r0:r0 + HD, qq + kb * P:qq + T],
                                  start=True, stop=True)
                    last.then_inc(ret_scores, 1)
                if 1 <= s <= NRET:
                    hd = s - 1
                    pe.wait_ge(ret_weighted, 4 * s)
                    if hd % 2 == 0 and hd >= 4:
                        pe.wait_ge(ret_out, hd // 2 - 1)
                    causal_values(pt_a if hd % 2 == 0 else pt_b, v_ret, hd, banks[3 + hd // 2 % 2]).then_inc(ret_pv, 1)
                if s % 2 == 1 and 3 <= s <= NRET + 1:
                    p = (s - 3) // 2
                    pe.wait_ge(ret_out, p + 1)
                    if p >= 1:
                        pe.wait_ge(gn_xc, p)
                    mm(banks[5][:, :], mean_head, chunk(proj, PR["rq"] + p), start=True, stop=True).then_inc(gn_mean, 1)
                if s % 2 == 0 and 4 <= s <= NRET + 2:
                    p = (s - 4) // 2
                    pe.wait_ge(gn_sq, p + 1)
                    if p >= 1:
                        pe.wait_ge(gn_rstd, p)
                    mm(banks[6][:, :], mean_head, chunk(tmp, p), start=True, stop=True).then_inc(gn_var, 1)
            bank_free[3] = [(ret_out, 3)]
            bank_free[4] = [(ret_out, 4)]
            bank_free[5] = [(gn_xc, 4)]
            bank_free[6] = [(gn_rstd, 4)]

            pe.wait_ge(hn_done, 8)
            pe.wait_ge(v_copied, 8)

            def fox_scores(hd):
                r0, c = hd % 2 * HD, hd // 2
                pe.wait_ge(f_ready, hd + 1)
                for q, b, o, w, _ in FOX_GROUPS:
                    qq = (PR["fq"] + c) * T + q * P
                    kk = (PR["fk"] + c) * T
                    out = banks[b][:, o:o + w]
                    mm(out, proj[r0:r0 + HD, qq:qq + P], proj[r0:r0 + HD, kk:kk + w], start=True, stop=False)
                    mm(out, lt[r0:r0 + HD, q * P:(q + 1) * P], rh[r0:r0 + HD, hd % 2 * T:hd % 2 * T + w],
                       start=False, stop=True)
                    last = mm(banks[b][:, o + w - P:o + w], ident, tab[:, TAB["window"][0] + P:TAB["window"][0] + 2 * P],
                              start=False, stop=True, skip_group_check=True)
                return last

            def fox_transposes(hd):
                for kb in range(QB):
                    b, o, _ = CAUSAL_KEYS[kb]
                    for q, _, _, _, po in FOX_GROUPS:
                        if q >= kb:
                            oo = o + (q - kb) * P
                            last = nc.tensor.transpose(banks[3 + b][:, oo:oo + P], fox.p[:, po + kb * P:po + (kb + 1) * P], ident)
                return last

            attention(fox, fox_scores, fox_transposes,
                      lambda hd: causal_values(fox.pt, v_fox, hd, banks[6 + hd // 2 % 2]), pair_out_free(fox))
            bank_free[6] = bank_free[7] = [(fox.s_lo, 4)]
            for b in (0, 1, 2):
                bank_free[b] = [(fox.s_exp, 4 * NFOX)]
            for b in (3, 4, 5):
                bank_free[b] = [(fox.s_pt_act, NFOX), (fox.s_pt_dve, 2 * NFOX)]
            pe.wait_ge(gn_lo, 4)
            pe.wait_ge(fox.s_lo, 4)
            dense("out", [X], T, (resid, RESID["out"]))

            norm_sums("xattn", T)
            dense("xq", [X], T, (copied, COPIED["xq"]), ready=(norm_lo, 8 * NORMS["xattn"], True))
            for hd in range(NX):
                take(4 + hd)
                for d in range(2):
                    pe.wait_ge(qn_sq, 2 * hd + d + 1)
                    last = mm(banks[4 + hd][:, :], mean_256, chunk(tmp, (2 * hd + d) % 4), start=d == 0, stop=d == 1)
                last.then_inc(qn_sum, 1)
                bank_free[4 + hd] = [(qn_rstd, hd + 1)]
            pe.wait_ge(kmem_done, C)
            pe.wait_ge(vmem_copied, 4)

            def xat_scores(hd):
                pe.wait_ge(qn_done, 2 * hd + 2)
                for q, b, o, w, _ in XAT_GROUPS:
                    for d in range(2):
                        c = 2 * hd + d
                        last = mm(banks[b][:, o:o + w], xq[:, c * T + q * P:c * T + (q + 1) * P], chunk(kmem, c, M),
                                  start=d == 0, stop=d == 1)
                return last

            def xat_transposes(hd):
                for kb in range(2):
                    for q in range(QB):
                        last = nc.tensor.transpose(banks[3 + kb][:, q * P:(q + 1) * P],
                                                   xat.p[:, q * M + kb * P:q * M + (kb + 1) * P], ident)
                return last

            def xat_values(hd):
                for d in range(2):
                    o = (2 * hd + d) * P
                    for kb in range(2):
                        last = mm(banks[6 + d][:, :], vmem[:, kb * D + o:kb * D + o + P], xat.pt[:, kb * T:(kb + 1) * T],
                                  start=kb == 0, stop=kb == 1)
                return last

            def xat_out_free(hd):
                if hd >= 1:
                    pe.wait_ge(xat.s_lo, 2 * hd)
            attention(xat, xat_scores, xat_transposes, xat_values, xat_out_free)
            for b in (0, 1):
                bank_free[b] = [(xat.s_exp, 4 * NX)]
            bank_free[3], bank_free[4] = [(xat.s_pt_act, NX)], [(xat.s_pt_dve, NX)]
            bank_free[6] = bank_free[7] = [(xat.s_lo, 8)]
            pe.wait_ge(xat.s_lo, 8)
            dense("xo", [X], T, (resid, RESID["xo"]))

            norm_sums("ffn", T)

            def ada_sums(g):
                for n in range(ADA_B):
                    o = g * ADA_B + n
                    if n == 0:
                        pe.wait_ge(ada_step, 8 * g + 8)
                    dst = banks[7][:, o:o + 1] if isinstance(o, int) else banks[7][:, bass.ds(o, 1)]
                    last = mm(dst, acc[:, n * P:(n + 1) * P], col("one"), start=True, stop=True)
                last.then_inc(ada_sum, 1)
            dense("gu", [X, X], T, (prod, PROD["gu"]), ready=(norm_lo, 8 * NORMS["ffn"], True), after_first=ada_sums)
            ada_sums(10)
            bank_free[7] = [(mods_done, 1)]

            def last_ada():
                ada_sums(11)
            down("down", HALVES["gu"] + FC, last_ada)

            norm_sums("ffn1_2", T)
            dense("gu1", [X, X], T, (prod, PROD["gu1"]), ready=(norm_lo, 8 * NORMS["ffn1_2"], True))
            down("down1", HALVES["gu1"] + FC)
            norm_sums("mix_2", T)
            dense("cu", [X, X], T, (prod, PROD["cu"]), ready=(norm_lo, 8 * NORMS["mix_2"], True))
            dense("qkv", [X], T, (copied, COPIED["qkv"]))
            rope(qkv, 0, 4, (copied, COPIED["qkv"] + 12))
            dense("b", [X], T, (prod, PROD["b"]), after_first=lambda g: rope(qkv, 4, 4, (copied, COPIED["qkv"] + 12)))
            rope(qkv, 8, 2, (copied, COPIED["qkv"] + 12))
            for n in range(2):
                take(4 + n)
                for s in range(2):
                    for c in range(2):
                        last = nc.tensor.transpose(banks[4 + n][:, s * 2 * P + c * P:s * 2 * P + (c + 1) * P],
                                                   qkv[:, (10 + c) * T + (2 * n + s) * P:(10 + c) * T + (2 * n + s + 1) * P], ident)
                last.then_inc(vsw_tr, 1)
                bank_free[4 + n] = [(vsw_copied, n + 1)]
            pe.wait_ge(half_lo, HALVES["b"] + C)
            dense("cz", [(yh, yl), X], T, (prod, PROD["cz"]))

            pe.wait_ge(kdup_in, 16 * 2 * NKV)
            pe.wait_ge(rope_done, 18)
            w0 = TAB["window"][0]

            def swa_scores(hd):
                r0, g = hd % 2 * HD, hd // (NSW // NKV)
                for q, b, o, w, _ in SWA_GROUPS:
                    qq = hd // 2 * T + q * P
                    k0 = g * T + (q + 1) * P - w
                    mm(banks[b][:, o:o + w], qkv[r0:r0 + HD, qq:qq + P], kdup[r0:r0 + HD, k0:k0 + w], start=True, stop=False)
                    last = mm(banks[b][:, o:o + w], ident, tab[:, w0 + 2 * P - w:w0 + 2 * P], start=False, stop=True)
                return last

            def swa_transposes(hd):
                for n, (q, kb) in enumerate(SWA_PAIRS):
                    last = nc.tensor.transpose(banks[3 + n // 4][:, n % 4 * P:(n % 4 + 1) * P], swa.p[:, n * P:(n + 1) * P], ident)
                return last

            def swa_values(hd):
                r0, g = hd % 2 * HD, hd // (NSW // NKV)
                bank = banks[6 + hd // 2 % 2]
                for n, (q, kb) in enumerate(SWA_PAIRS):
                    last = mm(bank[r0:r0 + HD, q * P:(q + 1) * P], v_sw[:, kb * 256 + g * HD:kb * 256 + (g + 1) * HD],
                              swa.pt[:, n * P:(n + 1) * P], start=q == 0 or kb < q, stop=kb == q)
                return last
            attention(swa, swa_scores, swa_transposes, swa_values, pair_out_free(swa))
            for b in (0, 1):
                bank_free[b] = [(swa.s_exp, 4 * NSW)]
            bank_free[3], bank_free[4] = [(swa.s_pt_act, NSW)], [(swa.s_pt_dve, NSW)]
            bank_free[6] = bank_free[7] = [(swa.s_lo, 8)]
            pe.wait_ge(swa.s_lo, 8)
            dense("az", [(yh, yl), X], T, (prod, PROD["az"]))
            pe.wait_ge(half_lo, HALVES["az"] + C)
            dense("out2", [(mh, ml)], T, (resid, RESID["out2"]))
            norm_sums("ffn2_2", T)
            dense("gu2", [X, X], T, (prod, PROD["gu2"]), ready=(norm_lo, 8 * NORMS["ffn2_2"], True))
            down("down2", HALVES["gu2"] + FC)
            norm_sums("final", T)


def constants():
    d = np.arange(P)
    rot = np.zeros((P, P), np.float32)
    for m in range(P):
        if m % HD < HD // 2:
            rot[m + HD // 2, m] = -1.0
        else:
            rot[m - HD // 2, m] = 1.0
    same_head = (d[:, None] // HD == d[None, :] // HD)
    row, colm = d[:, None], d[None, :]
    window = np.concatenate([np.where(colm > row, 0.0, NEG), np.where(colm <= row, 0.0, NEG)], 1)
    inv = (10000.0 ** (-np.arange(0, HD, 2, dtype=np.float32) / np.float32(HD))).astype(np.float32)
    ang = (inv[d % (HD // 2)][:, None] * np.arange(T, dtype=np.float32)[None, :]).astype(np.float32)
    tables = np.concatenate([np.eye(P), rot, np.full((P, P), 1.0 / D), same_head / HD, np.full((P, P), 1.0 / 256),
                             window, np.cos(ang), np.sin(ang)], 1).astype(np.float32)
    assert tables.shape == (P, NTAB)
    log_g = np.log(np.float32(1.0) - np.float32(2.0) ** (-5.0 - np.arange(NRET, dtype=np.float32))).astype(np.float32)
    s, t = np.arange(P)[:, None], np.arange(T)[None, :]
    seen = t // CHUNK >= s // CHUNK
    decays = np.stack([np.where(seen, np.exp(g * np.abs(t - s)), 0.0) * HD ** -0.5 for g in log_g]).astype(np.float32)
    return tables, decays


def column_units(w):
    return w.reshape(C, P, -1, P).transpose(2, 1, 0, 3).reshape(-1, P, UNIT)


def row_units(w):
    return w.reshape(FC // 2, 2, P, 2, 4, P).transpose(3, 0, 2, 1, 4, 5).reshape(-1, P, UNIT)


def interleave(a, b):
    return np.stack([a, b], 1).reshape(-1, P, UNIT)


def lay_out(i):
    def fm(v):
        return np.asarray(v).reshape(-1, P).T

    def split(w, sizes):
        at, out = 0, []
        for n in sizes:
            out.append(w[:, at:at + n])
            at += n
        return out
    rq, rk, rv, rg, fq, fk, fv, ff = split(i["w_in"][0], [512] * 7 + [8])
    ffp = np.zeros((D, P), np.float32)
    ffp[:, 0:8] = ff
    xk, xv = split(i["w_xkv"][0], [D, D])
    b2, c2, u2, q2, k2, v2, zc, za = split(i["w_in_2"][0], [D, D, D, D, 256, 256, D, D])
    cu_ = column_units
    gate, up = cu_(i["w_gate"][0]), cu_(i["w_up"][0])
    g1, p1 = (cu_(w) for w in split(i["w1_gu_2"][0], [FF, FF]))
    g2, p2 = (cu_(w) for w in split(i["w2_gu_2"][0], [FF, FF]))
    parts = [cu_(w) for w in (xk, xv, fq, fk, rq, rk, rv, rg, fv, ffp, i["w_out"][0], i["w_xq"][0], i["w_xo"][0])]
    parts += [interleave(gate, up), row_units(i["w_down"][0]), interleave(g1, p1), row_units(i["w1_down_2"][0]),
              interleave(cu_(c2), cu_(u2)), cu_(q2), cu_(k2), cu_(v2), cu_(b2),
              interleave(cu_(i["w_conv_proj_2"][0]), cu_(zc)), interleave(cu_(i["w_attn_proj_2"][0]), cu_(za)),
              cu_(i["w_out_2"][0]), interleave(g2, p2), row_units(i["w2_down_2"][0])]
    units = np.concatenate(parts, 0)
    assert units.shape == (UNITS, P, UNIT), units.shape
    head_mask = np.zeros((P, 8), np.float32)
    for r in range(P):
        if r % 32 < 8:
            head_mask[r, r % 32] = 1.0
    bf = np.zeros((P, 1), np.float32)
    bf[0:8, 0] = i["b_forget"][0]
    cols = {"g_mem": fm(i["g_mem"][0]), "g_mix": fm(i["g_mix"][0]), "g_xattn": fm(i["g_xattn"][0]),
            "g_ffn": fm(i["g_ffn"][0]), "g_ffn1_2": fm(i["g_ffn1_2"][0]), "g_mix_2": fm(i["g_mix_2"][0]),
            "g_ffn2_2": fm(i["g_ffn2_2"][0]), "g_final": fm(i["g_final_2"]), "g_ret_out": fm(i["g_ret_out"][0].reshape(-1)),
            "g_fox_q": np.tile(i["g_fox_q"][0], 2)[:, None], "g_fox_k": np.tile(i["g_fox_k"][0], 2)[:, None],
            "g_xq": fm(i["g_xq"][0]), "g_xk": fm(i["g_xk"][0]), "b_forget": bf, "conv": fm(i["conv_w_2"][0].reshape(-1)),
            "c": fm(i["c_2"][0]), "b_ada": fm(i["b_ada_2"][0]), "sinks": np.broadcast_to(i["sinks_2"][0][None, :], (P, NSW)),
            "eps": np.full((P, 1), EPS, np.float32), "one": np.ones((P, 1), np.float32), "head_mask": head_mask}
    vectors = np.concatenate([cols[n] for n in VEC], 1)
    assert vectors.shape == (P, NVEC)
    tables, decays = constants()
    out = {"x_t": i["x"][0].T, "mem_t": i["mem"][0].T, "units": units, "w_ada": i["w_ada_2"][0], "vectors": vectors,
           "tables": tables, "decays": decays}
    return {k: np.ascontiguousarray(v) for k, v in out.items()}


def build(nc, arrays):
    aps = {k: nc.dram_tensor(k, list(v.shape), mybir.dt.float32, kind="ExternalInput").ap() for k, v in arrays.items()}
    out_t = nc.dram_tensor("out_t", [D, T], mybir.dt.float32, kind="ExternalOutput").ap()
    two_block_kernel(nc, *[aps[k] for k in ("x_t", "mem_t", "units", "w_ada", "vectors", "tables", "decays")], out_t)


def kernel(**inputs):
    import concourse.bacc as bacc
    from concourse.bass_utils import run_bass_kernel_spmd

    arrays = lay_out({k: np.asarray(v) for k, v in inputs.items()})
    nc = bacc.Bacc("TRN2", target_bir_lowering=False, num_devices=1)
    build(nc, arrays)
    r = run_bass_kernel_spmd(nc, [arrays], core_ids=[0])
    return r.results[0]["out_t"].T[None]
```

```python
from contextlib import ExitStack

import numpy as np
import concourse.bass as bass
from concourse import mybir

D = 1024
T = 512
M = 256
P = 128
C = D // P
QB = T // P
FF = 2816
FC = FF // P
HD = 64
CHUNK = 64
NRET = 8
NFOX = 8
NX = 4
NSW = 16
NKV = 4
NMOD = 9
EPS = 1e-6
NEG = -1e30
UNIT = 8 * P
ADA_G = 12
ADA_W = NMOD * D // ADA_G
ADA_B = ADA_W // P


class Layer:

    def __init__(self, name, u0, n, per):
        self.name, self.u0, self.n, self.per = name, u0, n, per
        self.groups = n // per


def plan_layers():
    shape = [("fq", 4, 1), ("fk", 4, 1), ("rq", 4, 1), ("rk", 4, 1), ("rv", 4, 1), ("rg", 4, 1), ("fv", 4, 1),
             ("ff", 1, 1), ("xk", 8, 1), ("xv", 8, 1), ("out", 8, 1), ("xq", 8, 1), ("xo", 8, 1),
             ("gu", 2 * FC, 2), ("down", FC, 1), ("gu1", 2 * FC, 2), ("down1", FC, 1),
             ("kv", 4, 1), ("qa", 4, 1), ("qb", 4, 1), ("cu", 16, 2), ("b", 8, 1), ("cz", 16, 2), ("az", 16, 2), ("out2", 8, 1),
             ("gu2", 2 * FC, 2), ("down2", FC, 1)]
    layers, u = {}, 0
    for name, n, per in shape:
        layers[name] = Layer(name, u, n, per)
        u += n
    return layers, u


LAYERS, UNITS = plan_layers()
HI_BASE = {n: 8 * i for i, n in enumerate(["mix", "mem", "xattn", "ffn", "ffn1_2", "mix_2", "ffn2_2"])}


def bases(names):
    out, at = {}, 0
    for name in names:
        out[name] = at
        at += 8 if name.startswith("down") else LAYERS[name].groups
    return out


SCALED = bases(["fq", "fk", "rq", "rk", "rv", "rg", "fv", "ff", "xk", "xv", "xq"])
COPIED = bases(["kv", "qa", "qb"])
RESID = bases(["out", "xo", "down", "down1", "out2", "down2"])
PROD = bases(["gu", "gu1", "cu", "b", "cz", "az", "gu2"])
ACTED = bases(["gu", "gu1", "cu", "cz", "az", "gu2"])
HALVES = bases(["gu", "gu1", "b", "az", "gu2"])
SHIFTED = {"ffn1_2": 0, "mix_2": 1, "ffn2_2": 2}
NORMS = {n: i for i, n in enumerate(["mix", "mem", "xattn", "ffn", "ffn1_2", "mix_2", "ffn2_2", "final"])}

VEC = {}
for _name, _n in [("g_mem", 8), ("g_mix", 8), ("g_xattn", 8), ("g_ffn", 8), ("g_ffn1_2", 8), ("g_mix_2", 8),
                  ("g_ffn2_2", 8), ("g_final", 8), ("g_ret_out", 4), ("g_fox_q", 1), ("g_fox_k", 1), ("g_xq", 2),
                  ("g_xk", 2), ("b_forget", 1), ("conv", 24), ("c", 8), ("b_ada", 72), ("sinks", 16), ("eps", 1),
                  ("one", 1), ("head_mask", 8)]:
    VEC[_name] = (sum(n for _, n in VEC.values()), _n)
NVEC = sum(n for _, n in VEC.values())
TAB = {}
for _name, _n in [("ident", P), ("rot", P), ("mean_d", P), ("mean_head", P), ("mean_256", P),
                  ("cos", T), ("sin", T), ("window", 2 * P)]:
    TAB[_name] = (sum(n for _, n in TAB.values()), _n)
NTAB = sum(n for _, n in TAB.values())

FOX_GROUPS = [(3, 0, 0, 512, 768), (2, 1, 0, 384, 384), (0, 1, 384, 128, 0), (1, 2, 0, 256, 128)]
XAT_GROUPS = [(q, q // 2, q % 2 * M, M, q * M) for q in range(QB)]
SWA_GROUPS = [(0, 0, 0, 128, 0), (1, 0, 128, 256, 128), (2, 1, 0, 256, 384), (3, 1, 256, 256, 640)]
XAT_NORM_BANKS = (4, 5, 2, 5)
CAUSAL_KEYS = [(0, 0, 0), (1, 0, 512), (2, 0, 1024), (1, 384, 896)]
SWA_PAIRS = [(0, 0), (1, 0), (1, 1), (2, 1), (2, 2), (3, 2), (3, 3)]


def two_block_kernel(nc, x_t, mem_t, units, w_ada, vectors, tables, decays, out_t):
    f32, f32r = mybir.dt.float32, mybir.dt.float32r
    ALU, ACT, AX = mybir.AluOpType, mybir.ActivationFunctionType, mybir.AxisListType
    L = LAYERS

    with ExitStack() as ctx:
        def sb(name, cols, dt=f32):
            return ctx.enter_context(nc.sbuf_tensor(name, [P, cols], dt))

        def sem(name):
            return ctx.enter_context(nc.semaphore(name))

        h = sb("h", C * T)
        x_at = nc.sbuf_base
        xh, xl = sb("xh", C * T, f32r), sb("xl", C * T, f32r)
        raw, whi, wlo = sb("raw", 4 * UNIT), sb("whi", 2 * UNIT, f32r), sb("wlo", 2 * UNIT, f32r)
        tmp = sb("tmp", 4 * T)
        xn_at = nc.sbuf_base
        xn = sb("xn", 2 * T)
        ssum, rstd = sb("ssum", T), sb("rstd", T)
        r_mem = sb("r_mem", M)
        rcol = sb("rcol", 8)
        mask16 = sb("mask16", 3 * P, mybir.dt.bfloat16)
        tab = sb("tab", NTAB - 2 * P)
        vec = sb("vec", NVEC)
        mx, nm, sm, rs, es = (sb(n, 64) for n in ("mx", "nm", "sm", "rs", "es"))
        mods = sb("mods", NMOD * C)
        gmod = sb("gmod", 6 * C + 1 + C)
        arena_kb = 88
        side = sb("side", 12 * 256)
        arena = sb("arena", arena_kb * 256)

        end = nc.sbuf_base
        arena_at = end - arena_kb * 1024
        side_at = arena_at - 12 * 1024

        def at(name, kb, cols, dt=f32, base=arena_at):
            return nc.alloc_sbuf_tensor_at(name, [P, cols], dt, offset=base + int(kb * 1024))

        PR = {"fq": 0, "fk": 4, "rq": 8, "rk": 12, "rv": 16, "rg": 20, "fv": 24}
        proj = at("proj", 0, 28 * T)
        window = proj[:, PR["fv"] * T:PR["fv"] * T + 2 * P]
        memh, meml = at("memh", 56, C * M, f32r), at("meml", 64, C * M, f32r)
        mem_in = at("mem_in", 72, C * M)
        kmem, vmem = at("kmem", 72, C * M), at("vmem", 80, C * M)
        pt_a, pt_b = at("pt_a", 8, 1280, base=x_at), at("pt_b", 24, 1280, base=x_at)
        p_fox, pt_fox = at("p_fox", 24, 1280), at("pt_fox", 16, 1280)
        xq = at("xq", 32, C * T)
        p_x, pt_x = at("p_x", 48, 1024), at("pt_x", 52, 1024)
        hh, hl = at("hh", 0, FC * T, f32r), at("hl", 44, FC * T, f32r)
        yh, yl = at("yh", 0, C * T, f32r), at("yl", 16, C * T, f32r)
        conv = at("conv", 32, C * T)
        m1 = at("m1", 32, C * T)
        qkv = at("qkv", 48, 12 * T)
        kdup = at("kdup", 72, NKV * T)
        v_sw = at("v_sw", 80, QB * 256)
        p_sw = at("p_sw", 84, 896)
        oh = at("oh", 56, C * T, f32r)
        ol = (at("ol_a", 48, 4 * T, f32r), at("ol_b", 0, 4 * T, f32r, base=xn_at))
        lt = at("lt", 0, T, base=side_at)
        rb = at("rb", 2, T, base=side_at)
        rh = at("rh", 4, 2 * T, base=side_at)
        dec = at("dec", 8, 2 * T, base=side_at)
        ada_w = at("ada_w", 0, 4 * ADA_W, base=side_at)
        cpad = at("cpad", 0, 2 * 514, base=side_at)
        pt_sw = at("pt_sw", 5, 896, base=side_at)

        acc = xn

        banks = [ctx.enter_context(nc.psum_tensor(f"bank{i}", [P, T], f32)) for i in range(8)]

        def chunk(t, c, n=T):
            if isinstance(t, tuple):
                t, c = t[c // 4], c % 4
            return t[:, c * n:(c + 1) * n] if isinstance(c, int) else t[:, bass.ds(c * n, n)]

        def table(name):
            o, n = TAB[name]
            return tab[:, o:o + n]

        def col(name, c=0, rows=slice(None)):
            o = VEC[name][0] + c
            return vec[rows, o:o + 1] if isinstance(o, int) else vec[rows, bass.ds(o, 1)]

        def mod(m, c):
            o = m * C + c
            return mods[:, o:o + 1] if isinstance(o, int) else mods[:, bass.ds(o, 1)]

        def gm(m, c):
            return gmod[:, m * C + c:m * C + c + 1]
        gq8 = gmod[:, 6 * C:6 * C + 1]
        csilu = gmod[:, 6 * C + 1:7 * C + 1]

        ident, mean_d, mean_head, mean_256 = (table(n) for n in ("ident", "mean_d", "mean_head", "mean_256"))

        vec_in, consts_in, mem_loaded = sem("vec_in"), sem("consts_in"), sem("mem_loaded")
        x_loaded = [sem(f"x_loaded{c}") for c in range(C)]
        raw_loaded = [sem(f"raw_loaded{i}") for i in range(4)]
        hi_ready, lo_ready, unit_used = sem("hi_ready"), sem("lo_ready"), sem("unit_used")
        scaled, copied, resid, down_out = sem("scaled"), sem("copied"), sem("resid"), sem("down_out")
        prod, acted, half_hi, half_lo = sem("prod"), sem("acted"), sem("half_hi"), sem("half_lo")
        convolved, merged = sem("convolved"), sem("merged")
        norm_sq, norm_acc, norm_cols, norm_root = (sem(n) for n in ("norm_sq", "norm_acc", "norm_cols", "norm_root"))
        norm_recip, norm_bc, norm_r = sem("norm_recip"), sem("norm_bc"), sem("norm_r")
        norm_xn, norm_hi, norm_lo = sem("norm_xn"), sem("norm_hi"), sem("norm_lo")
        setup_done = sem("setup_done")
        vmem_f_done, vmem_tr, vmem_copied, gate_silu = (sem(n) for n in ("vmem_f_done", "vmem_tr", "vmem_copied", "gate_silu"))
        kmem_sq, kmem_sum, kmem_root, kmem_rstd, kmem_done = (
            sem(n) for n in ("kmem_sq", "kmem_sum", "kmem_root", "kmem_rstd", "kmem_done"))
        hn_sq, hn_sum, hn_root, hn_rstd, hn_done = (sem(n) for n in ("hn_sq", "hn_sum", "hn_root", "hn_rstd", "hn_done"))
        rope_rot, rope_sin, rope_cos, rope_done = (sem(n) for n in ("rope_rot", "rope_sin", "rope_cos", "rope_done"))
        v_tr, v_copied = sem("v_tr"), sem("v_copied")
        gate_scaled, up_scaled = sem("gate_scaled"), sem("up_scaled")
        gate_act, gate_dve, f_ready = sem("gate_act"), sem("gate_dve"), sem("f_ready")
        dec_in = [sem("dec_in0"), sem("dec_in1")]
        ret_scores, ret_weighted, ret_pv, ret_out = (sem(n) for n in ("ret_scores", "ret_weighted", "ret_pv", "ret_out"))
        gn_mean, gn_xc, gn_sq, gn_var, gn_root = (sem(n) for n in ("gn_mean", "gn_xc", "gn_sq", "gn_var", "gn_root"))
        gn_rstd, gn_t, gn_y, gn_hi, gn_lo = (sem(n) for n in ("gn_rstd", "gn_t", "gn_y", "gn_hi", "gn_lo"))
        rh_ready = sem("rh_ready")

        class Kind:

            def __init__(self, name, heads, groups, p, pt, scale, key_banks, out_banks, out_hi, out_lo, out_chunk0):
                self.heads, self.groups, self.p, self.pt, self.scale = heads, groups, p, pt, scale
                self.key_banks = key_banks
                self.out_banks = out_banks
                self.out_hi, self.out_lo, self.out_chunk0 = out_hi, out_lo, out_chunk0
                self.s_scores, self.s_max = sem(name + "_scores"), sem(name + "_max")
                self.s_sinkmax, self.s_negmax = sem(name + "_sinkmax"), sem(name + "_negmax")
                self.s_exp, self.s_sink = sem(name + "_exp"), sem(name + "_sink")
                self.s_sum, self.s_recip, self.s_pn = sem(name + "_sum"), sem(name + "_recip"), sem(name + "_pn")
                self.s_tr, self.s_pt_act, self.s_pt_dve = sem(name + "_tr"), sem(name + "_pt_act"), sem(name + "_pt_dve")
                self.s_pv, self.s_hi, self.s_lo = sem(name + "_pv"), sem(name + "_hi"), sem(name + "_lo")

        fox = Kind("fox", NFOX, FOX_GROUPS, p_fox, pt_fox, 1.0, [(3, 512, 0), (4, 512, 512), (5, 256, 1024)], (6,), xh, xl, 4)
        xat = Kind("xat", NX, XAT_GROUPS, p_x, pt_x, 256.0 ** -0.5, [(3, 512, 0), (4, 512, 512)], (6, 7), yh, yl, 0)
        swa = Kind("swa", NSW, SWA_GROUPS, p_sw, pt_sw, HD ** -0.5, [(3, 512, 0), (4, 384, 512)], (6, 7), oh, ol, 0)

        qn_sq, qn_sum, qn_root, qn_rstd, qn_done = (sem(n) for n in ("qn_sq", "qn_sum", "qn_root", "qn_rstd", "qn_done"))
        ada_in = [sem(f"ada_in{i}") for i in range(4)]
        csilu_done, ada_step, ada_sum, mods_done = sem("csilu_done"), sem("ada_step"), sem("ada_sum"), sem("mods_done")
        kdup_in, vsw_tr, vsw_copied = sem("kdup_in"), sem("vsw_tr"), sem("vsw_copied")
        final_done, stored = sem("final_done"), sem("stored")
        down_names = ("down", "down1", "down2")
        DOWN_BANKS = {"down": (4, 5, 6, 0, 1, 2, 3, 7), "down1": (4, 5, 6, 7, 0, 1, 2, 3), "down2": (4, 5, 6, 7, 0, 1, 2, 3)}

        block = ctx.enter_context(nc.Block())

        def repeat(eng, n, body):
            if n:
                body(0, True)
            if n - 1 >= 2:
                with eng.Fori(1, n) as i:
                    body(i, False)
            elif n == 2:
                body(1, False)

        @block.sync
        def _(sp):
            def load_unit(u, slot, first=False):
                if not first:
                    sp.wait_ge(lo_ready, u - 3)
                sp.dma_start(raw[:, slot * UNIT:(slot + 1) * UNIT],
                             units[u, :, :] if isinstance(u, int) else
                             units[bass.ds(u, 1), :, :].rearrange("a p n -> (a p) n")).then_inc(raw_loaded[slot], 16)

            def load_ada(g, k, first=False):
                slot = k % 4
                if not (first and k < 4):
                    sp.wait_ge(ada_step, g * 8 + k - 3)
                if first and k == 0:
                    sp.wait_ge(fox.s_pv, NFOX)
                cols = slice(g * ADA_W, (g + 1) * ADA_W) if isinstance(g, int) else bass.ds(g * ADA_W, ADA_W)
                sp.dma_start(ada_w[:, slot * ADA_W:(slot + 1) * ADA_W],
                             w_ada[k * P:(k + 1) * P, cols]).then_inc(ada_in[slot], 16)

            def load_x(cs):
                for c in cs:
                    sp.dma_start(chunk(h, c), x_t[c * P:(c + 1) * P, :]).then_inc(x_loaded[c], 16)
            load_unit(0, 0, True)
            load_x((0, 1))
            load_unit(1, 1, True)
            load_x(range(2, C))
            sp.dma_start(tab[:, :], tables[:, 0:NTAB - 2 * P]).then_inc(consts_in, 16)
            sp.dma_start(window, tables[:, NTAB - 2 * P:NTAB]).then_inc(consts_in, 16)
            load_unit(2, 2, True)
            load_unit(3, 3, True)
            sp.dma_start(mem_in[:, :].rearrange("p (c t) -> p c t", c=C),
                         mem_t.rearrange("(c p) t -> p c t", p=P)).then_inc(mem_loaded, 16)
            gu0 = L["gu"].u0
            lead = gu0 // 4 * 4
            with sp.Fori(1, lead // 4) as i:
                for j in range(4):
                    load_unit(4 * i + j, j)
            u = lead
            for _ in range(4):
                load_unit(u, u % 4)
                u += 1

            def round_with_ada(i, first):
                for j in range(4):
                    load_unit(lead + 4 + 4 * i + j, j)
                    load_ada(i, 2 * j, first)
                    load_ada(i, 2 * j + 1, first)
            repeat(sp, 11, round_with_ada)
            u = lead + 4 + 44
            for j in range(4):
                load_unit(u + j, j)
                load_ada(11, 2 * j)
                load_ada(11, 2 * j + 1)
            u += 4
            rounds = (UNITS - u) // 4
            with sp.Fori(0, rounds) as i:
                for j in range(4):
                    load_unit(u + 4 * i + j, j)
            for v in range(u + 4 * rounds, UNITS):
                load_unit(v, v % 4)
            for c in range(C):
                sp.wait_ge(final_done, c + 1)
                sp.dma_start(out_t[c * P:(c + 1) * P, :], chunk(h, c)).then_inc(stored, 16)
            sp.wait_ge(stored, 16 * C)

        @block.gpsimd
        def _(pool):
            def low_part(u, j):
                pool.wait_ge(hi_ready, u + 1)
                pool.tensor_tensor(wlo[:, j % 2 * UNIT:(j % 2 + 1) * UNIT], raw[:, j * UNIT:(j + 1) * UNIT],
                                   whi[:, j % 2 * UNIT:(j % 2 + 1) * UNIT].bitcast(f32), ALU.subtract).then_inc(lo_ready, 1)

            with pool.Fori(0, UNITS // 4) as i:
                for j in range(4):
                    low_part(4 * i + j, j)
            for v in range(UNITS // 4 * 4, UNITS):
                low_part(v, v % 4)

        @block.scalar
        def _(act):
            split_so_far = [0]

            def high_part(u0, i, j):
                v = u0 + j
                if isinstance(i, int):
                    if v + 4 * i >= UNITS or v + 4 * i < split_so_far[0]:
                        return
                    assert v + 4 * i == split_so_far[0]
                    split_so_far[0] += 1
                slot = v % 4
                act.wait_ge(raw_loaded[slot], 16 * (v // 4 + 1) + 16 * i)
                if not (isinstance(i, int) and v + 4 * i < 2):
                    act.wait_ge(unit_used, v - 1 + 4 * i)
                act.activation(whi[:, v % 2 * UNIT:(v % 2 + 1) * UNIT], raw[:, slot * UNIT:(slot + 1) * UNIT],
                               ACT.Copy).then_inc(hi_ready, 1)

            def run_layer(name, epilogue, between_units=None):
                lay = L[name]

                def body(i, first):
                    for j in range(4):
                        high_part(lay.u0, i, j + 1)
                        if between_units and j % 2 == 0:
                            between_units(i, first, j)
                        if (j + 1) % lay.per == 0:
                            act.wait_ge(unit_used, lay.u0 + j + 1 + 4 * i)
                            g = (4 * i + j) // lay.per if isinstance(i, int) else (
                                4 * i + j if lay.per == 1 else 2 * i + j // 2)
                            epilogue(g, j)
                repeat(act, lay.n // 4, body)
                if lay.n >= 12:
                    split_so_far[0] = lay.u0 + lay.n // 4 * 4 + 1
                for r in range(lay.n // 4 * 4, lay.n):
                    high_part(lay.u0, 0, r + 1)
                    act.wait_ge(unit_used, lay.u0 + r + 1)
                    epilogue(r, r % 4)

            def run_split_only(name):
                lay = L[name]

                def body(i, first):
                    for j in range(4):
                        high_part(lay.u0, i, j + 1)
                repeat(act, lay.n // 4, body)
                if lay.n >= 12:
                    split_so_far[0] = lay.u0 + lay.n // 4 * 4 + 1
                for r in range(lay.n // 4 * 4, lay.n):
                    high_part(lay.u0, 0, r + 1)

            def copy_to(dest, c0, n, func=ACT.Copy):
                def epilogue(g, j):
                    act.activation(chunk(dest, c0 + g, n), banks[j][:, 0:n], func).then_inc(copied, 1)
                return epilogue

            def norm_chunk(name, g, j, src=h, n=T, dst=None, gain=None):
                if not (isinstance(g, int) and g < 4):
                    act.wait_ge(norm_acc, 7 * NORMS[name] + g - 3)
                act.activation(tmp[:, j * T:j * T + n], chunk(src, g, n), ACT.Square).then_inc(norm_sq, 1)
                if dst is not None:
                    act.activation(chunk(dst, g, n), chunk(src, g, n), ACT.Copy, scale=col(gain, g)).then_inc(norm_hi, 1)

            def norm_root_of(name, n_blocks=QB, bank=7):
                i = NORMS[name]
                act.wait_ge(norm_cols, i + 1)
                act.activation(rcol[:, 0:n_blocks], banks[bank][:, 0:n_blocks], ACT.Sqrt, bias=col("eps")).then_inc(norm_root, 1)

            def norm_r_copy(name, n=T, bank=7, dst=rstd):
                act.wait_ge(norm_bc, NORMS[name] + 1)
                act.activation(dst[:, 0:n], banks[bank][:, 0:n], ACT.Copy).then_inc(norm_r, 1)

            def norm_high(name, dst, shift):
                for c in range(C):
                    act.wait_ge(norm_xn, 8 * SHIFTED[name] + c + 1)
                    act.activation(chunk(dst, c), xn[:, c % 2 * T:c % 2 * T + T], ACT.Identity,
                                   bias=mod(shift, c)).then_inc(norm_hi, 1)

            def residual_layer(name, norm, dst=None, gain=None, before_last=None):
                def epilogue(g, j):
                    act.wait_ge(resid, RESID[name] + g + 1)
                    norm_chunk(norm, g, j, dst=dst, gain=gain)
                run_layer(name, epilogue)

            def down_layer(name, norm, dst=None, gain=None):
                lay = L[name]
                half = FC // 2

                def chunks(cs):
                    for c in cs:
                        act.wait_ge(resid, RESID[name] + c + 1)
                        norm_chunk(norm, c, c % 4, dst=dst, gain=gain)

                def body(i, first, u0=0):
                    for j in range(4):
                        high_part(lay.u0 + u0, i, j + 1)
                repeat(act, 2, body)
                for r in range(8, half):
                    high_part(lay.u0, 0, r + 1)
                high_part(lay.u0, 0, half + 1)
                chunks((0, 1))
                high_part(lay.u0, 0, half + 2)
                chunks((2, 3))
                for r in range(half + 2, FC):
                    high_part(lay.u0, 0, r + 1)
                chunks((4, 5, 6, 7))

            def head_square(c0, b, c, ready):
                act.wait_ge(*ready)
                if b == 0:
                    act.wait_ge(norm_acc, 4 + c if c < 3 else 7)
                act.activation(chunk(tmp, c), chunk(proj, c0 + c), ACT.Square).then_inc(hn_sq, 1)

            def head_root(b, c):
                act.wait_ge(hn_sum, b + c + 1)
                act.activation(banks[4 + c][:, :], banks[4 + c][:, :], ACT.Sqrt, bias=col("eps")).then_inc(hn_root, 1)

            def pair_layer(name, func, split_to=None):
                member = {"gu": 0, "gu1": 0, "gu2": 0, "cu": 0, "cz": 1, "az": 1}[name]
                a0, h0, p0 = ACTED[name], HALVES.get(name, 0), PROD[name]

                def split_product(g, s):
                    if name == "az":
                        act.wait_ge(merged, g + 1)
                    else:
                        act.wait_ge(prod, p0 + g + 1)
                    act.activation(chunk(split_to, g), chunk(tmp, 2 + s), ACT.Copy).then_inc(half_hi, 1)

                def epilogue(g, j):
                    s = (j // 2) % 2
                    if name in ("gu",):
                        act.wait_ge(gate_scaled, g + 1)
                        act.activation(chunk(tmp, s), chunk(tmp, s), func).then_inc(acted, 1)
                    else:
                        act.wait_ge(prod, p0 + g - 1)
                        act.activation(chunk(tmp, s), banks[j - 1 + member][:, :], func).then_inc(acted, 1)

                def between_units(i, first, j):
                    if split_to is not None and not (first and j == 0):
                        split_product(2 * i + j // 2 - 1, (j // 2 + 1) % 2)
                run_layer(name, epilogue, between_units)
                if split_to is not None:
                    split_product(L[name].groups - 1, (L[name].groups - 1) % 2)

            def attention(k, evac, filler=None):
                for hd in range(k.heads + 1):
                    if filler:
                        filler(hd)
                    if hd >= 1:
                        act.wait_ge(k.s_tr, hd)
                        if hd >= 2:
                            act.wait_ge(k.s_pv, hd - 1)
                        b, w, o = k.key_banks[0]
                        act.activation(k.pt[:, o:o + w], banks[b][:, 0:w], ACT.Copy).then_inc(k.s_pt_act, 1)
                    if hd < k.heads:
                        act.wait_ge(k.s_negmax, hd + 1)
                        if hd >= 1:
                            act.wait_ge(k.s_tr, hd)
                        for q, b, o, w, po in k.groups:
                            act.activation(k.p[:, po:po + w], banks[b][:, o:o + w], ACT.Exp,
                                           bias=nm[:, 4 * hd + q:4 * hd + q + 1], scale=k.scale,
                                           accum_out=sm[:, 4 * hd + q:4 * hd + q + 1]).then_inc(k.s_exp, 1)
                        if k is swa:
                            act.activation(es[:, 4 * hd:4 * hd + 4], nm[:, 4 * hd:4 * hd + 4], ACT.Exp,
                                           bias=col("sinks", hd)).then_inc(k.s_sink, 1)
                    if hd >= 1:
                        evac(hd - 1)

            def pair_evac(k):
                def evac(hd):
                    if hd % 2:
                        act.wait_ge(k.s_pv, hd + 1)
                        act.activation(chunk(k.out_hi, k.out_chunk0 + hd // 2), banks[k.out_banks[hd // 2 % len(k.out_banks)]][:, :],
                                       ACT.Copy).then_inc(k.s_hi, 1)
                return evac

            act.dma_start(vec[:, :], vectors).then_inc(vec_in, 16)
            high_part(0, 0, 0)
            act.wait_ge(vec_in, 16)
            for c in range(C):
                act.wait_ge(x_loaded[c], 16)
                norm_chunk("mix", c, c % 4, dst=xh, gain="g_mix")
                if c == 0:
                    high_part(0, 0, 1)
            high_part(0, 0, 2)
            norm_root_of("mix")
            high_part(0, 0, 3)
            norm_r_copy("mix")
            run_split_only("fq")
            for j in range(4):
                high_part(L["fk"].u0, 0, j + 1)
                head_square(PR["fq"], 0, j, (scaled, SCALED["fq"] + j + 1))
            for j in range(4):
                high_part(L["rq"].u0, 0, j + 1)
                head_root(0, j)
                act.wait_ge(scaled, SCALED["fk"] + j + 1)
                head_square(PR["fk"], 4, j, (hn_sum, j + 1))
            for j in range(4):
                high_part(L["rk"].u0, 0, j + 1)
                head_root(4, j)
            act.wait_ge(mem_loaded, 16)
            act.wait_ge(hn_sum, 8)
            for j in range(4):
                high_part(L["rv"].u0, 0, j + 1)
                for c in (2 * j, 2 * j + 1):
                    norm_chunk("mem", c, c % 4, mem_in, M, memh, "g_mem")
            for j in range(4):
                high_part(L["rg"].u0, 0, j + 1)
                if j == 2:
                    norm_root_of("mem", 2, 4)
            norm_r_copy("mem", M, 4, r_mem)
            for c in range(4):
                act.wait_ge(scaled, SCALED["rg"] + c + 1)
                act.activation(chunk(proj, PR["rg"] + c), chunk(proj, PR["rg"] + c), ACT.Silu).then_inc(gate_silu, 1)
            for n in range(2):
                act.dma_start(chunk(dec, n), decays[n, :, :]).then_inc(dec_in[n], 16)
            run_split_only("fv")
            run_split_only("ff")
            act.wait_ge(scaled, SCALED["ff"] + 1)
            bf = col("b_forget", 0, slice(0, 8))
            act.activation(tmp[0:8, T:2 * T], tmp[0:8, 0:T], ACT.Abs, bias=bf).then_inc(gate_act, 1)
            act.wait_ge(gate_act, 1)
            act.activation(tmp[0:8, T:2 * T], tmp[0:8, T:2 * T], ACT.Exp, scale=-1.0).then_inc(gate_act, 1)
            act.wait_ge(gate_act, 2)
            act.activation(tmp[0:8, T:2 * T], tmp[0:8, T:2 * T], ACT.Ln, bias=col("one", 0, slice(0, 8))).then_inc(gate_act, 1)
            for n, (c0, b0) in enumerate(((PR["rv"], 4), (PR["fv"], 0))):
                act.wait_ge(v_tr, QB * (n + 1))
                for s in range(QB):
                    act.activation(chunk(proj, c0 + s), banks[b0 + s][:, :], ACT.Copy).then_inc(v_copied, 1)

            def split_ahead(u):
                if u + 1 < UNITS:
                    high_part(u + 1, 0, 0)

            act.wait_ge(f_ready, 1)
            for s in range(2 * QB + 4):
                if s < C:
                    split_ahead(L["xk"].u0 + s)
                if 1 <= s < NRET - 1:
                    act.wait_ge(ret_weighted, 4 * s)
                    act.dma_start(chunk(dec, (s + 1) % 2), decays[s + 1, :, :]).then_inc(dec_in[(s + 1) % 2], 16)
                if s % 2 == 0 and 2 <= s <= NRET:
                    p = s // 2 - 1
                    act.wait_ge(ret_pv, s)
                    act.activation(chunk(proj, PR["rq"] + p), banks[3 + p % 2][:, :], ACT.Copy).then_inc(ret_out, 1)
                if s % 2 == 1 and 3 <= s <= NRET + 1:
                    p = (s - 3) // 2
                    act.wait_ge(gn_xc, p + 1)
                    act.activation(chunk(tmp, p), chunk(proj, PR["rq"] + p), ACT.Square).then_inc(gn_sq, 1)
                if s % 2 == 0 and 4 <= s <= NRET + 2:
                    p = (s - 4) // 2
                    act.wait_ge(gn_var, p + 1)
                    act.activation(banks[6][:, :], banks[6][:, :], ACT.Sqrt, bias=col("eps")).then_inc(gn_root, 1)
                if s % 2 == 1 and 5 <= s:
                    p = (s - 5) // 2
                    act.wait_ge(gn_y, p + 1)
                    act.activation(chunk(xh, p), chunk(proj, PR["rg"] + p), ACT.Copy).then_inc(gn_hi, 1)
            def values_filler(hd):
                if hd < C:
                    split_ahead(L["xv"].u0 + hd)
                if hd >= 1:
                    act.wait_ge(vmem_tr, hd)
                    act.activation(vmem[:, :].rearrange("p (m n) -> p m n", m=2)[:, :, (hd - 1) * P:hd * P],
                                   banks[7][:, M:2 * M].rearrange("p (m n) -> p m n", m=2), ACT.Copy).then_inc(vmem_copied, 1)
            attention(fox, pair_evac(fox), values_filler)
            act.wait_ge(vmem_tr, C)
            for c in range(C):
                act.activation(chunk(tmp, c, M), chunk(kmem, c, M), ACT.Square).then_inc(kmem_sq, 1)
            act.wait_ge(kmem_sum, NX)
            for n in range(2):
                act.activation(banks[4 + n][:, :], banks[4 + n][:, :], ACT.Sqrt, bias=col("eps")).then_inc(kmem_root, 1)
            residual_layer("out", "xattn", yh, "g_xattn")

            def query_squares(half, js, tmp_free):
                for c in js:
                    act.wait_ge(scaled, SCALED["xq"] + 4 * half + c + 1)
                    if tmp_free and c % 2 == 0:
                        act.wait_ge(*tmp_free(c))
                    act.activation(chunk(tmp, c), chunk(xq, 4 * half + c), ACT.Square).then_inc(qn_sq, 1)

            def query_roots(ns):
                for n in ns:
                    act.wait_ge(qn_sum, n + 1)
                    b = banks[XAT_NORM_BANKS[n]]
                    act.activation(b[:, :], b[:, :], ACT.Sqrt,
                                   bias=col("eps")).then_inc(qn_root, 1)
            lay = L["xq"]
            high_part(lay.u0, 0, 1)
            norm_root_of("xattn")
            high_part(lay.u0, 0, 2)
            norm_r_copy("xattn")
            for r in range(2, 6):
                high_part(lay.u0, 0, r + 1)
            query_squares(0, range(4), None)
            high_part(lay.u0, 0, 7)
            query_roots((0, 1))
            high_part(lay.u0, 0, 8)
            query_squares(1, range(4), lambda c: (qn_sum, c // 2 + 1))

            def later_roots(hd):
                if hd in (1, 2):
                    query_roots((hd + 1,))

            def xat_evac(hd):
                act.wait_ge(xat.s_pv, hd + 1)
                for d in range(2):
                    act.activation(chunk(yh, 2 * hd + d), banks[6 + d][:, :], ACT.Copy).then_inc(xat.s_hi, 1)
            attention(xat, xat_evac, later_roots)
            residual_layer("xo", "ffn", xh, "g_ffn")
            act.activation(csilu, vec[:, VEC["c"][0]:VEC["c"][0] + C], ACT.Silu).then_inc(csilu_done, 1)
            high_part(L["gu"].u0, 0, 1)
            norm_root_of("ffn")
            high_part(L["gu"].u0, 0, 2)
            norm_r_copy("ffn")
            pair_layer("gu", ACT.Silu, hh)
            down_layer("down", "ffn1_2")
            norm_root_of("ffn1_2")
            high_part(L["gu1"].u0, 0, 1)
            norm_high("ffn1_2", xh, 0)
            pair_layer("gu1", ACT.Silu, hh)
            down_layer("down1", "mix_2")
            norm_root_of("mix_2")
            high_part(L["kv"].u0, 0, 1)
            norm_high("mix_2", xh, 3)
            run_layer("kv", copy_to(qkv, 0, T))
            run_layer("qa", copy_to(qkv, 4, T))
            for n in range(2):
                act.wait_ge(vsw_tr, n + 1)
                act.activation(chunk(v_sw, n), banks[6 + n][:, :], ACT.Copy).then_inc(vsw_copied, 1)
            run_layer("qb", copy_to(qkv, 8, T))
            act.wait_ge(rope_done, 10)
            for g in range(NKV):
                for half in range(2):
                    act.dma_start(kdup[half * HD:(half + 1) * HD, g * T:(g + 1) * T],
                                  qkv[g % 2 * HD:(g % 2 + 1) * HD, g // 2 * T:(g // 2 + 1) * T]).then_inc(kdup_in, 16)
            pair_layer("cu", ACT.Copy)

            def gated_high(g, j):
                s = j % 2
                act.wait_ge(prod, PROD["b"] + g + 1)
                act.activation(chunk(yh, g), chunk(tmp, 2 + s), ACT.Copy).then_inc(half_hi, 1)
            run_layer("b", gated_high)

            def conv_filler(hd):
                if hd < NSW:
                    split_ahead(L["cz"].u0 + hd)
                if hd % 2 == 0 and hd >= 2:
                    g = hd // 2 - 1
                    act.wait_ge(unit_used, L["cz"].u0 + hd)
                    act.wait_ge(prod, PROD["cz"] + g - 1)
                    act.activation(chunk(tmp, g % 2), banks[5][:, :], ACT.Sigmoid).then_inc(acted, 1)
            attention(swa, pair_evac(swa), conv_filler)
            pair_layer("az", ACT.Sigmoid, yh)
            residual_layer("out2", "ffn2_2")
            norm_root_of("ffn2_2")
            high_part(L["gu2"].u0, 0, 1)
            norm_high("ffn2_2", xh, 6)
            pair_layer("gu2", ACT.Silu, hh)
            down_layer("down2", "final")
            norm_root_of("final")

        @block.vector
        def _(dve):
            tt, ts, stt = dve.tensor_tensor, dve.tensor_scalar, dve.scalar_tensor_tensor

            def norm_chunk(name, c, src=h, n=T, dst=None, gain=None):
                i = NORMS[name]
                dve.wait_ge(norm_sq, 8 * i + c + 1)
                if c >= 1:
                    if c >= 2:
                        dve.wait_ge(norm_acc, 7 * i + c - 1)
                    t = tmp[:, c % 4 * T:c % 4 * T + n]
                    tt(ssum[:, 0:n], tmp[:, 0:n] if c == 1 else ssum[:, 0:n], t, ALU.add).then_inc(norm_acc, 1)
                if dst is not None:
                    dve.wait_ge(norm_hi, HI_BASE[name] + c + 1)
                    stt(chunk(dst[1], c, n), chunk(src, c, n), col(gain, c), chunk(dst[0], c, n).bitcast(f32),
                        ALU.mult, ALU.subtract).then_inc(norm_lo, 1)

            def norm_recip_of(name, n_blocks=QB):
                i = NORMS[name]
                dve.wait_ge(norm_root, i + 1)
                dve.reciprocal(rcol[:, 4:4 + n_blocks], rcol[:, 0:n_blocks]).then_inc(norm_recip, 1)

            def norm_shifted(name, dst, gain, shift):
                i, b, x0 = NORMS[name], HI_BASE[name], 8 * SHIFTED[name]
                norm_recip_of(name)
                dve.wait_ge(norm_bc, i + 1)

                def low(c):
                    dve.wait_ge(norm_hi, b + c + 1)
                    stt(chunk(dst[1], c), xn[:, c % 2 * T:c % 2 * T + T], mod(shift, c), chunk(dst[0], c).bitcast(f32),
                        ALU.add, ALU.subtract).then_inc(norm_lo, 1)

                for c in range(C):
                    if c >= 2:
                        dve.wait_ge(norm_lo, b + c - 1)
                    stt(xn[:, c % 2 * T:c % 2 * T + T], chunk(h, c), gain(c), banks[7][:, :],
                        ALU.mult, ALU.mult).then_inc(norm_xn, 1)
                    if c >= 1:
                        low(c - 1)
                low(C - 1)

            def scale_units(name, dest, n=T, first=0, last=None):
                lay = L[name]
                for j in range(first, lay.n if last is None else last):
                    dve.wait_ge(unit_used, lay.u0 + j + 1)
                    tt(dest(j), banks[j % 4][:, 0:n], rstd[:, 0:n], ALU.mult).then_inc(scaled, 1)

            def to_proj(c0):
                return lambda j: chunk(proj, c0 + j)

            def head_norm(c0, b, c, gain):
                dve.wait_ge(hn_root, b + c + 1)
                if b + c >= 2:
                    dve.wait_ge(hn_done, b + c - 1)
                dve.reciprocal(chunk(xn, c % 2), banks[4 + c][:, :]).then_inc(hn_rstd, 1)
                dve.wait_ge(hn_rstd, b + c + 1)
                stt(chunk(proj, c0 + c), chunk(proj, c0 + c), gain, chunk(xn, c % 2), ALU.mult, ALU.mult).then_inc(hn_done, 1)

            rope_n = [0]

            def rope(buf, c0, n, own=None, bank0=4):
                if own:
                    dve.wait_ge(*own)
                for c in range(n):
                    r = rope_n[0]
                    x = chunk(buf, c0 + c)
                    dve.wait_ge(rope_rot, r + 1)
                    if r >= 2:
                        dve.wait_ge(rope_done, r - 1)
                    tt(chunk(xn, r % 2), banks[4 + c % 4][:, :], table("sin"), ALU.mult).then_inc(rope_sin, 1)
                    tt(x, x, table("cos"), ALU.mult).then_inc(rope_cos, 1)
                    dve.wait_ge(rope_sin, r + 1)
                    dve.wait_ge(rope_cos, r + 1)
                    tt(x, x, chunk(xn, r % 2), ALU.add).then_inc(rope_done, 1)
                    rope_n[0] += 1

            def residual(name, norm, gate=None, dst=None, gain=None):
                lay = L[name]
                for j in range(C):
                    if name in down_names:
                        if j % 4 < 3:
                            dve.wait_ge(down_out, 6 * down_names.index(name) + j // 4 * 3 + j % 4 + 1)
                        else:
                            dve.wait_ge(unit_used, lay.u0 + FC // 2 * (j // 4 + 1))
                        bank = banks[DOWN_BANKS[name][j]]
                    else:
                        dve.wait_ge(unit_used, lay.u0 + j + 1)
                        bank = banks[j % 4]
                    if gate is None:
                        tt(chunk(h, j), bank[:, :], chunk(h, j), ALU.add).then_inc(resid, 1)
                    else:
                        stt(chunk(h, j), bank[:, :], gate(j), chunk(h, j), ALU.mult, ALU.add).then_inc(resid, 1)
                    norm_chunk(norm, j, dst=dst, gain=gain)

            def pairs(name, split_to=None, extra=None):
                lay = L[name]
                a0, h0, p0 = ACTED[name], HALVES.get(name, 0), PROD[name]

                def one(g, i, j):
                    dve.wait_ge(unit_used, lay.u0 + 2 * j + 2 + 4 * i)
                    if name == "gu":
                        if not (isinstance(g, int) and g < 2):
                            dve.wait_ge(half_lo, g - 1)
                        tt(chunk(tmp, j), banks[2 * j][:, :], rstd[:, :], ALU.mult).then_inc(gate_scaled, 1)
                        tt(chunk(tmp, 2 + j), banks[2 * j + 1][:, :], rstd[:, :], ALU.mult).then_inc(up_scaled, 1)
                        dve.wait_ge(acted, a0 + g + 1)
                        dve.wait_ge(up_scaled, g + 1)
                        t = chunk(tmp, 2 + j)
                        tt(t, t, chunk(tmp, j), ALU.mult).then_inc(prod, 1)
                        dve.wait_ge(half_hi, h0 + g + 1)
                        tt(chunk(split_to[1], g), t, chunk(split_to[0], g).bitcast(f32), ALU.subtract).then_inc(half_lo, 1)
                        return
                    dve.wait_ge(acted, a0 + g + 1)
                    member = 1 if name in ("gu", "gu1", "gu2", "cu") else 0
                    bank = banks[2 * j + member]
                    if name == "cu":
                        if not (isinstance(g, int) and g < 2):
                            dve.wait_ge(convolved, 3 * g - 3)
                        o = j * 514
                        tt(cpad[:, o + 2:o + 514], chunk(tmp, j), bank[:, :], ALU.mult).then_inc(prod, 1)
                        dve.wait_ge(prod, p0 + g + 1)
                        y = chunk(conv, g)
                        ts(y, cpad[:, o:o + T], col("conv", g), None, ALU.mult).then_inc(convolved, 1)
                        dve.wait_ge(convolved, 3 * g + 1)
                        stt(y, cpad[:, o + 1:o + 1 + T], col("conv", C + g), y, ALU.mult, ALU.add).then_inc(convolved, 1)
                        dve.wait_ge(convolved, 3 * g + 2)
                        stt(y, cpad[:, o + 2:o + 2 + T], col("conv", 2 * C + g), y, ALU.mult, ALU.add).then_inc(convolved, 1)
                    else:
                        t = chunk(tmp, 2 + j)
                        dve.wait_ge(half_lo, h0 + g - 1)
                        tt(t, chunk(tmp, j), bank[:, :], ALU.mult).then_inc(prod, 1)
                        if name == "az":
                            dve.wait_ge(prod, p0 + g + 1)
                            tt(t, t, chunk(m1, g), ALU.add).then_inc(merged, 1)
                        dve.wait_ge(half_hi, h0 + g + 1)
                        tt(chunk(split_to[1], g), t, chunk(split_to[0], g).bitcast(f32), ALU.subtract).then_inc(half_lo, 1)

                def body(i, first):
                    one(2 * i, i, 0)
                    if extra:
                        extra(i, first, range(0, 4))
                    one(2 * i + 1, i, 1)
                    if extra:
                        extra(i, first, range(4, 8))
                repeat(dve, lay.n // 4, body)

            def ada_group(g, first, ks=range(C)):
                if 0 in ks and first:
                    dve.wait_ge(csilu_done, 1)
                    dve.wait_ge(qn_done, C)
                elif 0 in ks:
                    dve.wait_ge(ada_sum, g)
                for k in ks:
                    dve.wait_ge(ada_in[k % 4], 32 * g + 16 * (k // 4) + 16)
                    w = ada_w[:, k % 4 * ADA_W:(k % 4 + 1) * ADA_W]
                    if k == 0:
                        ts(acc[:, 0:ADA_W], w, csilu[:, 0:1], None, ALU.mult).then_inc(ada_step, 1)
                    else:
                        dve.wait_ge(ada_step, 8 * g + k)
                        stt(acc[:, 0:ADA_W], w, csilu[:, k:k + 1], acc[:, 0:ADA_W], ALU.mult, ALU.add).then_inc(ada_step, 1)

            def attention(k, before_head=None, evac=None, filler=None):
                for hd in range(k.heads + 1):
                    if filler:
                        filler(hd)
                    if hd < k.heads:
                        if before_head:
                            before_head(hd)
                        dve.wait_ge(k.s_scores, hd + 1)
                        for q, b, o, w, _ in k.groups:
                            dve.reduce_max(mx[:, 4 * hd + q:4 * hd + q + 1], banks[b][:, o:o + w], AX.X).then_inc(k.s_max, 1)
                        dve.wait_ge(k.s_max, 4 * hd + 4)
                        m4, n4 = mx[:, 4 * hd:4 * hd + 4], nm[:, 4 * hd:4 * hd + 4]
                        if k is swa:
                            ts(m4, m4, k.scale, col("sinks", hd), ALU.mult, ALU.max).then_inc(k.s_sinkmax, 1)
                            dve.wait_ge(k.s_sinkmax, hd + 1)
                            ts(n4, m4, -1.0, None, ALU.mult).then_inc(k.s_negmax, 1)
                        else:
                            ts(n4, m4, -k.scale, None, ALU.mult).then_inc(k.s_negmax, 1)
                    if hd >= 1:
                        dve.wait_ge(k.s_tr, hd)
                        if hd >= 2:
                            dve.wait_ge(k.s_pv, hd - 1)
                        for b, w, o in k.key_banks[1:]:
                            dve.tensor_copy(k.pt[:, o:o + w], banks[b][:, 0:w]).then_inc(k.s_pt_dve, 1)
                    if hd < k.heads:
                        s4, r4 = sm[:, 4 * hd:4 * hd + 4], rs[:, 4 * hd:4 * hd + 4]
                        dve.wait_ge(k.s_exp, 4 * hd + 4)
                        if k is swa:
                            dve.wait_ge(k.s_sink, hd + 1)
                            tt(s4, s4, es[:, 4 * hd:4 * hd + 4], ALU.add).then_inc(k.s_sum, 1)
                            dve.wait_ge(k.s_sum, hd + 1)
                        dve.reciprocal(r4, s4).then_inc(k.s_recip, 1)
                        dve.wait_ge(k.s_recip, hd + 1)
                        for q, b, o, w, po in k.groups:
                            ts(k.p[:, po:po + w], k.p[:, po:po + w], rs[:, 4 * hd + q:4 * hd + q + 1], None,
                               ALU.mult).then_inc(k.s_pn, 1)
                    if hd >= 1:
                        evac(hd - 1)

            def pair_evac(k):
                def evac(hd):
                    if hd % 2:
                        c = k.out_chunk0 + hd // 2
                        dve.wait_ge(k.s_hi, hd // 2 + 1)
                        tt(chunk(k.out_lo, c), banks[k.out_banks[hd // 2 % len(k.out_banks)]][:, :], chunk(k.out_hi, c).bitcast(f32),
                           ALU.subtract).then_inc(k.s_lo, 1)
                return evac

            dve.memset(lt[:, :], 0.0).then_inc(setup_done, 1)
            dve.memset(rb[:, :], 0.0).then_inc(setup_done, 1)
            dve.wait_ge(setup_done, 2)
            for p0 in (0, HD):
                dve.memset(lt[p0 + 32:p0 + 40, :], -1.0).then_inc(setup_done, 1)
                dve.memset(rb[p0:p0 + 8, :], 1.0).then_inc(setup_done, 1)
            dve.wait_ge(vec_in, 16)
            for c in range(C):
                dve.wait_ge(x_loaded[c], 16)
                norm_chunk("mix", c, dst=(xh, xl), gain="g_mix")
            ts(gq8, col("g_fox_q"), HD ** -0.5, None, ALU.mult).then_inc(setup_done, 1)
            dve.wait_ge(consts_in, 32)
            o = TAB["ident"][0]
            dve.tensor_copy(mask16[:, 0:P], tab[:, o:o + P]).then_inc(setup_done, 1)
            dve.tensor_copy(mask16[:, P:3 * P], window).then_inc(setup_done, 1)
            norm_recip_of("mix")
            dve.wait_ge(norm_r, 1)
            scale_units("fq", to_proj(PR["fq"]))
            scale_units("fk", to_proj(PR["fk"]))
            dve.wait_ge(setup_done, 9)
            for j in range(4):
                scale_units("rq", to_proj(PR["rq"]), first=j, last=j + 1)
                head_norm(PR["fq"], 0, j, gq8)
            for j in range(4):
                scale_units("rk", to_proj(PR["rk"]), first=j, last=j + 1)
                head_norm(PR["fk"], 4, j, col("g_fox_k"))
            dve.wait_ge(mem_loaded, 16)
            for j in range(4):
                scale_units("rv", to_proj(PR["rv"]), first=j, last=j + 1)
                for c in (2 * j, 2 * j + 1):
                    norm_chunk("mem", c, mem_in, M, (memh, meml), "g_mem")
            scale_units("rg", to_proj(PR["rg"]), last=3)
            norm_recip_of("mem", 2)
            scale_units("rg", to_proj(PR["rg"]), first=3)
            rope(proj, PR["rq"], 4, (hn_done, 8))
            scale_units("fv", to_proj(PR["fv"]))

            dve.wait_ge(hn_sum, 8)
            dve.wait_ge(norm_acc, 14)
            dve.wait_ge(unit_used, L["ff"].u0 + 1)
            tt(tmp[0:8, 0:T], banks[0][0:8, :], rstd[0:8, :], ALU.mult).then_inc(scaled, 1)
            rope(proj, PR["rk"], 4)
            dve.wait_ge(scaled, SCALED["ff"] + 1)
            ts(tmp[0:8, 2 * T:3 * T], tmp[0:8, 0:T], col("b_forget", 0, slice(0, 8)), 0.0, ALU.add, ALU.min).then_inc(gate_dve, 1)
            dve.wait_ge(gate_dve, 1)
            dve.wait_ge(gate_act, 3)
            tt(tmp[0:8, 3 * T:4 * T], tmp[0:8, 2 * T:3 * T], tmp[0:8, T:2 * T], ALU.subtract).then_inc(gate_dve, 1)
            dve.wait_ge(gate_dve, 2)
            dve.tensor_tensor_scan(lt[0:8, :], rb[0:8, :], tmp[0:8, 3 * T:4 * T], 0.0, ALU.mult, ALU.add).then_inc(gate_dve, 1)
            dve.wait_ge(gate_dve, 3)
            for n, dst in enumerate((rb[32:40, :], lt[HD:HD + 8, :], rb[HD + 32:HD + 40, :])):
                dve.tensor_copy(dst, lt[0:8, :]).then_inc(gate_dve, 1)
            dve.wait_ge(gate_dve, 6)
            ts(rh[:, 0:T], rb[:, :], col("head_mask", 0), None, ALU.mult).then_inc(f_ready, 1)

            for s in range(2 * QB + 4):
                if 1 <= s <= C:
                    dve.wait_ge(unit_used, L["xk"].u0 + s)
                    tt(chunk(kmem, s - 1, M), banks[7][:, 0:M], r_mem[:, :], ALU.mult).then_inc(scaled, 1)
                if s < NRET:
                    dve.wait_ge(dec_in[s % 2], 16 * (s // 2 + 1))
                    dve.wait_ge(ret_scores, s + 1)
                    if s >= 2:
                        dve.wait_ge(ret_pv, s - 1)
                    pt = pt_a if s % 2 == 0 else pt_b
                    for kb in range(QB):
                        b, o, so = CAUSAL_KEYS[kb]
                        w = T - kb * P
                        tt(pt[:, so:so + w], banks[b][:, o:o + w], dec[:, s % 2 * T:s % 2 * T + w],
                           ALU.mult).then_inc(ret_weighted, 1)
                if s % 2 == 1 and 3 <= s <= NRET + 1:
                    p = (s - 3) // 2
                    ro = chunk(proj, PR["rq"] + p)
                    dve.wait_ge(gn_mean, p + 1)
                    tt(ro, ro, banks[5][:, :], ALU.subtract).then_inc(gn_xc, 1)
                if s % 2 == 0 and 4 <= s <= NRET + 2:
                    p = (s - 4) // 2
                    dve.wait_ge(gn_root, p + 1)
                    if p >= 1:
                        dve.wait_ge(gn_t, p)
                    else:
                        dve.wait_ge(rope_done, 8)
                    dve.reciprocal(chunk(xn, 0), banks[6][:, :]).then_inc(gn_rstd, 1)
                    dve.wait_ge(gn_rstd, p + 1)
                    if p >= 1:
                        dve.wait_ge(gn_y, p)
                    stt(chunk(xn, 1), chunk(proj, PR["rq"] + p), col("g_ret_out", p), chunk(xn, 0),
                        ALU.mult, ALU.mult).then_inc(gn_t, 1)
                    dve.wait_ge(gn_t, p + 1)
                    dve.wait_ge(gate_silu, p + 1)
                    tt(chunk(proj, PR["rg"] + p), chunk(xn, 1), chunk(proj, PR["rg"] + p), ALU.mult).then_inc(gn_y, 1)
                if s % 2 == 1 and 5 <= s:
                    p = (s - 5) // 2
                    dve.wait_ge(gn_hi, p + 1)
                    tt(chunk(xl, p), chunk(proj, PR["rg"] + p), chunk(xh, p).bitcast(f32), ALU.subtract).then_inc(gn_lo, 1)

            def next_right_rows(hd):
                if hd + 1 < NFOX:
                    if hd >= 1:
                        dve.wait_ge(fox.s_scores, hd)
                    ts(chunk(rh, (hd + 1) % 2), rb[:, :], col("head_mask", hd + 1), None, ALU.mult).then_inc(f_ready, 1)

            def values_filler(hd):
                if hd >= 1:
                    if hd == 1:
                        dve.wait_ge(gn_var, 4)
                    if hd >= 3:
                        dve.wait_ge(vmem_tr, hd - 2)
                    dve.wait_ge(unit_used, L["xv"].u0 + hd)
                    tt(chunk(tmp, hd % 2)[:, 0:M], banks[7][:, 0:M], r_mem[:, :], ALU.mult).then_inc(scaled, 1)
            attention(fox, next_right_rows, pair_evac(fox), values_filler)
            dve.wait_ge(gn_y, 4)
            for n in range(2):
                dve.wait_ge(kmem_root, n + 1)
                dve.reciprocal(chunk(xn, n), banks[4 + n][:, :]).then_inc(kmem_rstd, 1)
            dve.wait_ge(kmem_rstd, 2)
            for c in range(C):
                stt(chunk(kmem, c, M), chunk(kmem, c, M), col("g_xk", c % 2), chunk(xn, c // 2, M),
                    ALU.mult, ALU.mult).then_inc(kmem_done, 1)
            residual("out", "xattn", None, (yh, yl), "g_xattn")
            norm_recip_of("xattn")
            dve.wait_ge(kmem_done, C)
            dve.wait_ge(norm_r, 3)

            def query_norm(n):
                dve.wait_ge(qn_root, n + 1)
                if n >= 2:
                    dve.wait_ge(qn_done, 2 * (n - 1))
                dve.reciprocal(chunk(xn, n % 2), banks[XAT_NORM_BANKS[n]][:, :]).then_inc(qn_rstd, 1)
                dve.wait_ge(qn_rstd, n + 1)
                for d in range(2):
                    x = chunk(xq, 2 * n + d)
                    stt(x, x, col("g_xq", d), chunk(xn, n % 2), ALU.mult, ALU.mult).then_inc(qn_done, 1)

            def later_queries(hd):
                if hd in (1, 2):
                    query_norm(hd + 1)
            scale_units("xq", lambda j: chunk(xq, j), last=6)
            query_norm(0)
            scale_units("xq", lambda j: chunk(xq, j), first=6)
            query_norm(1)

            def xat_evac(hd):
                for d in range(2):
                    c = 2 * hd + d
                    dve.wait_ge(xat.s_hi, c + 1)
                    tt(chunk(yl, c), banks[6 + d][:, :], chunk(yh, c).bitcast(f32), ALU.subtract).then_inc(xat.s_lo, 1)
            attention(xat, None, xat_evac, later_queries)
            residual("xo", "ffn", None, (xh, xl), "g_ffn")
            norm_recip_of("ffn")
            dve.wait_ge(norm_r, 4)
            pairs("gu", (hh, hl), ada_group)
            ada_group(11, False)
            dve.wait_ge(ada_sum, ADA_G)
            o = VEC["b_ada"][0]
            tt(mods[:, :], banks[7][:, 0:NMOD * C], vec[:, o:o + NMOD * C], ALU.add).then_inc(mods_done, 1)
            dve.wait_ge(mods_done, 1)
            for m, gname in enumerate(("g_ffn1_2", "g_mix_2", "g_ffn2_2")):
                go = VEC[gname][0]
                stt(gmod[:, m * C:(m + 1) * C], mods[:, (3 * m + 1) * C:(3 * m + 2) * C], 1.0, vec[:, go:go + C],
                    ALU.add, ALU.mult).then_inc(mods_done, 1)
            for m in (0, 2):
                ts(gmod[:, (3 + m) * C:(4 + m) * C], mods[:, (3 * m + 2) * C:(3 * m + 3) * C], 0.5, None,
                   ALU.mult).then_inc(mods_done, 1)
            residual("down", "ffn1_2")
            dve.wait_ge(mods_done, 6)
            norm_shifted("ffn1_2", (xh, xl), lambda c: gm(0, c), 0)
            pairs("gu1", (hh, hl))
            residual("down1", "mix_2", lambda j: gm(3, j))
            norm_shifted("mix_2", (xh, xl), lambda c: gm(1, c), 3)
            dve.wait_ge(ada_step, 8 * ADA_G)
            for n in range(2):
                dve.memset(cpad[:, n * 514:n * 514 + 2], 0.0).then_inc(setup_done, 1)
            dve.wait_ge(norm_lo, HI_BASE["mix_2"] + C)
            rope(qkv, 0, 2, bank0=4)
            rope(qkv, 4, 4, bank0=4)
            dve.wait_ge(setup_done, 11)
            pairs("cu")
            dve.wait_ge(convolved, 3 * C)
            rope(qkv, 8, 4)
            for g in range(C):
                dve.wait_ge(unit_used, L["b"].u0 + g + 1)
                dve.wait_ge(half_lo, HALVES["b"] + g - 1)
                tt(chunk(tmp, 2 + g % 2), banks[g % 4][:, :], chunk(conv, g), ALU.mult).then_inc(prod, 1)
                dve.wait_ge(half_hi, HALVES["b"] + g + 1)
                tt(chunk(yl, g), chunk(tmp, 2 + g % 2), chunk(yh, g).bitcast(f32), ALU.subtract).then_inc(half_lo, 1)

            def conv_filler(hd):
                if hd % 2 == 0 and hd >= 2:
                    g = hd // 2 - 1
                    dve.wait_ge(acted, ACTED["cz"] + g + 1)
                    tt(chunk(m1, g), chunk(tmp, g % 2), banks[2][:, :], ALU.mult).then_inc(prod, 1)
            attention(swa, None, pair_evac(swa), conv_filler)
            pairs("az", (yh, yl))
            residual("out2", "ffn2_2", lambda j: mod(5, j))
            norm_shifted("ffn2_2", (xh, xl), lambda c: gm(2, c), 6)
            pairs("gu2", (hh, hl))
            residual("down2", "final", lambda j: gm(5, j))
            norm_recip_of("final")
            dve.wait_ge(norm_bc, NORMS["final"] + 1)
            for c in range(C):
                stt(chunk(h, c), chunk(h, c), col("g_final", c), banks[7][:, :], ALU.mult, ALU.mult).then_inc(final_done, 1)

        @block.tensor
        def _(pe):
            mm = nc.tensor.matmul
            bank_free = {}

            def take(b):
                if b in bank_free:
                    for s, v in bank_free.pop(b):
                        pe.wait_ge(s, v)

            def tile_product(slot, t, bank, rhs, n):
                o = slot * UNIT + t * P
                wh, wl = whi[:, o:o + P], wlo[:, o:o + P]
                rh_, rl_ = chunk(rhs[0], t, n), chunk(rhs[1], t, n)
                mm(bank[:, 0:n], wh, rh_, start=t == 0, stop=False)
                mm(bank[:, 0:n], wh, rl_, start=False, stop=False)
                return mm(bank[:, 0:n], wl, rh_, start=False, stop=t == 7)

            def unit_product(u, slot, bank, rhs, n, ready=None):
                if ready:
                    pe.wait_ge(lo_ready, u + 1)
                    for t in range(8):
                        pe.wait_ge(ready[0], ready[1] + t + 1)
                        last = tile_product(slot, t, bank, rhs, n)
                else:
                    pe.wait_ge(hi_ready, u + 1)
                    high_passes(slot, range(8), bank, rhs, n)
                    pe.wait_ge(lo_ready, u + 1)
                    last = low_pass(slot, bank, rhs, n)
                last.then_inc(unit_used, 1)

            def high_passes(slot, ts, bank, rhs, n):
                for t in ts:
                    wh = whi[:, slot * UNIT + t * P:slot * UNIT + (t + 1) * P]
                    mm(bank[:, 0:n], wh, chunk(rhs[0], t, n), start=t == 0, stop=False)
                    mm(bank[:, 0:n], wh, chunk(rhs[1], t, n), start=False, stop=False)

            def low_pass(slot, bank, rhs, n):
                for t in range(8):
                    last = mm(bank[:, 0:n], wlo[:, slot * UNIT + t * P:slot * UNIT + (t + 1) * P], chunk(rhs[0], t, n),
                              start=False, stop=t == 7)
                return last

            def half_unit(u, slot, bank, rhs, n, half):
                if half == 0:
                    pe.wait_ge(hi_ready, u + 1)
                    high_passes(slot, range(6), bank, rhs, n)
                else:
                    high_passes(slot, (6, 7), bank, rhs, n)
                    pe.wait_ge(lo_ready, u + 1)
                    low_pass(slot, bank, rhs, n).then_inc(unit_used, 1)

            def two_units(u, slots, bs, rhs, n, ready):
                pe.wait_ge(lo_ready, u + 2)
                for t in range(8):
                    pe.wait_ge(ready[0], ready[1] + t + 1)
                    last = [tile_product(slots[m], t, banks[bs[m]], rhs[m], n) for m in range(2)]
                for ins in last:
                    ins.then_inc(unit_used, 1)

            def dense(name, rhs, n, free, ready=None, together=None, hooks=None, after_second=None):
                lay = L[name]
                sem_free, base = free
                ring = 4 // lay.per
                hooks = hooks or {}

                def body(i, first):
                    if first and together:
                        take(0)
                        take(1)
                        two_units(lay.u0, [lay.u0 % 2, (lay.u0 + 1) % 2], [0, 1], [rhs[0], rhs[-1]], n, together)
                        if 1 in hooks:
                            hooks[1]()
                    for j in range(2 if first and together else 0, 4):
                        if j % lay.per == 0:
                            if first:
                                for b in range(j, j + lay.per):
                                    take(b)
                            else:
                                g = (4 * i + j) if lay.per == 1 else 2 * i + j // 2
                                pe.wait_ge(sem_free, base + g - ring + 1)
                        unit_product(lay.u0 + j + 4 * i, (lay.u0 + j) % 2, banks[j], rhs[j % lay.per], n,
                                     ready if first and j == 0 else None)
                        if isinstance(i, int) and 4 * i + j in hooks:
                            hooks[4 * i + j]()
                        if j == 1 and after_second and not first:
                            after_second(i - 1)
                if lay.n >= 4:
                    repeat(pe, lay.n // 4, body)
                else:
                    for j in range(lay.n):
                        take(j)
                        unit_product(lay.u0 + j, (lay.u0 + j) % 2, banks[j], rhs[0], n)
                for b in range(min(4, lay.n)):
                    bank_free[b] = [(sem_free, base + lay.groups - ring + b // lay.per + 1)] if lay.n >= 4 else [
                        (sem_free, base + b + 1)]

            def down(name, ready_value, extra=None):
                lay = L[name]
                n_half = FC // 2
                for half in range(2):
                    for b in range(4):
                        take(DOWN_BANKS[name][4 * half + b])
                    if half == 0:
                        pe.wait_ge(half_lo, ready_value - 2)

                    def unit(u, par, k0, first, last_unit):
                        if last_unit and half == 0:
                            pe.wait_ge(half_lo, ready_value)
                        pe.wait_ge(lo_ready, u + 1)
                        order = [(kk, o) for o in range(4) for kk in range(2)] if last_unit else [
                            (kk, o) for kk in range(2) for o in range(4)]
                        for kk, o in order:
                            w0 = par * UNIT + (4 * kk + o) * P
                            wh, wl = whi[:, w0:w0 + P], wlo[:, w0:w0 + P]
                            rh_, rl_ = chunk(hh, k0 + kk), chunk(hl, k0 + kk)
                            bank = banks[DOWN_BANKS[name][4 * half + o]]
                            mm(bank[:, :], wh, rh_, start=first and kk == 0, stop=False)
                            mm(bank[:, :], wh, rl_, start=False, stop=False)
                            done = mm(bank[:, :], wl, rh_, start=False, stop=last_unit and kk == 1)
                            if last_unit and kk == 1 and o < 3:
                                done.then_inc(down_out, 1)
                        done.then_inc(unit_used, 1)
                    u0 = lay.u0 + n_half * half
                    unit(u0, u0 % 2, 0, True, False)
                    with pe.Fori(0, (n_half - 3) // 2) as i:
                        for j in range(2):
                            unit(u0 + 1 + j + 2 * i, (u0 + 1 + j) % 2, 2 + 2 * j + 4 * i, False, False)
                    if half == 0 and extra:
                        extra()
                    unit(u0 + n_half - 2, (u0 + n_half - 2) % 2, 2 * (n_half - 2), False, False)
                    unit(u0 + n_half - 1, (u0 + n_half - 1) % 2, 2 * (n_half - 1), False, True)
                for j, b in enumerate(DOWN_BANKS[name]):
                    bank_free[b] = [(resid, RESID[name] + j + 1)]

            def norm_columns(name, n_blocks=QB, bank=7):
                i = NORMS[name]
                take(bank)
                pe.wait_ge(norm_acc, 7 * i + 7)
                for j in range(n_blocks):
                    last = mm(banks[bank][:, j:j + 1], ssum[:, j * P:(j + 1) * P], mean_d[:, 0:1], start=True, stop=True)
                last.then_inc(norm_cols, 1)

            def norm_spread(name, n_blocks=QB, bank=7, free=None):
                i = NORMS[name]
                pe.wait_ge(norm_recip, i + 1)
                for j in range(n_blocks):
                    last = mm(banks[bank][:, j * P:(j + 1) * P], rcol[:, 4 + j:5 + j].broadcast_to([P, P]), ident,
                              start=True, stop=True)
                last.then_inc(norm_bc, 1)
                if free:
                    bank_free[bank] = [free]

            def head_sums(b):
                for c in range(4):
                    take(4 + c)
                    pe.wait_ge(hn_sq, b + c + 1)
                    mm(banks[4 + c][:, :], mean_head, chunk(tmp, c), start=True, stop=True).then_inc(hn_sum, 1)
                    bank_free[4 + c] = [(hn_rstd, b + c + 1)]

            rope_n = [0]

            def rope(buf, c0, n, ready):
                pe.wait_ge(*ready)
                for c in range(n):
                    take(4 + c)
                    mm(banks[4 + c][:, :], table("rot"), chunk(buf, c0 + c), start=True, stop=True).then_inc(rope_rot, 1)
                    rope_n[0] += 1
                    bank_free[4 + c] = [(rope_sin, rope_n[0])]

            def values_to_tokens(c0, ready, b, b0):
                pe.wait_ge(scaled, ready)
                for s in range(QB):
                    take(b0 + s)
                    for c in range(4):
                        last = nc.tensor.transpose(banks[b0 + s][:, c * P:(c + 1) * P],
                                                   proj[:, (c0 + c) * T + s * P:(c0 + c) * T + (s + 1) * P], ident)
                    last.then_inc(v_tr, 1)
                    bank_free[b0 + s] = [(v_copied, b + s + 1)]

            def all_banks_taken():
                for b in list(bank_free):
                    take(b)

            def attention(k, scores, transposes, weighted, evacuated, before=None, fill=None):
                all_banks_taken()
                for hd in range(k.heads + 1):
                    if hd < k.heads:
                        if hd >= 1:
                            pe.wait_ge(k.s_exp, 4 * hd)
                        scores(hd).then_inc(k.s_scores, 1)
                    if before:
                        before(hd)
                    if fill:
                        fill(hd, 0)
                    if hd >= 1:
                        d = hd - 1
                        pe.wait_ge(k.s_pn, 4 * d + 4)
                        if d >= 1:
                            pe.wait_ge(k.s_pt_act, d)
                            pe.wait_ge(k.s_pt_dve, d * (len(k.key_banks) - 1))
                        transposes(d).then_inc(k.s_tr, 1)
                    if fill:
                        fill(hd, 1)
                    if hd >= 1:
                        pe.wait_ge(k.s_pt_act, d + 1)
                        pe.wait_ge(k.s_pt_dve, (d + 1) * (len(k.key_banks) - 1))
                        evacuated(d)
                        weighted(d).then_inc(k.s_pv, 1)

            def pair_out_free(k):
                def f(hd):
                    n = len(k.out_banks)
                    if hd % 2 == 0 and hd >= 2 * n:
                        pe.wait_ge(k.s_lo, hd // 2 - n + 1)
                return f

            X, Y = (xh, xl), (yh, yl)
            sc = scaled

            def spread_hooks(name):
                return {0: lambda: norm_columns(name), 1: lambda: norm_spread(name, free=(norm_r, NORMS[name] + 1))}

            def wait_consts_then_columns():
                pe.wait_ge(consts_in, 32)
                norm_columns("mix")
            dense("fq", [X], T, (sc, SCALED["fq"]), together=(norm_lo, 0),
                  hooks={1: wait_consts_then_columns, 2: lambda: norm_spread("mix", free=(norm_r, 1))})
            dense("fk", [X], T, (sc, SCALED["fk"]))
            head_sums(0)
            dense("rq", [X], T, (sc, SCALED["rq"]))
            head_sums(4)
            dense("rk", [X], T, (sc, SCALED["rk"]))
            dense("rv", [X], T, (sc, SCALED["rv"]))
            dense("rg", [X], T, (sc, SCALED["rg"]), hooks={1: lambda: norm_columns("mem", 2, 4),
                                                           3: lambda: norm_spread("mem", 2, 4, (norm_r, 2))})
            rope(proj, PR["rq"], 4, (sc, SCALED["rq"] + 4))
            dense("fv", [X], T, (sc, SCALED["fv"]))
            dense("ff", [X], T, (sc, SCALED["ff"]))
            rope(proj, PR["rk"], 4, (sc, SCALED["rk"] + 4))
            values_to_tokens(PR["rv"], SCALED["rv"] + 4, 0, 4)
            values_to_tokens(PR["fv"], SCALED["fv"] + 4, 4, 0)

            all_banks_taken()
            pe.wait_ge(rope_done, 8)
            pe.wait_ge(v_copied, 4)

            def causal_values(k_pt, c0, hd, bank):
                r0 = hd % 2 * HD
                for kb in range(QB):
                    so, w = CAUSAL_KEYS[kb][2], T - kb * P
                    vv = (c0 + kb) * T + hd * HD
                    last = mm(bank[r0:r0 + HD, kb * P:T], proj[:, vv:vv + HD],
                              k_pt[:, so:so + w], start=kb == 0, stop=kb == QB - 1)
                return last

            for s in range(NRET + 3):
                if s < NRET:
                    if s >= 1:
                        pe.wait_ge(ret_weighted, 4 * s)
                    r0, c = s % 2 * HD, s // 2
                    for kb in range(QB):
                        b, o, _ = CAUSAL_KEYS[kb]
                        w = T - kb * P
                        kk = (PR["rk"] + c) * T + kb * P
                        qq = (PR["rq"] + c) * T
                        last = mm(banks[b][:, o:o + w], proj[r0:r0 + HD, kk:kk + P], proj[r0:r0 + HD, qq + kb * P:qq + T],
                                  start=True, stop=True)
                    last.then_inc(ret_scores, 1)
                if 1 <= s <= NRET:
                    hd = s - 1
                    pe.wait_ge(ret_weighted, 4 * s)
                    if hd % 2 == 0 and hd >= 4:
                        pe.wait_ge(ret_out, hd // 2 - 1)
                    causal_values(pt_a if hd % 2 == 0 else pt_b, PR["rv"], hd, banks[3 + hd // 2 % 2]).then_inc(ret_pv, 1)
                if s % 2 == 1 and 3 <= s <= NRET + 1:
                    p = (s - 3) // 2
                    pe.wait_ge(ret_out, p + 1)
                    if p >= 1:
                        pe.wait_ge(gn_xc, p)
                    mm(banks[5][:, :], mean_head, chunk(proj, PR["rq"] + p), start=True, stop=True).then_inc(gn_mean, 1)
                if s % 2 == 0 and 4 <= s <= NRET + 2:
                    p = (s - 4) // 2
                    pe.wait_ge(gn_sq, p + 1)
                    if p >= 1:
                        pe.wait_ge(gn_rstd, p)
                    mm(banks[6][:, :], mean_head, chunk(tmp, p), start=True, stop=True).then_inc(gn_var, 1)
                if s < C:
                    if s == 0:
                        pe.wait_ge(norm_lo, HI_BASE["mem"] + C)
                    else:
                        pe.wait_ge(sc, SCALED["xk"] + s)
                    u = L["xk"].u0 + s
                    unit_product(u, u % 2, banks[7], (memh, meml), M)
            bank_free[7] = [(sc, SCALED["xk"] + C)]
            bank_free[3] = [(ret_out, 3)]
            bank_free[4] = [(ret_out, 4)]
            bank_free[5] = [(gn_xc, 4)]
            bank_free[6] = [(gn_rstd, 4)]

            pe.wait_ge(hn_done, 8)
            pe.wait_ge(v_copied, 8)

            def fox_scores(hd):
                r0, c = hd % 2 * HD, hd // 2
                pe.wait_ge(f_ready, hd + 1)
                for q, b, o, w, _ in FOX_GROUPS:
                    qq = (PR["fq"] + c) * T + q * P
                    kk = (PR["fk"] + c) * T
                    out = banks[b][:, o:o + w]
                    mm(out, proj[r0:r0 + HD, qq:qq + P], proj[r0:r0 + HD, kk:kk + w], start=True, stop=False)
                    mm(out, lt[r0:r0 + HD, q * P:(q + 1) * P], rh[r0:r0 + HD, hd % 2 * T:hd % 2 * T + w],
                       start=False, stop=True)
                    last = mm(banks[b][:, o + w - P:o + w], mask16[:, 0:P], mask16[:, 2 * P:3 * P],
                              start=False, stop=True, skip_group_check=True)
                return last

            def fox_transposes(hd):
                for kb in range(QB):
                    b, o, _ = CAUSAL_KEYS[kb]
                    for q, _, _, _, po in FOX_GROUPS:
                        if q >= kb:
                            oo = o + (q - kb) * P
                            last = nc.tensor.transpose(banks[3 + b][:, oo:oo + P], fox.p[:, po + kb * P:po + (kb + 1) * P], ident)
                return last

            def memory_values_to_tokens(hd):
                if hd >= 1:
                    pe.wait_ge(sc, SCALED["xv"] + hd)
                    for m in range(2):
                        last = nc.tensor.transpose(banks[7][:, M + m * P:M + (m + 1) * P],
                                                   tmp[:, hd % 2 * T + m * P:hd % 2 * T + (m + 1) * P], ident)
                    last.then_inc(vmem_tr, 1)

            def memory_values_unit(hd, half):
                if hd < C:
                    if hd >= 1 and half == 0:
                        pe.wait_ge(vmem_copied, hd)
                    u = L["xv"].u0 + hd
                    half_unit(u, u % 2, banks[7], (memh, meml), M, half)
            attention(fox, fox_scores, fox_transposes, lambda hd: causal_values(pt_fox, PR["fv"], hd, banks[6]),
                      pair_out_free(fox), memory_values_to_tokens, memory_values_unit)
            bank_free[6] = [(fox.s_lo, 4)]
            bank_free[7] = [(vmem_copied, C)]
            for b in (0, 1, 2):
                bank_free[b] = [(fox.s_exp, 4 * NFOX)]
            for b in (3, 4, 5):
                bank_free[b] = [(fox.s_pt_act, NFOX), (fox.s_pt_dve, 2 * NFOX)]
            for hd in range(NX):
                if hd % 2 == 0:
                    take(4 + hd // 2)
                for d in range(2):
                    pe.wait_ge(kmem_sq, 2 * hd + d + 1)
                    last = mm(banks[4 + hd // 2][:, hd % 2 * M:(hd % 2 + 1) * M], mean_256, chunk(tmp, 2 * hd + d, M),
                              start=d == 0, stop=d == 1)
                last.then_inc(kmem_sum, 1)
            for n in range(2):
                bank_free[4 + n] = [(kmem_rstd, n + 1)]
            pe.wait_ge(gn_lo, 4)
            pe.wait_ge(fox.s_lo, 4)
            dense("out", [X], T, (resid, RESID["out"]))

            def query_sums(hd):
                b = XAT_NORM_BANKS[hd]
                take(b)
                for d in range(2):
                    pe.wait_ge(qn_sq, 2 * hd + d + 1)
                    last = mm(banks[b][:, :], mean_256, chunk(tmp, (2 * hd + d) % 4), start=d == 0, stop=d == 1)
                last.then_inc(qn_sum, 1)
                bank_free[b] = [(qn_rstd, hd + 1)]

            def first_query_sums():
                query_sums(0)
                query_sums(1)
            hooks = spread_hooks("xattn")
            hooks[5] = first_query_sums
            dense("xq", [Y], T, (sc, SCALED["xq"]), ready=(norm_lo, HI_BASE["xattn"]), hooks=hooks)
            pe.wait_ge(kmem_done, C)
            pe.wait_ge(vmem_copied, C)

            def xat_scores(hd):
                pe.wait_ge(qn_done, 2 * hd + 2)
                for q, b, o, w, _ in XAT_GROUPS:
                    for d in range(2):
                        c = 2 * hd + d
                        last = mm(banks[b][:, o:o + w], xq[:, c * T + q * P:c * T + (q + 1) * P], chunk(kmem, c, M),
                                  start=d == 0, stop=d == 1)
                return last

            def xat_transposes(hd):
                for kb in range(2):
                    for q in range(QB):
                        last = nc.tensor.transpose(banks[3 + kb][:, q * P:(q + 1) * P],
                                                   xat.p[:, q * M + kb * P:q * M + (kb + 1) * P], ident)
                return last

            def xat_values(hd):
                for d in range(2):
                    o = (2 * hd + d) * P
                    for kb in range(2):
                        last = mm(banks[6 + d][:, :], vmem[:, kb * D + o:kb * D + o + P], xat.pt[:, kb * T:(kb + 1) * T],
                                  start=kb == 0, stop=kb == 1)
                return last

            def xat_out_free(hd):
                if hd >= 1:
                    pe.wait_ge(xat.s_lo, 2 * hd)

            def later_query_sums(hd):
                if hd == 0:
                    query_sums(2)
                    bank_free[5] = [(qn_rstd, 2)]
                    query_sums(3)
            bank_free.pop(4)
            bank_free.pop(5)
            attention(xat, xat_scores, xat_transposes, xat_values, xat_out_free, later_query_sums)
            for b in (0, 1):
                bank_free[b] = [(xat.s_exp, 4 * NX)]
            bank_free[3], bank_free[4] = [(xat.s_pt_act, NX)], [(xat.s_pt_dve, NX)]
            bank_free[6] = bank_free[7] = [(xat.s_lo, 8)]
            pe.wait_ge(xat.s_lo, 8)
            dense("xo", [Y], T, (resid, RESID["xo"]))

            def ada_sums(g):
                for n in range(ADA_B):
                    o = g * ADA_B + n
                    if n == 0:
                        pe.wait_ge(ada_step, 8 * g + 8)
                    dst = banks[7][:, o:o + 1] if isinstance(o, int) else banks[7][:, bass.ds(o, 1)]
                    last = mm(dst, acc[:, n * P:(n + 1) * P], col("one"), start=True, stop=True)
                last.then_inc(ada_sum, 1)
            dense("gu", [X, X], T, (up_scaled, 0), ready=(norm_lo, HI_BASE["ffn"]), hooks=spread_hooks("ffn"),
                  after_second=ada_sums)
            ada_sums(10)
            bank_free[7] = [(mods_done, 1)]

            def last_ada():
                ada_sums(11)
            down("down", HALVES["gu"] + FC, last_ada)

            def shifted_norm(name):
                norm_columns(name)
                norm_spread(name, free=(norm_xn, 8 * SHIFTED[name] + C))
            shifted_norm("ffn1_2")
            dense("gu1", [X, X], T, (prod, PROD["gu1"]), together=(norm_lo, HI_BASE["ffn1_2"]))
            down("down1", HALVES["gu1"] + FC)
            shifted_norm("mix_2")
            dense("kv", [X], T, (copied, COPIED["kv"]), together=(norm_lo, HI_BASE["mix_2"]))
            dense("qa", [X], T, (copied, COPIED["qa"]))
            rope(qkv, 0, 2, (copied, COPIED["kv"] + 2))
            for n in range(2):
                take(6 + n)
                if n == 0:
                    pe.wait_ge(copied, COPIED["kv"] + 4)
                for s in range(2):
                    for c in range(2):
                        last = nc.tensor.transpose(banks[6 + n][:, s * 2 * P + c * P:s * 2 * P + (c + 1) * P],
                                                   qkv[:, (2 + c) * T + (2 * n + s) * P:(2 + c) * T + (2 * n + s + 1) * P], ident)
                last.then_inc(vsw_tr, 1)
                bank_free[6 + n] = [(vsw_copied, n + 1)]
            dense("qb", [X], T, (copied, COPIED["qb"]))
            rope(qkv, 4, 4, (copied, COPIED["qa"] + 4))
            dense("cu", [X, X], T, (prod, PROD["cu"]))
            rope(qkv, 8, 4, (copied, COPIED["qb"] + 4))
            dense("b", [X], T, (prod, PROD["b"]))

            pe.wait_ge(kdup_in, 16 * 2 * NKV)
            pe.wait_ge(rope_done, 18)
            pe.wait_ge(half_lo, HALVES["b"] + C)

            def swa_scores(hd):
                r0, g = hd % 2 * HD, hd // (NSW // NKV)
                for q, b, o, w, _ in SWA_GROUPS:
                    qq = (4 + hd // 2) * T + q * P
                    k0 = g * T + (q + 1) * P - w
                    mm(banks[b][:, o:o + w], qkv[r0:r0 + HD, qq:qq + P], kdup[r0:r0 + HD, k0:k0 + w], start=True, stop=False)
                    last = mm(banks[b][:, o:o + w], mask16[:, 0:P], mask16[:, 3 * P - w:3 * P], start=False, stop=True)
                return last

            def swa_transposes(hd):
                for n, (q, kb) in enumerate(SWA_PAIRS):
                    last = nc.tensor.transpose(banks[3 + n // 4][:, n % 4 * P:(n % 4 + 1) * P], swa.p[:, n * P:(n + 1) * P], ident)
                return last

            def swa_values(hd):
                r0, g = hd % 2 * HD, hd // (NSW // NKV)
                bank = banks[6 + hd // 2 % 2]
                for n, (q, kb) in enumerate(SWA_PAIRS):
                    last = mm(bank[r0:r0 + HD, q * P:(q + 1) * P], v_sw[:, kb * 256 + g * HD:kb * 256 + (g + 1) * HD],
                              swa.pt[:, n * P:(n + 1) * P], start=q == 0 or kb < q, stop=kb == q)
                return last

            def conv_unit(hd, half):
                if hd < NSW:
                    if hd >= 2 and half == 0:
                        pe.wait_ge(prod, PROD["cz"] + hd // 2)
                    u = L["cz"].u0 + hd
                    half_unit(u, u % 2, banks[5 if hd % 2 else 2], X if hd % 2 else Y, T, half)
            attention(swa, swa_scores, swa_transposes, swa_values, pair_out_free(swa), fill=conv_unit)
            bank_free[2] = bank_free[5] = [(prod, PROD["cz"] + C)]
            for b in (0, 1):
                bank_free[b] = [(swa.s_exp, 4 * NSW)]
            bank_free[3], bank_free[4] = [(swa.s_pt_act, NSW)], [(swa.s_pt_dve, NSW)]
            bank_free[6] = bank_free[7] = [(swa.s_lo, 8)]
            pe.wait_ge(swa.s_lo, 8)
            dense("az", [(oh, ol), X], T, (prod, PROD["az"]))
            pe.wait_ge(half_lo, HALVES["az"] + C)
            dense("out2", [Y], T, (resid, RESID["out2"]))
            shifted_norm("ffn2_2")
            dense("gu2", [X, X], T, (prod, PROD["gu2"]), together=(norm_lo, HI_BASE["ffn2_2"]))
            down("down2", HALVES["gu2"] + FC)
            norm_columns("final")
            norm_spread("final")


def constants():
    d = np.arange(P)
    rot = np.zeros((P, P), np.float32)
    for m in range(P):
        if m % HD < HD // 2:
            rot[m + HD // 2, m] = -1.0
        else:
            rot[m - HD // 2, m] = 1.0
    same_head = (d[:, None] // HD == d[None, :] // HD)
    row, colm = d[:, None], d[None, :]
    window = np.concatenate([np.where(colm > row, 0.0, NEG), np.where(colm <= row, 0.0, NEG)], 1)
    inv = (10000.0 ** (-np.arange(0, HD, 2, dtype=np.float32) / np.float32(HD))).astype(np.float32)
    ang = (inv[d % (HD // 2)][:, None] * np.arange(T, dtype=np.float32)[None, :]).astype(np.float32)
    tables = np.concatenate([np.eye(P), rot, np.full((P, P), 1.0 / D), same_head / HD, np.full((P, P), 1.0 / 256),
                             np.cos(ang), np.sin(ang), window], 1).astype(np.float32)
    assert tables.shape == (P, NTAB)
    log_g = np.log(np.float32(1.0) - np.float32(2.0) ** (-5.0 - np.arange(NRET, dtype=np.float32))).astype(np.float32)
    s, t = np.arange(P)[:, None], np.arange(T)[None, :]
    seen = t // CHUNK >= s // CHUNK
    decays = np.stack([np.where(seen, np.exp(g * np.abs(t - s)), 0.0) * HD ** -0.5 for g in log_g]).astype(np.float32)
    return tables, decays


def column_units(w):
    return w.reshape(C, P, -1, P).transpose(2, 1, 0, 3).reshape(-1, P, UNIT)


def row_units(w):
    return w.reshape(FC // 2, 2, P, 2, 4, P).transpose(3, 0, 2, 1, 4, 5).reshape(-1, P, UNIT)


def interleave(a, b):
    return np.stack([a, b], 1).reshape(-1, P, UNIT)


def lay_out(i):
    def fm(v):
        return np.asarray(v).reshape(-1, P).T

    def split(w, sizes):
        at, out = 0, []
        for n in sizes:
            out.append(w[:, at:at + n])
            at += n
        return out
    rq, rk, rv, rg, fq, fk, fv, ff = split(i["w_in"][0], [512] * 7 + [8])
    ffp = np.zeros((D, P), np.float32)
    ffp[:, 0:8] = ff
    xk, xv = split(i["w_xkv"][0], [D, D])
    b2, c2, u2, q2, k2, v2, zc, za = split(i["w_in_2"][0], [D, D, D, D, 256, 256, D, D])
    cu_ = column_units
    gate, up = cu_(i["w_gate"][0]), cu_(i["w_up"][0])
    g1, p1 = (cu_(w) for w in split(i["w1_gu_2"][0], [FF, FF]))
    g2, p2 = (cu_(w) for w in split(i["w2_gu_2"][0], [FF, FF]))
    parts = [cu_(w) for w in (fq, fk, rq, rk, rv, rg, fv, ffp, xk, xv, i["w_out"][0], i["w_xq"][0], i["w_xo"][0])]
    parts += [interleave(gate, up), row_units(i["w_down"][0]), interleave(g1, p1), row_units(i["w1_down_2"][0]),
              cu_(k2), cu_(v2), cu_(q2), interleave(cu_(c2), cu_(u2)), cu_(b2),
              interleave(cu_(i["w_conv_proj_2"][0]), cu_(zc)), interleave(cu_(i["w_attn_proj_2"][0]), cu_(za)),
              cu_(i["w_out_2"][0]), interleave(g2, p2), row_units(i["w2_down_2"][0])]
    units = np.concatenate(parts, 0)
    assert units.shape == (UNITS, P, UNIT), units.shape
    head_mask = np.zeros((P, 8), np.float32)
    for r in range(P):
        if r % 32 < 8:
            head_mask[r, r % 32] = 1.0
    bf = np.zeros((P, 1), np.float32)
    bf[0:8, 0] = i["b_forget"][0]
    cols = {"g_mem": fm(i["g_mem"][0]), "g_mix": fm(i["g_mix"][0]), "g_xattn": fm(i["g_xattn"][0]),
            "g_ffn": fm(i["g_ffn"][0]), "g_ffn1_2": fm(i["g_ffn1_2"][0]), "g_mix_2": fm(i["g_mix_2"][0]),
            "g_ffn2_2": fm(i["g_ffn2_2"][0]), "g_final": fm(i["g_final_2"]), "g_ret_out": fm(i["g_ret_out"][0].reshape(-1)),
            "g_fox_q": np.tile(i["g_fox_q"][0], 2)[:, None], "g_fox_k": np.tile(i["g_fox_k"][0], 2)[:, None],
            "g_xq": fm(i["g_xq"][0]), "g_xk": fm(i["g_xk"][0]), "b_forget": bf, "conv": fm(i["conv_w_2"][0].reshape(-1)),
            "c": fm(i["c_2"][0]), "b_ada": fm(i["b_ada_2"][0]), "sinks": np.broadcast_to(i["sinks_2"][0][None, :], (P, NSW)),
            "eps": np.full((P, 1), EPS, np.float32), "one": np.ones((P, 1), np.float32), "head_mask": head_mask}
    vectors = np.concatenate([cols[n] for n in VEC], 1)
    assert vectors.shape == (P, NVEC)
    tables, decays = constants()
    out = {"x_t": i["x"][0].T, "mem_t": i["mem"][0].T, "units": units, "w_ada": i["w_ada_2"][0], "vectors": vectors,
           "tables": tables, "decays": decays}
    return {k: np.ascontiguousarray(v) for k, v in out.items()}


def build(nc, arrays):
    aps = {k: nc.dram_tensor(k, list(v.shape), mybir.dt.float32, kind="ExternalInput").ap() for k, v in arrays.items()}
    out_t = nc.dram_tensor("out_t", [D, T], mybir.dt.float32, kind="ExternalOutput").ap()
    two_block_kernel(nc, *[aps[k] for k in ("x_t", "mem_t", "units", "w_ada", "vectors", "tables", "decays")], out_t)


def kernel(**inputs):
    import concourse.bacc as bacc
    from concourse.bass_utils import run_bass_kernel_spmd

    arrays = lay_out({k: np.asarray(v) for k, v in inputs.items()})
    nc = bacc.Bacc("TRN2", target_bir_lowering=False, num_devices=1)
    build(nc, arrays)
    r = run_bass_kernel_spmd(nc, [arrays], core_ids=[0])
    return r.results[0]["out_t"].T[None]
```

```python
from contextlib import ExitStack

import numpy as np
import concourse.bass as bass
from concourse import mybir

D = 1024
T = 512
M = 256
P = 128
C = D // P
QB = T // P
FF = 2816
FC = FF // P
HD = 64
CHUNK = 64
NRET = 8
NFOX = 8
NX = 4
NSW = 16
NKV = 4
NMOD = 9
EPS = 1e-6
NEG = -1e30
UNIT = 8 * P
ADA_G = 12
ADA_W = NMOD * D // ADA_G
ADA_B = ADA_W // P


class Layer:

    def __init__(self, name, u0, n, per):
        self.name, self.u0, self.n, self.per = name, u0, n, per
        self.groups = n // per


def plan_layers():
    shape = [("fq", 4, 1), ("fk", 4, 1), ("rq", 4, 1), ("rk", 4, 1), ("rv", 4, 1), ("rg", 4, 1), ("fv", 4, 1),
             ("ff", 1, 1), ("xk", 8, 1), ("xv", 8, 1), ("out", 8, 1), ("xq", 8, 1), ("xo", 8, 1),
             ("gu", 2 * FC, 2), ("down", FC, 1), ("gu1", 2 * FC, 2), ("down1", FC, 1),
             ("kv", 4, 1), ("qa", 4, 1), ("qb", 4, 1), ("cu", 16, 2), ("b", 8, 1), ("cz", 16, 2), ("az", 16, 2), ("out2", 8, 1),
             ("gu2", 2 * FC, 2), ("down2", FC, 1)]
    layers, u = {}, 0
    for name, n, per in shape:
        layers[name] = Layer(name, u, n, per)
        u += n
    return layers, u


LAYERS, UNITS = plan_layers()
HI_BASE = {n: 8 * i for i, n in enumerate(["mix", "mem", "xattn", "ffn", "ffn1_2", "mix_2", "ffn2_2"])}


def bases(names):
    out, at = {}, 0
    for name in names:
        out[name] = at
        at += 8 if name.startswith("down") else LAYERS[name].groups
    return out


SCALED = bases(["fq", "fk", "rq", "rk", "rv", "rg", "fv", "ff", "xk", "xv", "xq"])
COPIED = bases(["kv", "qa", "qb"])
RESID = bases(["out", "xo", "down", "down1", "out2", "down2"])
PROD = bases(["gu", "gu1", "cu", "b", "cz", "az", "gu2"])
ACTED = bases(["gu", "gu1", "cu", "cz", "az", "gu2"])
HALVES = bases(["gu", "gu1", "b", "az", "gu2"])
SHIFTED = {"ffn1_2": 0, "mix_2": 1, "ffn2_2": 2}
NORMS = {n: i for i, n in enumerate(["mix", "mem", "xattn", "ffn", "ffn1_2", "mix_2", "ffn2_2", "final"])}

VEC = {}
for _name, _n in [("g_mem", 8), ("g_mix", 8), ("g_xattn", 8), ("g_ffn", 8), ("g_ffn1_2", 8), ("g_mix_2", 8),
                  ("g_ffn2_2", 8), ("g_final", 8), ("g_ret_out", 4), ("g_fox_q", 1), ("g_fox_k", 1), ("g_xq", 2),
                  ("g_xk", 2), ("b_forget", 1), ("conv", 24), ("c", 8), ("b_ada", 72), ("sinks", 16), ("eps", 1),
                  ("one", 1), ("head_mask", 8)]:
    VEC[_name] = (sum(n for _, n in VEC.values()), _n)
NVEC = sum(n for _, n in VEC.values())
TAB = {}
for _name, _n in [("ident", P), ("rot", P), ("mean_d", P), ("mean_head", P), ("mean_256", P),
                  ("cos", T), ("sin", T), ("window", 2 * P)]:
    TAB[_name] = (sum(n for _, n in TAB.values()), _n)
NTAB = sum(n for _, n in TAB.values())

FOX_GROUPS = [(3, 0, 0, 512, 768), (2, 1, 0, 384, 384), (0, 1, 384, 128, 0), (1, 2, 0, 256, 128)]
XAT_GROUPS = [(q, q // 2, q % 2 * M, M, q * M) for q in range(QB)]
SWA_GROUPS = [(0, 0, 0, 128, 0), (1, 0, 128, 256, 128), (2, 1, 0, 256, 384), (3, 1, 256, 256, 640)]
XAT_NORM_BANKS = (4, 5, 2, 5)
CAUSAL_KEYS = [(0, 0, 0), (1, 0, 512), (2, 0, 1024), (1, 384, 896)]
SWA_PAIRS = [(0, 0), (1, 0), (1, 1), (2, 1), (2, 2), (3, 2), (3, 3)]


def two_block_kernel(nc, x_t, mem_t, units, w_ada, vectors, tables, decays, out_t):
    f32, f32r = mybir.dt.float32, mybir.dt.float32r
    ALU, ACT, AX = mybir.AluOpType, mybir.ActivationFunctionType, mybir.AxisListType
    L = LAYERS

    with ExitStack() as ctx:
        def sb(name, cols, dt=f32):
            return ctx.enter_context(nc.sbuf_tensor(name, [P, cols], dt))

        def sem(name):
            return ctx.enter_context(nc.semaphore(name))

        h = sb("h", C * T)
        x_at = nc.sbuf_base
        xh, xl = sb("xh", C * T, f32r), sb("xl", C * T, f32r)
        raw, whi, wlo = sb("raw", 4 * UNIT), sb("whi", 2 * UNIT, f32r), sb("wlo", 2 * UNIT, f32r)
        tmp = sb("tmp", 4 * T)
        xn_at = nc.sbuf_base
        xn = sb("xn", 2 * T)
        ssum, rstd = sb("ssum", T), sb("rstd", T)
        r_mem = sb("r_mem", M)
        rcol = sb("rcol", 8)
        mask16 = sb("mask16", 3 * P, mybir.dt.bfloat16)
        tab = sb("tab", NTAB - 2 * P)
        vec = sb("vec", NVEC)
        mx, nm, sm, rs, es = (sb(n, 64) for n in ("mx", "nm", "sm", "rs", "es"))
        mods = sb("mods", NMOD * C)
        gmod = sb("gmod", 6 * C + 1 + C)
        arena_kb = 88
        side = sb("side", 12 * 256)
        arena = sb("arena", arena_kb * 256)

        end = nc.sbuf_base
        arena_at = end - arena_kb * 1024
        side_at = arena_at - 12 * 1024

        def at(name, kb, cols, dt=f32, base=arena_at):
            return nc.alloc_sbuf_tensor_at(name, [P, cols], dt, offset=base + int(kb * 1024))

        PR = {"fq": 0, "fk": 4, "rq": 8, "rk": 12, "rv": 16, "rg": 20, "fv": 24}
        proj = at("proj", 0, 28 * T)
        window = proj[:, PR["fv"] * T:PR["fv"] * T + 2 * P]
        memh, meml = at("memh", 56, C * M, f32r), at("meml", 64, C * M, f32r)
        mem_in = at("mem_in", 72, C * M)
        kmem, vmem = at("kmem", 72, C * M), at("vmem", 80, C * M)
        pt_a, pt_b = at("pt_a", 8, 1280, base=x_at), at("pt_b", 24, 1280, base=x_at)
        p_fox = (at("p_fox", 24, 1280), tmp[:, 4 * T - 1280:4 * T])
        pt_fox = at("pt_fox", 16, 1280)
        xq = at("xq", 32, C * T)
        qroot, qrec = es[:, 0:16], es[:, 16:32]
        p_x, pt_x = (at("p_x0", 48, 1024), at("p_x1", 56, 1024)), at("pt_x", 52, 1024)
        hh, hl = at("hh", 0, FC * T, f32r), at("hl", 44, FC * T, f32r)
        yh, yl = at("yh", 0, C * T, f32r), at("yl", 16, C * T, f32r)
        conv = at("conv", 32, C * T)
        m1 = at("m1", 32, C * T)
        qkv = at("qkv", 48, 12 * T)
        kdup = at("kdup", 72, NKV * T)
        v_sw = at("v_sw", 80, QB * 256)
        p_sw = (at("p_sw", 84, 896), tmp[:, 2 * T:2 * T + 896])
        oh = at("oh", 56, C * T, f32r)
        ol = (at("ol_a", 48, 4 * T, f32r), at("ol_b", 0, 4 * T, f32r, base=xn_at))
        lt = at("lt", 0, T, base=side_at)
        rb = at("rb", 2, T, base=side_at)
        rh = at("rh", 4, 2 * T, base=side_at)
        dec = at("dec", 8, 2 * T, base=side_at)
        ada_w = at("ada_w", 0, 4 * ADA_W, base=side_at)
        cpad = at("cpad", 0, 2 * 514, base=side_at)
        pt_sw = at("pt_sw", 5, 896, base=side_at)

        acc = xn

        banks = [ctx.enter_context(nc.psum_tensor(f"bank{i}", [P, T], f32)) for i in range(8)]

        def chunk(t, c, n=T):
            if isinstance(t, tuple):
                t, c = t[c // 4], c % 4
            return t[:, c * n:(c + 1) * n] if isinstance(c, int) else t[:, bass.ds(c * n, n)]

        def table(name):
            o, n = TAB[name]
            return tab[:, o:o + n]

        def col(name, c=0, rows=slice(None)):
            o = VEC[name][0] + c
            return vec[rows, o:o + 1] if isinstance(o, int) else vec[rows, bass.ds(o, 1)]

        def mod(m, c):
            o = m * C + c
            return mods[:, o:o + 1] if isinstance(o, int) else mods[:, bass.ds(o, 1)]

        def gm(m, c):
            return gmod[:, m * C + c:m * C + c + 1]
        gq8 = gmod[:, 6 * C:6 * C + 1]
        csilu = gmod[:, 6 * C + 1:7 * C + 1]

        ident, mean_d, mean_head, mean_256 = (table(n) for n in ("ident", "mean_d", "mean_head", "mean_256"))

        vec_in, consts_in, mem_loaded = sem("vec_in"), sem("consts_in"), sem("mem_loaded")
        x_loaded = [sem(f"x_loaded{c}") for c in range(C)]
        raw_loaded = [sem(f"raw_loaded{i}") for i in range(4)]
        hi_ready, lo_ready, unit_used = sem("hi_ready"), sem("lo_ready"), sem("unit_used")
        scaled, copied, resid, down_out = sem("scaled"), sem("copied"), sem("resid"), sem("down_out")
        prod, acted, half_hi, half_lo = sem("prod"), sem("acted"), sem("half_hi"), sem("half_lo")
        convolved, merged = sem("convolved"), sem("merged")
        norm_sq, norm_acc, norm_cols, norm_root = (sem(n) for n in ("norm_sq", "norm_acc", "norm_cols", "norm_root"))
        norm_recip, norm_bc, norm_r = sem("norm_recip"), sem("norm_bc"), sem("norm_r")
        norm_xn, norm_hi, norm_lo = sem("norm_xn"), sem("norm_hi"), sem("norm_lo")
        setup_done = sem("setup_done")
        vmem_tr, vmem_copied, gate_silu = (sem(n) for n in ("vmem_tr", "vmem_copied", "gate_silu"))
        kmem_sq, kmem_sum, kmem_root, kmem_rstd, kmem_done = (
            sem(n) for n in ("kmem_sq", "kmem_sum", "kmem_root", "kmem_rstd", "kmem_done"))
        hn_sq, hn_sum, hn_root, hn_rstd, hn_done = (sem(n) for n in ("hn_sq", "hn_sum", "hn_root", "hn_rstd", "hn_done"))
        rope_rot, rope_sin, rope_cos, rope_done = (sem(n) for n in ("rope_rot", "rope_sin", "rope_cos", "rope_done"))
        v_tr, v_copied = sem("v_tr"), sem("v_copied")
        gate_scaled, up_scaled = sem("gate_scaled"), sem("up_scaled")
        gate_act, gate_dve, f_ready = sem("gate_act"), sem("gate_dve"), sem("f_ready")
        dec_in = [sem("dec_in0"), sem("dec_in1")]
        ret_scores, ret_weighted, ret_pv, ret_out = (sem(n) for n in ("ret_scores", "ret_weighted", "ret_pv", "ret_out"))
        gn_mean, gn_xc, gn_sq, gn_var, gn_root = (sem(n) for n in ("gn_mean", "gn_xc", "gn_sq", "gn_var", "gn_root"))
        gn_rstd, gn_t, gn_y, gn_hi, gn_lo = (sem(n) for n in ("gn_rstd", "gn_t", "gn_y", "gn_hi", "gn_lo"))

        class Kind:

            def __init__(self, name, heads, groups, p, pt, scale, key_banks, out_banks, out_hi, out_lo, out_chunk0):
                self.heads, self.groups, self.p, self.pt, self.scale = heads, groups, p, pt, scale
                self.key_banks = key_banks
                self.out_banks = out_banks
                self.out_hi, self.out_lo, self.out_chunk0 = out_hi, out_lo, out_chunk0
                self.s_scores, self.s_max = sem(name + "_scores"), sem(name + "_max")
                self.s_sinkmax, self.s_negmax = sem(name + "_sinkmax"), sem(name + "_negmax")
                self.s_exp, self.s_sink = sem(name + "_exp"), sem(name + "_sink")
                self.s_sum, self.s_recip, self.s_pn = sem(name + "_sum"), sem(name + "_recip"), sem(name + "_pn")
                self.s_tr, self.s_pt_act, self.s_pt_dve = sem(name + "_tr"), sem(name + "_pt_act"), sem(name + "_pt_dve")
                self.s_pv, self.s_hi, self.s_lo = sem(name + "_pv"), sem(name + "_hi"), sem(name + "_lo")

        fox = Kind("fox", NFOX, FOX_GROUPS, p_fox, pt_fox, 1.0, [(3, 512, 0), (4, 512, 512), (5, 256, 1024)], (6,), xh, xl, 4)
        xat = Kind("xat", NX, XAT_GROUPS, p_x, pt_x, 256.0 ** -0.5, [(3, 512, 0), (4, 512, 512)], (6, 7), yh, yl, 0)
        swa = Kind("swa", NSW, SWA_GROUPS, p_sw, pt_sw, HD ** -0.5, [(3, 512, 0), (4, 384, 512)], (6, 7), oh, ol, 0)

        qn_sq, qn_pair, qn_sum, qn_root, qn_rstd, qn_bc, qn_done = (
            sem(n) for n in ("qn_sq", "qn_pair", "qn_sum", "qn_root", "qn_rstd", "qn_bc", "qn_done"))
        ada_in = [sem(f"ada_in{i}") for i in range(4)]
        csilu_done, ada_step, ada_sum, mods_done = sem("csilu_done"), sem("ada_step"), sem("ada_sum"), sem("mods_done")
        kdup_in, vsw_tr, vsw_copied = sem("kdup_in"), sem("vsw_tr"), sem("vsw_copied")
        final_done, stored = sem("final_done"), sem("stored")
        down_names = ("down", "down1", "down2")
        DOWN_BANKS = {"down": (4, 5, 6, 0, 1, 2, 3, 7), "down1": (4, 5, 6, 7, 0, 1, 2, 3), "down2": (4, 5, 6, 7, 0, 1, 2, 3)}

        block = ctx.enter_context(nc.Block())

        def repeat(eng, n, body):
            if n:
                body(0, True)
            if n - 1 >= 2:
                with eng.Fori(1, n) as i:
                    body(i, False)
            elif n == 2:
                body(1, False)

        @block.sync
        def _(sp):
            def load_unit(u, slot, first=False):
                if not first:
                    sp.wait_ge(lo_ready, u - 3)
                sp.dma_start(raw[:, slot * UNIT:(slot + 1) * UNIT],
                             units[u, :, :] if isinstance(u, int) else
                             units[bass.ds(u, 1), :, :].rearrange("a p n -> (a p) n")).then_inc(raw_loaded[slot], 16)

            def load_ada(g, k, first=False):
                slot = k % 4
                if not (first and k < 4):
                    sp.wait_ge(ada_step, g * 8 + k - 3)
                if first and k == 0:
                    sp.wait_ge(fox.s_pv, NFOX)
                cols = slice(g * ADA_W, (g + 1) * ADA_W) if isinstance(g, int) else bass.ds(g * ADA_W, ADA_W)
                sp.dma_start(ada_w[:, slot * ADA_W:(slot + 1) * ADA_W],
                             w_ada[k * P:(k + 1) * P, cols]).then_inc(ada_in[slot], 16)

            def load_x(cs):
                for c in cs:
                    sp.dma_start(chunk(h, c), x_t[c * P:(c + 1) * P, :]).then_inc(x_loaded[c], 16)
            load_unit(0, 0, True)
            load_x((0, 1))
            load_unit(1, 1, True)
            load_x(range(2, C))
            sp.dma_start(tab[:, :], tables[:, 0:NTAB - 2 * P]).then_inc(consts_in, 16)
            sp.dma_start(window, tables[:, NTAB - 2 * P:NTAB]).then_inc(consts_in, 16)
            load_unit(2, 2, True)
            load_unit(3, 3, True)
            sp.dma_start(mem_in[:, :].rearrange("p (c t) -> p c t", c=C),
                         mem_t.rearrange("(c p) t -> p c t", p=P)).then_inc(mem_loaded, 16)
            gu0 = L["gu"].u0
            lead = gu0 // 4 * 4
            with sp.Fori(1, lead // 4) as i:
                for j in range(4):
                    load_unit(4 * i + j, j)
            u = lead
            for _ in range(4):
                load_unit(u, u % 4)
                u += 1

            def round_with_ada(i, first):
                for j in range(4):
                    load_unit(lead + 4 + 4 * i + j, j)
                    load_ada(i, 2 * j, first)
                    load_ada(i, 2 * j + 1, first)
            repeat(sp, 11, round_with_ada)
            u = lead + 4 + 44
            for j in range(4):
                load_unit(u + j, j)
                load_ada(11, 2 * j)
                load_ada(11, 2 * j + 1)
            u += 4
            rounds = (UNITS - u) // 4
            with sp.Fori(0, rounds) as i:
                for j in range(4):
                    load_unit(u + 4 * i + j, j)
            for v in range(u + 4 * rounds, UNITS):
                load_unit(v, v % 4)
            for c in range(C):
                sp.wait_ge(final_done, c + 1)
                sp.dma_start(out_t[c * P:(c + 1) * P, :], chunk(h, c)).then_inc(stored, 16)
            sp.wait_ge(stored, 16 * C)

        @block.gpsimd
        def _(pool):
            def low_part(u, j):
                pool.wait_ge(hi_ready, u + 1)
                pool.tensor_tensor(wlo[:, j % 2 * UNIT:(j % 2 + 1) * UNIT], raw[:, j * UNIT:(j + 1) * UNIT],
                                   whi[:, j % 2 * UNIT:(j % 2 + 1) * UNIT].bitcast(f32), ALU.subtract).then_inc(lo_ready, 1)

            with pool.Fori(0, UNITS // 4) as i:
                for j in range(4):
                    low_part(4 * i + j, j)
            for v in range(UNITS // 4 * 4, UNITS):
                low_part(v, v % 4)

        @block.scalar
        def _(act):
            split_so_far = [0]

            def high_part(u0, i, j):
                v = u0 + j
                if isinstance(i, int):
                    if v + 4 * i >= UNITS or v + 4 * i < split_so_far[0]:
                        return
                    assert v + 4 * i == split_so_far[0]
                    split_so_far[0] += 1
                slot = v % 4
                act.wait_ge(raw_loaded[slot], 16 * (v // 4 + 1) + 16 * i)
                if not (isinstance(i, int) and v + 4 * i < 2):
                    act.wait_ge(unit_used, v - 1 + 4 * i)
                act.activation(whi[:, v % 2 * UNIT:(v % 2 + 1) * UNIT], raw[:, slot * UNIT:(slot + 1) * UNIT],
                               ACT.Copy).then_inc(hi_ready, 1)

            def run_layer(name, epilogue, between_units=None, second_ahead=False):
                lay = L[name]

                def body(i, first):
                    for j in range(4):
                        high_part(lay.u0, i, j + 1)
                        if between_units and j % 2 == 0:
                            between_units(i, first, j)
                        if (j + 1) % lay.per == 0:
                            act.wait_ge(unit_used, lay.u0 + j + 1 + 4 * i)
                            if second_ahead and isinstance(i, int) and 4 * i + j == lay.n - 1:
                                high_part(lay.u0, i, j + 2)
                            g = (4 * i + j) // lay.per if isinstance(i, int) else (
                                4 * i + j if lay.per == 1 else 2 * i + j // 2)
                            epilogue(g, j)
                repeat(act, lay.n // 4, body)
                if lay.n >= 12:
                    split_so_far[0] = lay.u0 + lay.n // 4 * 4 + 1
                for r in range(lay.n // 4 * 4, lay.n):
                    high_part(lay.u0, 0, r + 1)
                    act.wait_ge(unit_used, lay.u0 + r + 1)
                    epilogue(r, r % 4)

            def run_split_only(name):
                lay = L[name]

                def body(i, first):
                    for j in range(4):
                        high_part(lay.u0, i, j + 1)
                repeat(act, lay.n // 4, body)
                if lay.n >= 12:
                    split_so_far[0] = lay.u0 + lay.n // 4 * 4 + 1
                for r in range(lay.n // 4 * 4, lay.n):
                    high_part(lay.u0, 0, r + 1)

            def copy_to(dest, c0, n, func=ACT.Copy):
                def epilogue(g, j):
                    act.activation(chunk(dest, c0 + g, n), banks[j][:, 0:n], func).then_inc(copied, 1)
                return epilogue

            def norm_chunk(name, g, j, src=h, n=T, dst=None, gain=None):
                if not (isinstance(g, int) and g < 4):
                    act.wait_ge(norm_acc, 6 * NORMS[name] + g - 3)
                act.activation(tmp[:, j * T:j * T + n], chunk(src, g, n), ACT.Square).then_inc(norm_sq, 1)
                if dst is not None:
                    act.activation(chunk(dst, g, n), chunk(src, g, n), ACT.Copy, scale=col(gain, g)).then_inc(norm_hi, 1)

            def norm_root_of(name, n_blocks=QB, bank=7):
                i = NORMS[name]
                act.wait_ge(norm_cols, i + 1)
                act.activation(rcol[:, 0:n_blocks], banks[bank][:, 0:n_blocks], ACT.Sqrt, bias=col("eps")).then_inc(norm_root, 1)

            def norm_r_copy(name, n=T, bank=7, dst=rstd):
                act.wait_ge(norm_bc, NORMS[name] + 1)
                act.activation(dst[:, 0:n], banks[bank][:, 0:n], ACT.Copy).then_inc(norm_r, 1)

            def norm_high(name, dst, shift):
                for c in range(C):
                    act.wait_ge(norm_xn, 8 * SHIFTED[name] + c + 1)
                    act.activation(chunk(dst, c), xn[:, c % 2 * T:c % 2 * T + T], ACT.Identity,
                                   bias=mod(shift, c)).then_inc(norm_hi, 1)

            def residual_layer(name, norm, dst=None, gain=None):
                def epilogue(g, j):
                    act.wait_ge(resid, RESID[name] + g + 1)
                    norm_chunk(norm, g, j, dst=dst, gain=gain)
                run_layer(name, epilogue, second_ahead=True)

            def down_layer(name, norm, dst=None, gain=None):
                lay = L[name]
                half = FC // 2

                def chunks(cs):
                    for c in cs:
                        act.wait_ge(resid, RESID[name] + c + 1)
                        norm_chunk(norm, c, c % 4, dst=dst, gain=gain)

                def body(i, first, u0=0):
                    for j in range(4):
                        high_part(lay.u0 + u0, i, j + 1)
                repeat(act, 2, body)
                for r in range(8, half):
                    high_part(lay.u0, 0, r + 1)
                high_part(lay.u0, 0, half + 1)
                chunks((0, 1))
                high_part(lay.u0, 0, half + 2)
                chunks((2, 3))
                for r in range(half + 2, FC):
                    high_part(lay.u0, 0, r + 1)
                chunks((4, 5, 6, 7))

            def values_copy(n, c0, b0):
                act.wait_ge(v_tr, QB * (n + 1))
                for s in range(QB):
                    act.activation(chunk(proj, c0 + s), banks[b0 + s][:, :], ACT.Copy).then_inc(v_copied, 1)

            def head_square(c0, b, c, ready):
                act.wait_ge(*ready)
                if b == 0:
                    if c < 3:
                        act.wait_ge(norm_acc, 4 + c)
                act.activation(chunk(tmp, c), chunk(proj, c0 + c), ACT.Square).then_inc(hn_sq, 1)

            def head_root(b, c):
                act.wait_ge(hn_sum, b + c + 1)
                act.activation(banks[4 + c][:, :], banks[4 + c][:, :], ACT.Sqrt, bias=col("eps")).then_inc(hn_root, 1)

            def pair_layer(name, func, split_to=None):
                member = {"gu": 0, "gu1": 0, "gu2": 0, "cu": 0, "cz": 1, "az": 1}[name]
                a0, h0, p0 = ACTED[name], HALVES.get(name, 0), PROD[name]

                def split_product(g, s):
                    if name == "az":
                        act.wait_ge(merged, g + 1)
                    else:
                        act.wait_ge(prod, p0 + g + 1)
                    act.activation(chunk(split_to, g), chunk(tmp, 2 + s), ACT.Copy).then_inc(half_hi, 1)

                def epilogue(g, j):
                    s = (j // 2) % 2
                    if name in ("gu",):
                        act.wait_ge(gate_scaled, g + 1)
                        act.activation(chunk(tmp, s), chunk(tmp, s), func).then_inc(acted, 1)
                    else:
                        act.wait_ge(prod, p0 + g - 1)
                        act.activation(chunk(tmp, s), banks[j - 1 + member][:, :], func).then_inc(acted, 1)

                def between_units(i, first, j):
                    if split_to is not None and not (first and j == 0):
                        split_product(2 * i + j // 2 - 1, (j // 2 + 1) % 2)
                run_layer(name, epilogue, between_units)
                if split_to is not None:
                    split_product(L[name].groups - 1, (L[name].groups - 1) % 2)

            def copy_transposed(k, hd):
                if hd >= 1:
                    act.wait_ge(k.s_tr, hd)
                    if hd >= 2:
                        act.wait_ge(k.s_pv, hd - 1)
                    b, w, o = k.key_banks[0]
                    act.activation(k.pt[:, o:o + w], banks[b][:, 0:w], ACT.Copy).then_inc(k.s_pt_act, 1)

            def attention(k, evac, filler=None, copy_first=False):
                for hd in range(k.heads + 1):
                    if filler:
                        filler(hd)
                    if copy_first:
                        copy_transposed(k, hd)
                    if hd < k.heads:
                        act.wait_ge(k.s_negmax, hd + 1)
                        if hd >= 2:
                            act.wait_ge(k.s_tr, hd - 1)
                        p = k.p[hd % 2]
                        for q, b, o, w, po in k.groups:
                            act.activation(p[:, po:po + w], banks[b][:, o:o + w], ACT.Exp,
                                           bias=nm[:, 4 * hd + q:4 * hd + q + 1], scale=k.scale,
                                           accum_out=sm[:, 4 * hd + q:4 * hd + q + 1]).then_inc(k.s_exp, 1)
                        if k is swa:
                            act.activation(es[:, 4 * hd:4 * hd + 4], nm[:, 4 * hd:4 * hd + 4], ACT.Exp,
                                           bias=col("sinks", hd)).then_inc(k.s_sink, 1)
                    if not copy_first:
                        copy_transposed(k, hd)
                    if hd >= 1:
                        evac(hd - 1)

            def pair_evac(k):
                def evac(hd):
                    if hd % 2:
                        act.wait_ge(k.s_pv, hd + 1)
                        act.activation(chunk(k.out_hi, k.out_chunk0 + hd // 2), banks[k.out_banks[hd // 2 % len(k.out_banks)]][:, :],
                                       ACT.Copy).then_inc(k.s_hi, 1)
                return evac

            act.dma_start(vec[:, :], vectors).then_inc(vec_in, 16)
            high_part(0, 0, 0)
            act.wait_ge(vec_in, 16)
            for c in range(C):
                act.wait_ge(x_loaded[c], 16)
                norm_chunk("mix", c, c % 4, dst=xh, gain="g_mix")
                if c == 0:
                    high_part(0, 0, 1)
            high_part(0, 0, 2)
            norm_root_of("mix")
            high_part(0, 0, 3)
            norm_r_copy("mix")
            run_split_only("fq")
            for j in range(4):
                high_part(L["fk"].u0, 0, j + 1)
                head_square(PR["fq"], 0, j, (scaled, SCALED["fq"] + j + 1))
            for j in range(4):
                high_part(L["rq"].u0, 0, j + 1)
                head_root(0, j)
                act.wait_ge(scaled, SCALED["fk"] + j + 1)
                head_square(PR["fk"], 4, j, (hn_sum, j + 1))
            for j in range(4):
                high_part(L["rk"].u0, 0, j + 1)
                head_root(4, j)
            act.wait_ge(mem_loaded, 16)
            act.wait_ge(hn_sum, 8)
            for j in range(4):
                high_part(L["rv"].u0, 0, j + 1)
                for c in (2 * j, 2 * j + 1):
                    norm_chunk("mem", c, c % 4, mem_in, M, memh, "g_mem")
            for j in range(4):
                high_part(L["rg"].u0, 0, j + 1)
                if j == 2:
                    norm_root_of("mem", 2, 4)
            norm_r_copy("mem", M, 4, r_mem)
            for c in range(4):
                act.wait_ge(scaled, SCALED["rg"] + c + 1)
                act.activation(chunk(proj, PR["rg"] + c), chunk(proj, PR["rg"] + c), ACT.Silu).then_inc(gate_silu, 1)
            for n in range(2):
                act.dma_start(chunk(dec, n), decays[n, :, :]).then_inc(dec_in[n], 16)
            run_split_only("fv")
            run_split_only("ff")
            values_copy(0, PR["rv"], 4)
            values_copy(1, PR["fv"], 0)

            def split_ahead(u):
                if u + 1 < UNITS:
                    high_part(u + 1, 0, 0)

            def forget_gate():
                act.wait_ge(scaled, SCALED["ff"] + 1)
                bf = col("b_forget", 0, slice(0, 8))
                act.activation(tmp[0:8, T:2 * T], tmp[0:8, 0:T], ACT.Abs, bias=bf).then_inc(gate_act, 1)
                act.wait_ge(gate_act, 1)
                act.activation(tmp[0:8, T:2 * T], tmp[0:8, T:2 * T], ACT.Exp, scale=-1.0).then_inc(gate_act, 1)
                act.wait_ge(gate_act, 2)
                act.activation(tmp[0:8, T:2 * T], tmp[0:8, T:2 * T], ACT.Ln, bias=col("one", 0, slice(0, 8))).then_inc(gate_act, 1)

            def ret_norm_step(s):
                if s % 2 == 1 and 3 <= s <= NRET + 1:
                    p = (s - 3) // 2
                    act.wait_ge(gn_xc, p + 1)
                    act.activation(chunk(tmp, p), chunk(proj, PR["rq"] + p), ACT.Square).then_inc(gn_sq, 1)
                if s % 2 == 0 and 4 <= s <= NRET + 2:
                    p = (s - 4) // 2
                    act.wait_ge(gn_var, p + 1)
                    act.activation(banks[6][:, :], banks[6][:, :], ACT.Sqrt, bias=col("eps")).then_inc(gn_root, 1)
                if s % 2 == 1 and 5 <= s:
                    p = (s - 5) // 2
                    act.wait_ge(gn_y, p + 1)
                    act.activation(chunk(xh, p), chunk(proj, PR["rg"] + p), ACT.Copy).then_inc(gn_hi, 1)

            for s in range(NRET + 1):
                if s < C:
                    split_ahead(L["xk"].u0 + s)
                if s == 0:
                    forget_gate()
                if s == 3:
                    act.wait_ge(f_ready, 1)
                if 1 <= s < NRET - 1:
                    act.wait_ge(ret_weighted, 4 * s)
                    act.dma_start(chunk(dec, (s + 1) % 2), decays[s + 1, :, :]).then_inc(dec_in[(s + 1) % 2], 16)
                if s % 2 == 0 and 2 <= s <= NRET:
                    p = s // 2 - 1
                    act.wait_ge(ret_pv, s)
                    act.activation(chunk(proj, PR["rq"] + p), banks[3 + p % 2][:, :], ACT.Copy).then_inc(ret_out, 1)
                ret_norm_step(s)

            def values_filler(hd):
                if hd <= C:
                    split_ahead(L["xv"].u0 + hd)
                if hd < 3:
                    ret_norm_step(NRET + 1 + hd)
                if hd >= 1:
                    act.wait_ge(vmem_tr, hd)
                    act.activation(vmem[:, :].rearrange("p (m n) -> p m n", m=2)[:, :, (hd - 1) * P:hd * P],
                                   banks[7][:, M:2 * M].rearrange("p (m n) -> p m n", m=2), ACT.Copy).then_inc(vmem_copied, 1)
            attention(fox, pair_evac(fox), values_filler)
            act.wait_ge(vmem_tr, C)
            for c in range(C):
                act.activation(chunk(tmp, c, M), chunk(kmem, c, M), ACT.Square).then_inc(kmem_sq, 1)
            high_part(L["out"].u0, 0, 2)
            high_part(L["out"].u0, 0, 3)
            act.wait_ge(kmem_sum, NX)
            for n in range(2):
                act.activation(banks[4 + n][:, :], banks[4 + n][:, :], ACT.Sqrt, bias=col("eps")).then_inc(kmem_root, 1)
            residual_layer("out", "xattn", yh, "g_xattn")

            def query_squares(half, js, tmp_free):
                for c in js:
                    act.wait_ge(scaled, SCALED["xq"] + 4 * half + c + 1)
                    if tmp_free and c % 2 == 0:
                        act.wait_ge(*tmp_free(c))
                    act.activation(chunk(tmp, c), chunk(xq, 4 * half + c), ACT.Square).then_inc(qn_sq, 1)

            def query_roots(pair):
                act.wait_ge(qn_sum, pair + 1)
                act.activation(qroot[:, 8 * pair:8 * pair + 8], banks[6 + pair][:, 0:8], ACT.Sqrt,
                               bias=col("eps")).then_inc(qn_root, 1)
            lay = L["xq"]
            high_part(lay.u0, 0, 1)
            high_part(lay.u0, 0, 2)
            high_part(lay.u0, 0, 3)
            norm_root_of("xattn")
            norm_r_copy("xattn")
            for r in range(3, 6):
                high_part(lay.u0, 0, r + 1)
            query_squares(0, range(4), None)
            high_part(lay.u0, 0, 7)
            query_roots(0)
            high_part(lay.u0, 0, 8)
            query_squares(1, range(4), lambda c: (qn_sum, 1))

            def later_roots(hd):
                if hd == 1:
                    query_roots(1)
                if hd == 2:
                    high_part(L["xo"].u0, 0, 1)

            def xat_evac(hd):
                act.wait_ge(xat.s_pv, hd + 1)
                for d in range(2):
                    act.activation(chunk(yh, 2 * hd + d), banks[6 + d][:, :], ACT.Copy).then_inc(xat.s_hi, 1)
            attention(xat, xat_evac, later_roots, copy_first=True)
            act.activation(csilu, vec[:, VEC["c"][0]:VEC["c"][0] + C], ACT.Silu).then_inc(csilu_done, 1)
            high_part(L["xo"].u0, 0, 2)
            high_part(L["xo"].u0, 0, 3)
            residual_layer("xo", "ffn", xh, "g_ffn")
            high_part(L["gu"].u0, 0, 1)
            high_part(L["gu"].u0, 0, 2)
            high_part(L["gu"].u0, 0, 3)
            norm_root_of("ffn")
            norm_r_copy("ffn")
            pair_layer("gu", ACT.Silu, hh)
            down_layer("down", "ffn1_2")
            norm_root_of("ffn1_2")
            high_part(L["gu1"].u0, 0, 1)
            norm_high("ffn1_2", xh, 0)
            pair_layer("gu1", ACT.Silu, hh)
            down_layer("down1", "mix_2")
            norm_root_of("mix_2")
            high_part(L["kv"].u0, 0, 1)
            norm_high("mix_2", xh, 3)
            run_layer("kv", copy_to(qkv, 0, T))
            run_layer("qa", copy_to(qkv, 4, T))
            for n in range(2):
                act.wait_ge(vsw_tr, n + 1)
                act.activation(chunk(v_sw, n), banks[6 + n][:, :], ACT.Copy).then_inc(vsw_copied, 1)
            run_layer("qb", copy_to(qkv, 8, T))
            act.wait_ge(rope_done, 10)
            for g in range(NKV):
                for half in range(2):
                    act.dma_start(kdup[half * HD:(half + 1) * HD, g * T:(g + 1) * T],
                                  qkv[g % 2 * HD:(g % 2 + 1) * HD, g // 2 * T:(g // 2 + 1) * T]).then_inc(kdup_in, 16)
            pair_layer("cu", ACT.Copy)

            def gated_high(g, j):
                s = j % 2
                act.wait_ge(prod, PROD["b"] + g + 1)
                act.activation(chunk(yh, g), chunk(tmp, 2 + s), ACT.Copy).then_inc(half_hi, 1)
            run_layer("b", gated_high)

            def conv_filler(hd):
                if hd <= NSW:
                    split_ahead(L["cz"].u0 + hd)
                if hd % 2 == 0 and hd >= 2:
                    g = hd // 2 - 1
                    act.wait_ge(unit_used, L["cz"].u0 + hd)
                    act.wait_ge(prod, PROD["cz"] + g - 1)
                    act.activation(chunk(tmp, g % 2), banks[5][:, :], ACT.Sigmoid).then_inc(acted, 1)
            attention(swa, pair_evac(swa), conv_filler)
            pair_layer("az", ACT.Sigmoid, yh)
            residual_layer("out2", "ffn2_2")
            norm_root_of("ffn2_2")
            high_part(L["gu2"].u0, 0, 1)
            norm_high("ffn2_2", xh, 6)
            pair_layer("gu2", ACT.Silu, hh)
            down_layer("down2", "final")
            norm_root_of("final")

        @block.vector
        def _(dve):
            tt, ts, stt = dve.tensor_tensor, dve.tensor_scalar, dve.scalar_tensor_tensor

            def norm_chunk(name, c, src=h, n=T, dst=None, gain=None):
                i = NORMS[name]
                dve.wait_ge(norm_sq, 8 * i + c + 1)
                if 1 <= c < C - 1:
                    if c >= 2:
                        dve.wait_ge(norm_acc, 6 * i + c - 1)
                    t = tmp[:, c % 4 * T:c % 4 * T + n]
                    tt(ssum[:, 0:n], tmp[:, 0:n] if c == 1 else ssum[:, 0:n], t, ALU.add).then_inc(norm_acc, 1)
                if dst is not None:
                    dve.wait_ge(norm_hi, HI_BASE[name] + c + 1)
                    stt(chunk(dst[1], c, n), chunk(src, c, n), col(gain, c), chunk(dst[0], c, n).bitcast(f32),
                        ALU.mult, ALU.subtract).then_inc(norm_lo, 1)

            def norm_recip_of(name, n_blocks=QB):
                i = NORMS[name]
                dve.wait_ge(norm_root, i + 1)
                dve.reciprocal(rcol[:, 4:4 + n_blocks], rcol[:, 0:n_blocks]).then_inc(norm_recip, 1)

            def norm_shifted(name, dst, gain, shift):
                i, b = NORMS[name], HI_BASE[name]
                norm_recip_of(name)
                dve.wait_ge(norm_bc, i + 1)

                def low(c):
                    dve.wait_ge(norm_hi, b + c + 1)
                    stt(chunk(dst[1], c), xn[:, c % 2 * T:c % 2 * T + T], mod(shift, c), chunk(dst[0], c).bitcast(f32),
                        ALU.add, ALU.subtract).then_inc(norm_lo, 1)

                for c in range(C):
                    if c >= 2:
                        dve.wait_ge(norm_lo, b + c - 1)
                    stt(xn[:, c % 2 * T:c % 2 * T + T], chunk(h, c), gain(c), banks[7][:, :],
                        ALU.mult, ALU.mult).then_inc(norm_xn, 1)
                    if c >= 1:
                        low(c - 1)
                low(C - 1)

            def scale_units(name, dest, n=T, first=0, last=None):
                lay = L[name]
                for j in range(first, lay.n if last is None else last):
                    dve.wait_ge(unit_used, lay.u0 + j + 1)
                    tt(dest(j), banks[j % 4][:, 0:n], rstd[:, 0:n], ALU.mult).then_inc(scaled, 1)

            def to_proj(c0):
                return lambda j: chunk(proj, c0 + j)

            def head_norm(c0, b, c, gain):
                dve.wait_ge(hn_root, b + c + 1)
                if b + c >= 2:
                    dve.wait_ge(hn_done, b + c - 1)
                dve.reciprocal(chunk(xn, c % 2), banks[4 + c][:, :]).then_inc(hn_rstd, 1)
                dve.wait_ge(hn_rstd, b + c + 1)
                stt(chunk(proj, c0 + c), chunk(proj, c0 + c), gain, chunk(xn, c % 2), ALU.mult, ALU.mult).then_inc(hn_done, 1)

            rope_n = [0]

            def rope(buf, c0, n, own=None):
                if own:
                    dve.wait_ge(*own)
                for c in range(n):
                    r = rope_n[0]
                    x = chunk(buf, c0 + c)
                    dve.wait_ge(rope_rot, r + 1)
                    if r >= 2:
                        dve.wait_ge(rope_done, r - 1)
                    tt(chunk(xn, r % 2), banks[4 + c % 4][:, :], table("sin"), ALU.mult).then_inc(rope_sin, 1)
                    tt(x, x, table("cos"), ALU.mult).then_inc(rope_cos, 1)
                    dve.wait_ge(rope_sin, r + 1)
                    dve.wait_ge(rope_cos, r + 1)
                    tt(x, x, chunk(xn, r % 2), ALU.add).then_inc(rope_done, 1)
                    rope_n[0] += 1

            def residual(name, norm, gate=None, dst=None, gain=None, between=None):
                lay = L[name]
                for j in range(C):
                    if name in down_names:
                        if j % 4 < 3:
                            dve.wait_ge(down_out, 6 * down_names.index(name) + j // 4 * 3 + j % 4 + 1)
                        else:
                            dve.wait_ge(unit_used, lay.u0 + FC // 2 * (j // 4 + 1))
                        bank = banks[DOWN_BANKS[name][j]]
                    else:
                        dve.wait_ge(unit_used, lay.u0 + j + 1)
                        bank = banks[j % 4]
                    if gate is None:
                        tt(chunk(h, j), bank[:, :], chunk(h, j), ALU.add).then_inc(resid, 1)
                    else:
                        stt(chunk(h, j), bank[:, :], gate(j), chunk(h, j), ALU.mult, ALU.add).then_inc(resid, 1)
                    if j >= 1:
                        norm_chunk(norm, j - 1, dst=dst, gain=gain)
                    if between:
                        between(j)
                norm_chunk(norm, C - 1, dst=dst, gain=gain)

            def pairs(name, split_to=None, extra=None):
                lay = L[name]
                a0, h0, p0 = ACTED[name], HALVES.get(name, 0), PROD[name]

                def one(g, i, j):
                    dve.wait_ge(unit_used, lay.u0 + 2 * j + 2 + 4 * i)
                    if name == "gu":
                        if not (isinstance(g, int) and g < 2):
                            dve.wait_ge(half_lo, g - 1)
                        tt(chunk(tmp, j), banks[2 * j][:, :], rstd[:, :], ALU.mult).then_inc(gate_scaled, 1)
                        tt(chunk(tmp, 2 + j), banks[2 * j + 1][:, :], rstd[:, :], ALU.mult).then_inc(up_scaled, 1)
                        dve.wait_ge(acted, a0 + g + 1)
                        dve.wait_ge(up_scaled, g + 1)
                        t = chunk(tmp, 2 + j)
                        tt(t, t, chunk(tmp, j), ALU.mult).then_inc(prod, 1)
                        dve.wait_ge(half_hi, h0 + g + 1)
                        tt(chunk(split_to[1], g), t, chunk(split_to[0], g).bitcast(f32), ALU.subtract).then_inc(half_lo, 1)
                        return
                    dve.wait_ge(acted, a0 + g + 1)
                    member = 1 if name in ("gu", "gu1", "gu2", "cu") else 0
                    bank = banks[2 * j + member]
                    if name == "cu":
                        if not (isinstance(g, int) and g < 2):
                            dve.wait_ge(convolved, 3 * g - 3)
                        o = j * 514
                        tt(cpad[:, o + 2:o + 514], chunk(tmp, j), bank[:, :], ALU.mult).then_inc(prod, 1)
                        dve.wait_ge(prod, p0 + g + 1)
                        y = chunk(conv, g)
                        ts(y, cpad[:, o:o + T], col("conv", g), None, ALU.mult).then_inc(convolved, 1)
                        dve.wait_ge(convolved, 3 * g + 1)
                        stt(y, cpad[:, o + 1:o + 1 + T], col("conv", C + g), y, ALU.mult, ALU.add).then_inc(convolved, 1)
                        dve.wait_ge(convolved, 3 * g + 2)
                        stt(y, cpad[:, o + 2:o + 2 + T], col("conv", 2 * C + g), y, ALU.mult, ALU.add).then_inc(convolved, 1)
                    else:
                        t = chunk(tmp, 2 + j)
                        dve.wait_ge(half_lo, h0 + g - 1)
                        tt(t, chunk(tmp, j), bank[:, :], ALU.mult).then_inc(prod, 1)
                        if name == "az":
                            dve.wait_ge(prod, p0 + g + 1)
                            tt(t, t, chunk(m1, g), ALU.add).then_inc(merged, 1)
                        dve.wait_ge(half_hi, h0 + g + 1)
                        tt(chunk(split_to[1], g), t, chunk(split_to[0], g).bitcast(f32), ALU.subtract).then_inc(half_lo, 1)

                def body(i, first):
                    one(2 * i, i, 0)
                    if extra:
                        extra(i, first, range(0, 4))
                    one(2 * i + 1, i, 1)
                    if extra:
                        extra(i, first, range(4, 8))
                repeat(dve, lay.n // 4, body)

            def ada_group(g, first, ks=range(C)):
                if 0 in ks and first:
                    dve.wait_ge(csilu_done, 1)
                    dve.wait_ge(qn_done, C)
                elif 0 in ks:
                    dve.wait_ge(ada_sum, g)
                for k in ks:
                    dve.wait_ge(ada_in[k % 4], 32 * g + 16 * (k // 4) + 16)
                    w = ada_w[:, k % 4 * ADA_W:(k % 4 + 1) * ADA_W]
                    if k == 0:
                        ts(acc[:, 0:ADA_W], w, csilu[:, 0:1], None, ALU.mult).then_inc(ada_step, 1)
                    else:
                        dve.wait_ge(ada_step, 8 * g + k)
                        stt(acc[:, 0:ADA_W], w, csilu[:, k:k + 1], acc[:, 0:ADA_W], ALU.mult, ALU.add).then_inc(ada_step, 1)

            def attention(k, before_head=None, evac=None, filler=None, during_exp=None):
                for hd in range(k.heads + 1):
                    if filler:
                        filler(hd)
                    if hd < k.heads:
                        if before_head:
                            before_head(hd)
                        dve.wait_ge(k.s_scores, hd + 1)
                        for q, b, o, w, _ in k.groups:
                            dve.reduce_max(mx[:, 4 * hd + q:4 * hd + q + 1], banks[b][:, o:o + w], AX.X).then_inc(k.s_max, 1)
                        dve.wait_ge(k.s_max, 4 * hd + 4)
                        m4, n4 = mx[:, 4 * hd:4 * hd + 4], nm[:, 4 * hd:4 * hd + 4]
                        if k is swa:
                            ts(m4, m4, k.scale, col("sinks", hd), ALU.mult, ALU.max).then_inc(k.s_sinkmax, 1)
                            dve.wait_ge(k.s_sinkmax, hd + 1)
                            ts(n4, m4, -1.0, None, ALU.mult).then_inc(k.s_negmax, 1)
                        else:
                            ts(n4, m4, -k.scale, None, ALU.mult).then_inc(k.s_negmax, 1)
                    if hd >= 1:
                        dve.wait_ge(k.s_tr, hd)
                        if hd >= 2:
                            dve.wait_ge(k.s_pv, hd - 1)
                        for b, w, o in k.key_banks[1:]:
                            dve.tensor_copy(k.pt[:, o:o + w], banks[b][:, 0:w]).then_inc(k.s_pt_dve, 1)
                    if during_exp:
                        during_exp(hd)
                    if hd < k.heads:
                        s4, r4 = sm[:, 4 * hd:4 * hd + 4], rs[:, 4 * hd:4 * hd + 4]
                        dve.wait_ge(k.s_exp, 4 * hd + 4)
                        if k is swa:
                            dve.wait_ge(k.s_sink, hd + 1)
                            tt(s4, s4, es[:, 4 * hd:4 * hd + 4], ALU.add).then_inc(k.s_sum, 1)
                            dve.wait_ge(k.s_sum, hd + 1)
                        dve.reciprocal(r4, s4).then_inc(k.s_recip, 1)
                        dve.wait_ge(k.s_recip, hd + 1)
                        for q, b, o, w, po in k.groups:
                            p = k.p[hd % 2][:, po:po + w]
                            ts(p, p, rs[:, 4 * hd + q:4 * hd + q + 1], None,
                               ALU.mult).then_inc(k.s_pn, 1)
                    if hd >= 1:
                        evac(hd - 1)

            def pair_evac(k):
                def evac(hd):
                    if hd % 2:
                        c = k.out_chunk0 + hd // 2
                        dve.wait_ge(k.s_hi, hd // 2 + 1)
                        tt(chunk(k.out_lo, c), banks[k.out_banks[hd // 2 % len(k.out_banks)]][:, :], chunk(k.out_hi, c).bitcast(f32),
                           ALU.subtract).then_inc(k.s_lo, 1)
                return evac

            dve.memset(lt[:, :], 0.0).then_inc(setup_done, 1)
            dve.memset(rb[:, :], 0.0).then_inc(setup_done, 1)
            dve.wait_ge(setup_done, 2)
            for p0 in (0, HD):
                dve.memset(lt[p0 + 32:p0 + 40, :], -1.0).then_inc(setup_done, 1)
                dve.memset(rb[p0:p0 + 8, :], 1.0).then_inc(setup_done, 1)
            dve.wait_ge(vec_in, 16)
            for c in range(C):
                dve.wait_ge(x_loaded[c], 16)
                norm_chunk("mix", c, dst=(xh, xl), gain="g_mix")
            ts(gq8, col("g_fox_q"), HD ** -0.5, None, ALU.mult).then_inc(setup_done, 1)
            dve.wait_ge(consts_in, 32)
            o = TAB["ident"][0]
            dve.tensor_copy(mask16[:, 0:P], tab[:, o:o + P]).then_inc(setup_done, 1)
            dve.tensor_copy(mask16[:, P:3 * P], window).then_inc(setup_done, 1)
            norm_recip_of("mix")
            dve.wait_ge(norm_r, 1)
            scale_units("fq", to_proj(PR["fq"]))
            scale_units("fk", to_proj(PR["fk"]))
            dve.wait_ge(setup_done, 9)
            for j in range(4):
                scale_units("rq", to_proj(PR["rq"]), first=j, last=j + 1)
                head_norm(PR["fq"], 0, j, gq8)
            for j in range(4):
                scale_units("rk", to_proj(PR["rk"]), first=j, last=j + 1)
                head_norm(PR["fk"], 4, j, col("g_fox_k"))
            dve.wait_ge(mem_loaded, 16)
            for j in range(4):
                scale_units("rv", to_proj(PR["rv"]), first=j, last=j + 1)
                for c in (2 * j, 2 * j + 1):
                    norm_chunk("mem", c, mem_in, M, (memh, meml), "g_mem")
            scale_units("rg", to_proj(PR["rg"]), last=3)
            norm_recip_of("mem", 2)
            scale_units("rg", to_proj(PR["rg"]), first=3)
            rope(proj, PR["rq"], 4, (hn_done, 8))
            scale_units("fv", to_proj(PR["fv"]))
            rope(proj, PR["rk"], 4)
            dve.wait_ge(hn_sum, 8)
            dve.wait_ge(norm_cols, 2)
            dve.wait_ge(unit_used, L["ff"].u0 + 1)
            tt(tmp[0:8, 0:T], banks[0][0:8, :], rstd[0:8, :], ALU.mult).then_inc(scaled, 1)
            def cumulative_forget():
                dve.wait_ge(scaled, SCALED["ff"] + 1)
                ts(tmp[0:8, 2 * T:3 * T], tmp[0:8, 0:T], col("b_forget", 0, slice(0, 8)), 0.0, ALU.add, ALU.min).then_inc(gate_dve, 1)
                dve.wait_ge(gate_dve, 1)
                dve.wait_ge(gate_act, 3)
                tt(tmp[0:8, 3 * T:4 * T], tmp[0:8, 2 * T:3 * T], tmp[0:8, T:2 * T], ALU.subtract).then_inc(gate_dve, 1)
                dve.wait_ge(gate_dve, 2)
                dve.tensor_tensor_scan(lt[0:8, :], rb[0:8, :], tmp[0:8, 3 * T:4 * T], 0.0, ALU.mult, ALU.add).then_inc(gate_dve, 1)
                dve.wait_ge(gate_dve, 3)
                for n, dst in enumerate((rb[32:40, :], lt[HD:HD + 8, :], rb[HD + 32:HD + 40, :])):
                    dve.tensor_copy(dst, lt[0:8, :]).then_inc(gate_dve, 1)
                dve.wait_ge(gate_dve, 6)
                ts(rh[:, 0:T], rb[:, :], col("head_mask", 0), None, ALU.mult).then_inc(f_ready, 1)

            def ret_norm_step(s):
                if s % 2 == 1 and 3 <= s <= NRET + 1:
                    p = (s - 3) // 2
                    ro = chunk(proj, PR["rq"] + p)
                    dve.wait_ge(gn_mean, p + 1)
                    tt(ro, ro, banks[5][:, :], ALU.subtract).then_inc(gn_xc, 1)
                if s % 2 == 0 and 4 <= s <= NRET + 2:
                    p = (s - 4) // 2
                    dve.wait_ge(gn_root, p + 1)
                    if p >= 1:
                        dve.wait_ge(gn_t, p)
                    else:
                        dve.wait_ge(rope_done, 8)
                    dve.reciprocal(chunk(xn, 0), banks[6][:, :]).then_inc(gn_rstd, 1)
                    dve.wait_ge(gn_rstd, p + 1)
                    if p >= 1:
                        dve.wait_ge(gn_y, p)
                    stt(chunk(xn, 1), chunk(proj, PR["rq"] + p), col("g_ret_out", p), chunk(xn, 0),
                        ALU.mult, ALU.mult).then_inc(gn_t, 1)
                    dve.wait_ge(gn_t, p + 1)
                    dve.wait_ge(gate_silu, p + 1)
                    tt(chunk(proj, PR["rg"] + p), chunk(xn, 1), chunk(proj, PR["rg"] + p), ALU.mult).then_inc(gn_y, 1)
                if s % 2 == 1 and 5 <= s:
                    p = (s - 5) // 2
                    dve.wait_ge(gn_hi, p + 1)
                    tt(chunk(xl, p), chunk(proj, PR["rg"] + p), chunk(xh, p).bitcast(f32), ALU.subtract).then_inc(gn_lo, 1)

            for s in range(NRET + 1):
                if 1 <= s <= C:
                    dve.wait_ge(unit_used, L["xk"].u0 + s)
                    tt(chunk(kmem, s - 1, M), banks[7][:, 0:M], r_mem[:, :], ALU.mult).then_inc(scaled, 1)
                if s < NRET:
                    dve.wait_ge(dec_in[s % 2], 16 * (s // 2 + 1))
                    dve.wait_ge(ret_scores, s + 1)
                    if s >= 2:
                        dve.wait_ge(ret_pv, s - 1)
                    pt = pt_a if s % 2 == 0 else pt_b
                    for kb in range(QB):
                        b, o, so = CAUSAL_KEYS[kb]
                        w = T - kb * P
                        tt(pt[:, so:so + w], banks[b][:, o:o + w], dec[:, s % 2 * T:s % 2 * T + w],
                           ALU.mult).then_inc(ret_weighted, 1)
                if s == 1:
                    cumulative_forget()
                ret_norm_step(s)

            def next_right_rows(hd):
                if hd + 1 < NFOX:
                    if hd >= 1:
                        dve.wait_ge(fox.s_scores, hd)
                    ts(chunk(rh, (hd + 1) % 2), rb[:, :], col("head_mask", hd + 1), None, ALU.mult).then_inc(f_ready, 1)

            def values_filler(hd):
                if hd < 3:
                    ret_norm_step(NRET + 1 + hd)
                if hd >= 1:
                    if hd == 1:
                        dve.wait_ge(gn_var, 4)
                    if hd >= 3:
                        dve.wait_ge(vmem_tr, hd - 2)
                    dve.wait_ge(unit_used, L["xv"].u0 + hd)
                    tt(chunk(tmp, hd % 2)[:, 0:M], banks[7][:, 0:M], r_mem[:, :], ALU.mult).then_inc(scaled, 1)
            attention(fox, next_right_rows, pair_evac(fox), values_filler)
            dve.wait_ge(gn_y, 4)
            def memory_key_norm(j):
                if j in (2, 4):
                    n = j // 2 - 1
                    dve.wait_ge(kmem_root, n + 1)
                    dve.reciprocal(chunk(xn, n), banks[4 + n][:, :]).then_inc(kmem_rstd, 1)
                elif j in (3, 5):
                    n = j // 2 - 1
                    dve.wait_ge(kmem_rstd, n + 1)
                    for c in range(4 * n, 4 * n + 4):
                        stt(chunk(kmem, c, M), chunk(kmem, c, M), col("g_xk", c % 2), chunk(xn, c // 2, M),
                            ALU.mult, ALU.mult).then_inc(kmem_done, 1)
            residual("out", "xattn", None, (yh, yl), "g_xattn", memory_key_norm)
            norm_recip_of("xattn")
            dve.wait_ge(kmem_done, C)
            dve.wait_ge(norm_r, 3)

            def query_square_sums(pair):
                for n in range(2):
                    dve.wait_ge(qn_sq, 4 * pair + 2 * n + 2)
                    tt(chunk(tmp, 2 * n), chunk(tmp, 2 * n), chunk(tmp, 2 * n + 1), ALU.add).then_inc(qn_pair, 1)

            def query_recips(pair):
                dve.wait_ge(qn_root, pair + 1)
                dve.reciprocal(qrec[:, 8 * pair:8 * pair + 8], qroot[:, 8 * pair:8 * pair + 8]).then_inc(qn_rstd, 1)

            def query_norm(n):
                dve.wait_ge(qn_bc, n + 1)
                for d in range(2):
                    x = chunk(xq, 2 * n + d)
                    stt(x, x, col("g_xq", d), banks[XAT_NORM_BANKS[n]][:, :], ALU.mult, ALU.mult).then_inc(qn_done, 1)

            def later_recips(hd):
                if hd == 1:
                    query_recips(1)

            def later_queries(hd):
                if hd == 1:
                    query_norm(2)
                    query_norm(3)
            scale_units("xq", lambda j: chunk(xq, j), last=5)
            query_square_sums(0)
            scale_units("xq", lambda j: chunk(xq, j), first=5, last=6)
            query_recips(0)
            scale_units("xq", lambda j: chunk(xq, j), first=6, last=7)
            query_norm(0)
            scale_units("xq", lambda j: chunk(xq, j), first=7)
            query_norm(1)
            query_square_sums(1)

            def xat_evac(hd):
                for d in range(2):
                    c = 2 * hd + d
                    dve.wait_ge(xat.s_hi, c + 1)
                    tt(chunk(yl, c), banks[6 + d][:, :], chunk(yh, c).bitcast(f32), ALU.subtract).then_inc(xat.s_lo, 1)
            attention(xat, None, xat_evac, later_recips, later_queries)
            residual("xo", "ffn", None, (xh, xl), "g_ffn")
            norm_recip_of("ffn")
            dve.wait_ge(norm_r, 4)
            pairs("gu", (hh, hl), ada_group)
            ada_group(11, False)
            dve.wait_ge(ada_sum, ADA_G)
            o = VEC["b_ada"][0]
            tt(mods[:, :], banks[7][:, 0:NMOD * C], vec[:, o:o + NMOD * C], ALU.add).then_inc(mods_done, 1)
            dve.wait_ge(mods_done, 1)
            for m, gname in enumerate(("g_ffn1_2", "g_mix_2", "g_ffn2_2")):
                go = VEC[gname][0]
                stt(gmod[:, m * C:(m + 1) * C], mods[:, (3 * m + 1) * C:(3 * m + 2) * C], 1.0, vec[:, go:go + C],
                    ALU.add, ALU.mult).then_inc(mods_done, 1)
            for m in (0, 2):
                ts(gmod[:, (3 + m) * C:(4 + m) * C], mods[:, (3 * m + 2) * C:(3 * m + 3) * C], 0.5, None,
                   ALU.mult).then_inc(mods_done, 1)
            residual("down", "ffn1_2")
            dve.wait_ge(mods_done, 6)
            norm_shifted("ffn1_2", (xh, xl), lambda c: gm(0, c), 0)
            pairs("gu1", (hh, hl))
            residual("down1", "mix_2", lambda j: gm(3, j))
            norm_shifted("mix_2", (xh, xl), lambda c: gm(1, c), 3)
            dve.wait_ge(ada_step, 8 * ADA_G)
            for n in range(2):
                dve.memset(cpad[:, n * 514:n * 514 + 2], 0.0).then_inc(setup_done, 1)
            dve.wait_ge(norm_lo, HI_BASE["mix_2"] + C)
            rope(qkv, 0, 2)
            rope(qkv, 4, 4)
            dve.wait_ge(setup_done, 11)
            pairs("cu")
            dve.wait_ge(convolved, 3 * C)
            rope(qkv, 8, 4)
            for g in range(C):
                dve.wait_ge(unit_used, L["b"].u0 + g + 1)
                dve.wait_ge(half_lo, HALVES["b"] + g - 1)
                tt(chunk(tmp, 2 + g % 2), banks[g % 4][:, :], chunk(conv, g), ALU.mult).then_inc(prod, 1)
                dve.wait_ge(half_hi, HALVES["b"] + g + 1)
                tt(chunk(yl, g), chunk(tmp, 2 + g % 2), chunk(yh, g).bitcast(f32), ALU.subtract).then_inc(half_lo, 1)

            def conv_filler(hd):
                if hd % 2 == 0 and hd >= 2:
                    g = hd // 2 - 1
                    dve.wait_ge(acted, ACTED["cz"] + g + 1)
                    tt(chunk(m1, g), chunk(tmp, g % 2), banks[2][:, :], ALU.mult).then_inc(prod, 1)
            attention(swa, None, pair_evac(swa), conv_filler)
            pairs("az", (yh, yl))
            residual("out2", "ffn2_2", lambda j: mod(5, j))
            norm_shifted("ffn2_2", (xh, xl), lambda c: gm(2, c), 6)
            pairs("gu2", (hh, hl))
            residual("down2", "final", lambda j: gm(5, j))
            norm_recip_of("final")
            dve.wait_ge(norm_bc, NORMS["final"] + 1)
            for c in range(C):
                stt(chunk(h, c), chunk(h, c), col("g_final", c), banks[7][:, :], ALU.mult, ALU.mult).then_inc(final_done, 1)

        @block.tensor
        def _(pe):
            mm = nc.tensor.matmul
            bank_free = {}

            def take(b):
                if b in bank_free:
                    for s, v in bank_free.pop(b):
                        pe.wait_ge(s, v)

            def tile_product(slot, t, bank, rhs, n):
                o = slot * UNIT + t * P
                wh, wl = whi[:, o:o + P], wlo[:, o:o + P]
                rh_, rl_ = chunk(rhs[0], t, n), chunk(rhs[1], t, n)
                mm(bank[:, 0:n], wh, rh_, start=t == 0, stop=False)
                mm(bank[:, 0:n], wh, rl_, start=False, stop=False)
                return mm(bank[:, 0:n], wl, rh_, start=False, stop=t == 7)

            def unit_product(u, slot, bank, rhs, n, ready=None):
                if ready:
                    pe.wait_ge(lo_ready, u + 1)
                    for t in range(8):
                        if ready[1] + t + 1 > 0:
                            pe.wait_ge(ready[0], ready[1] + t + 1)
                        last = tile_product(slot, t, bank, rhs, n)
                else:
                    pe.wait_ge(hi_ready, u + 1)
                    high_passes(slot, range(8), bank, rhs, n)
                    pe.wait_ge(lo_ready, u + 1)
                    last = low_pass(slot, bank, rhs, n)
                last.then_inc(unit_used, 1)

            def high_passes(slot, ts, bank, rhs, n):
                for t in ts:
                    wh = whi[:, slot * UNIT + t * P:slot * UNIT + (t + 1) * P]
                    mm(bank[:, 0:n], wh, chunk(rhs[0], t, n), start=t == 0, stop=False)
                    mm(bank[:, 0:n], wh, chunk(rhs[1], t, n), start=False, stop=False)

            def low_pass(slot, bank, rhs, n):
                for t in range(8):
                    last = mm(bank[:, 0:n], wlo[:, slot * UNIT + t * P:slot * UNIT + (t + 1) * P], chunk(rhs[0], t, n),
                              start=False, stop=t == 7)
                return last

            def half_unit(u, slot, bank, rhs, n, half):
                if half == 0:
                    pe.wait_ge(hi_ready, u + 1)
                    high_passes(slot, range(6), bank, rhs, n)
                else:
                    high_passes(slot, (6, 7), bank, rhs, n)
                    pe.wait_ge(lo_ready, u + 1)
                    low_pass(slot, bank, rhs, n).then_inc(unit_used, 1)

            paced = [(0, 0)] + [p for t in range(7) for p in ((0, t + 1), (1, t))] + [(1, 7)]

            def held(late):
                return ([(0, t) for t in range(late)], [(1, t) for t in range(4)],
                        [(0, t) for t in range(late, 8)] + [(1, t) for t in range(4, 8)])

            def two_units(u, rhs, ready, order, awaiting=(0, 1)):
                for m, t in order:
                    if t == 0:
                        take(m)
                        pe.wait_ge(lo_ready, u + m + 1)
                    if m in awaiting and ready[1] + t + 1 > 0:
                        pe.wait_ge(ready[0], ready[1] + t + 1)
                    last = tile_product((u + m) % 2, t, banks[m], rhs[m], T)
                    if t == 7:
                        last.then_inc(unit_used, 1)

            def dense(name, rhs, n, free, ready=None, together=None, begun=False, hooks=None, after_second=None):
                lay = L[name]
                sem_free, base = free
                ring = 4 // lay.per
                hooks = hooks or {}

                def body(i, first):
                    if first and together:
                        two_units(lay.u0, [rhs[0], rhs[-1]], *together)
                    if first and (together or begun) and 1 in hooks:
                        hooks[1]()
                    for j in range(2 if first and (together or begun) else 0, 4):
                        if j % lay.per == 0:
                            if first:
                                for b in range(j, j + lay.per):
                                    take(b)
                            else:
                                g = (4 * i + j) if lay.per == 1 else 2 * i + j // 2
                                pe.wait_ge(sem_free, base + g - ring + 1)
                        unit_product(lay.u0 + j + 4 * i, (lay.u0 + j) % 2, banks[j], rhs[j % lay.per], n,
                                     ready if first and j == 0 else None)
                        if isinstance(i, int) and 4 * i + j in hooks:
                            hooks[4 * i + j]()
                        if j == 1 and after_second and not first:
                            after_second(i - 1)
                if lay.n >= 4:
                    repeat(pe, lay.n // 4, body)
                else:
                    for j in range(lay.n):
                        take(j)
                        unit_product(lay.u0 + j, (lay.u0 + j) % 2, banks[j], rhs[0], n)
                for b in range(min(4, lay.n)):
                    bank_free[b] = [(sem_free, base + lay.groups - ring + b // lay.per + 1)] if lay.n >= 4 else [
                        (sem_free, base + b + 1)]

            def down(name, ready_value, extra=None):
                lay = L[name]
                n_half = FC // 2
                for half in range(2):
                    for b in range(4):
                        take(DOWN_BANKS[name][4 * half + b])
                    if half == 0:
                        pe.wait_ge(half_lo, ready_value - 2)

                    def unit(u, par, k0, first, last_unit):
                        if last_unit and half == 0:
                            pe.wait_ge(half_lo, ready_value)
                        pe.wait_ge(lo_ready, u + 1)
                        order = [(kk, o) for o in range(4) for kk in range(2)] if last_unit else [
                            (kk, o) for kk in range(2) for o in range(4)]
                        for kk, o in order:
                            w0 = par * UNIT + (4 * kk + o) * P
                            wh, wl = whi[:, w0:w0 + P], wlo[:, w0:w0 + P]
                            rh_, rl_ = chunk(hh, k0 + kk), chunk(hl, k0 + kk)
                            bank = banks[DOWN_BANKS[name][4 * half + o]]
                            mm(bank[:, :], wh, rh_, start=first and kk == 0, stop=False)
                            mm(bank[:, :], wh, rl_, start=False, stop=False)
                            done = mm(bank[:, :], wl, rh_, start=False, stop=last_unit and kk == 1)
                            if last_unit and kk == 1 and o < 3:
                                done.then_inc(down_out, 1)
                        done.then_inc(unit_used, 1)
                    u0 = lay.u0 + n_half * half
                    for j in range(3):
                        unit(u0 + j, (u0 + j) % 2, 2 * j, j == 0, False)
                    if half == 0 and extra:
                        extra[0]()
                    with pe.Fori(0, (n_half - 5) // 2) as i:
                        for j in range(2):
                            unit(u0 + 3 + j + 2 * i, (u0 + 3 + j) % 2, 6 + 2 * j + 4 * i, False, False)
                    if half == 0 and extra:
                        extra[1]()
                    unit(u0 + n_half - 2, (u0 + n_half - 2) % 2, 2 * (n_half - 2), False, False)
                    unit(u0 + n_half - 1, (u0 + n_half - 1) % 2, 2 * (n_half - 1), False, True)
                for j, b in enumerate(DOWN_BANKS[name]):
                    bank_free[b] = [(resid, RESID[name] + j + 1)]

            def norm_columns(name, n_blocks=QB, bank=7):
                i = NORMS[name]
                take(bank)
                pe.wait_ge(norm_acc, 6 * i + 6)
                pe.wait_ge(norm_sq, 8 * i + 8)
                for j in range(n_blocks):
                    mm(banks[bank][:, j:j + 1], ssum[:, j * P:(j + 1) * P], mean_d[:, 0:1], start=True, stop=False)
                    last = mm(banks[bank][:, j:j + 1], tmp[:, 3 * T + j * P:3 * T + (j + 1) * P], mean_d[:, 0:1],
                              start=False, stop=True)
                last.then_inc(norm_cols, 1)

            def norm_spread(name, n_blocks=QB, bank=7, free=None):
                i = NORMS[name]
                pe.wait_ge(norm_recip, i + 1)
                for j in range(n_blocks):
                    last = mm(banks[bank][:, j * P:(j + 1) * P], rcol[:, 4 + j:5 + j].broadcast_to([P, P]), ident,
                              start=True, stop=True)
                last.then_inc(norm_bc, 1)
                if free:
                    bank_free[bank] = [free]

            def head_sums(b):
                for c in range(4):
                    take(4 + c)
                    pe.wait_ge(hn_sq, b + c + 1)
                    mm(banks[4 + c][:, :], mean_head, chunk(tmp, c), start=True, stop=True).then_inc(hn_sum, 1)
                    bank_free[4 + c] = [(hn_rstd, b + c + 1)]

            rope_n = [0]

            def rope(buf, c0, n, ready):
                pe.wait_ge(*ready)
                for c in range(n):
                    take(4 + c)
                    mm(banks[4 + c][:, :], table("rot"), chunk(buf, c0 + c), start=True, stop=True).then_inc(rope_rot, 1)
                    rope_n[0] += 1
                    bank_free[4 + c] = [(rope_sin, rope_n[0])]

            def values_to_tokens(c0, ready, b, b0):
                pe.wait_ge(scaled, ready)
                for s in range(QB):
                    take(b0 + s)
                    for c in range(4):
                        last = nc.tensor.transpose(banks[b0 + s][:, c * P:(c + 1) * P],
                                                   proj[:, (c0 + c) * T + s * P:(c0 + c) * T + (s + 1) * P], ident)
                    last.then_inc(v_tr, 1)
                    bank_free[b0 + s] = [(v_copied, b + s + 1)]

            def all_banks_taken():
                for b in list(bank_free):
                    take(b)

            def attention(k, scores, transposes, weighted, evacuated, before=None, fill=None):
                all_banks_taken()
                for hd in range(k.heads + 1):
                    if hd < k.heads:
                        if hd >= 1:
                            pe.wait_ge(k.s_exp, 4 * hd)
                        scores(hd).then_inc(k.s_scores, 1)
                    if before:
                        before(hd)
                    if fill:
                        fill(hd, 0)
                    if hd >= 1:
                        d = hd - 1
                        pe.wait_ge(k.s_pn, 4 * d + 4)
                        if d >= 1:
                            pe.wait_ge(k.s_pt_act, d)
                            pe.wait_ge(k.s_pt_dve, d * (len(k.key_banks) - 1))
                        transposes(d).then_inc(k.s_tr, 1)
                    if fill:
                        fill(hd, 1)
                    if hd >= 1:
                        pe.wait_ge(k.s_pt_act, d + 1)
                        pe.wait_ge(k.s_pt_dve, (d + 1) * (len(k.key_banks) - 1))
                        evacuated(d)
                        weighted(d).then_inc(k.s_pv, 1)

            def pair_out_free(k):
                def f(hd):
                    n = len(k.out_banks)
                    if hd % 2 == 0 and hd >= 2 * n:
                        pe.wait_ge(k.s_lo, hd // 2 - n + 1)
                return f

            X, Y = (xh, xl), (yh, yl)
            sc = scaled

            def spread_hooks(name):
                return {1: lambda: norm_columns(name), 2: lambda: norm_spread(name, free=(norm_r, NORMS[name] + 1))}

            def wait_consts_then_columns():
                pe.wait_ge(consts_in, 32)
                norm_columns("mix")
            dense("fq", [X], T, (sc, SCALED["fq"]), together=((norm_lo, 0), paced),
                  hooks={1: wait_consts_then_columns, 2: lambda: norm_spread("mix", free=(norm_r, 1))})
            dense("fk", [X], T, (sc, SCALED["fk"]))
            head_sums(0)
            dense("rq", [X], T, (sc, SCALED["rq"]))
            head_sums(4)
            dense("rk", [X], T, (sc, SCALED["rk"]))
            dense("rv", [X], T, (sc, SCALED["rv"]))
            dense("rg", [X], T, (sc, SCALED["rg"]), hooks={1: lambda: norm_columns("mem", 2, 4),
                                                           3: lambda: norm_spread("mem", 2, 4, (norm_r, 2))})
            rope(proj, PR["rq"], 4, (sc, SCALED["rq"] + 4))
            dense("fv", [X], T, (sc, SCALED["fv"]))
            rope(proj, PR["rk"], 4, (sc, SCALED["rk"] + 4))
            dense("ff", [X], T, (sc, SCALED["ff"]))
            values_to_tokens(PR["rv"], SCALED["rv"] + 4, 0, 4)
            values_to_tokens(PR["fv"], SCALED["fv"] + 4, 4, 0)

            all_banks_taken()
            pe.wait_ge(rope_done, 8)
            pe.wait_ge(v_copied, 4)

            def causal_values(k_pt, c0, hd, bank):
                r0 = hd % 2 * HD
                for kb in range(QB):
                    so, w = CAUSAL_KEYS[kb][2], T - kb * P
                    vv = (c0 + kb) * T + hd * HD
                    last = mm(bank[r0:r0 + HD, kb * P:T], proj[:, vv:vv + HD],
                              k_pt[:, so:so + w], start=kb == 0, stop=kb == QB - 1)
                return last

            def ret_norm_step(s):
                if s % 2 == 1 and 3 <= s <= NRET + 1:
                    p = (s - 3) // 2
                    pe.wait_ge(ret_out, p + 1)
                    if p >= 1:
                        pe.wait_ge(gn_xc, p)
                    mm(banks[5][:, :], mean_head, chunk(proj, PR["rq"] + p), start=True, stop=True).then_inc(gn_mean, 1)
                if s % 2 == 0 and 4 <= s <= NRET + 2:
                    p = (s - 4) // 2
                    pe.wait_ge(gn_sq, p + 1)
                    if p >= 1:
                        pe.wait_ge(gn_rstd, p)
                    mm(banks[6][:, :], mean_head, chunk(tmp, p), start=True, stop=True).then_inc(gn_var, 1)

            for s in range(NRET + 1):
                if s < NRET:
                    if s >= 1:
                        pe.wait_ge(ret_weighted, 4 * s)
                    r0, c = s % 2 * HD, s // 2
                    for kb in range(QB):
                        b, o, _ = CAUSAL_KEYS[kb]
                        w = T - kb * P
                        kk = (PR["rk"] + c) * T + kb * P
                        qq = (PR["rq"] + c) * T
                        last = mm(banks[b][:, o:o + w], proj[r0:r0 + HD, kk:kk + P], proj[r0:r0 + HD, qq + kb * P:qq + T],
                                  start=True, stop=True)
                    last.then_inc(ret_scores, 1)
                if 1 <= s <= NRET:
                    hd = s - 1
                    pe.wait_ge(ret_weighted, 4 * s)
                    if hd % 2 == 0 and hd >= 4:
                        pe.wait_ge(ret_out, hd // 2 - 1)
                    causal_values(pt_a if hd % 2 == 0 else pt_b, PR["rv"], hd, banks[3 + hd // 2 % 2]).then_inc(ret_pv, 1)
                ret_norm_step(s)
                if s < C:
                    if s == 0:
                        pe.wait_ge(norm_lo, HI_BASE["mem"] + C)
                    else:
                        pe.wait_ge(sc, SCALED["xk"] + s)
                    u = L["xk"].u0 + s
                    unit_product(u, u % 2, banks[7], (memh, meml), M)
            bank_free[7] = [(sc, SCALED["xk"] + C)]
            bank_free[3] = [(ret_out, 3)]
            bank_free[4] = [(ret_out, 4)]

            pe.wait_ge(hn_done, 8)
            pe.wait_ge(v_copied, 8)

            def fox_scores(hd):
                r0, c = hd % 2 * HD, hd // 2
                pe.wait_ge(f_ready, hd + 1)
                for q, b, o, w, _ in FOX_GROUPS:
                    qq = (PR["fq"] + c) * T + q * P
                    kk = (PR["fk"] + c) * T
                    out = banks[b][:, o:o + w]
                    mm(out, proj[r0:r0 + HD, qq:qq + P], proj[r0:r0 + HD, kk:kk + w], start=True, stop=False)
                    mm(out, lt[r0:r0 + HD, q * P:(q + 1) * P], rh[r0:r0 + HD, hd % 2 * T:hd % 2 * T + w],
                       start=False, stop=True)
                    last = mm(banks[b][:, o + w - P:o + w], mask16[:, 0:P], mask16[:, 2 * P:3 * P],
                              start=False, stop=True, skip_group_check=True)
                return last

            def fox_transposes(hd):
                if hd == 0:
                    pe.wait_ge(gn_xc, 4)
                for kb in range(QB):
                    b, o, _ = CAUSAL_KEYS[kb]
                    for q, _, _, _, po in FOX_GROUPS:
                        if q >= kb:
                            oo = o + (q - kb) * P
                            last = nc.tensor.transpose(banks[3 + b][:, oo:oo + P], fox.p[hd % 2][:, po + kb * P:po + (kb + 1) * P], ident)
                return last

            def memory_values_to_tokens(hd):
                if hd == 0:
                    ret_norm_step(NRET + 1)
                if hd >= 1:
                    pe.wait_ge(sc, SCALED["xv"] + hd)
                    for m in range(2):
                        last = nc.tensor.transpose(banks[7][:, M + m * P:M + (m + 1) * P],
                                                   tmp[:, hd % 2 * T + m * P:hd % 2 * T + (m + 1) * P], ident)
                    last.then_inc(vmem_tr, 1)

            def fox_out_free(hd):
                if hd == 0:
                    pe.wait_ge(gn_rstd, 4)
                pair_out_free(fox)(hd)

            fox_first = held(7)

            def memory_values_unit(hd, half):
                if hd == NFOX:
                    if half == 0:
                        pe.wait_ge(fox.s_exp, 4 * NFOX)
                        pe.wait_ge(gn_lo, 4)
                    two_units(L["out"].u0, [X, X], (fox.s_lo, -4), fox_first[half])
                if hd < C:
                    if hd >= 1 and half == 0:
                        pe.wait_ge(vmem_copied, hd)
                    u = L["xv"].u0 + hd
                    half_unit(u, u % 2, banks[7], (memh, meml), M, half)
                if hd == 0 and half == 1:
                    ret_norm_step(NRET + 2)
            attention(fox, fox_scores, fox_transposes, lambda hd: causal_values(pt_fox, PR["fv"], hd, banks[6]),
                      fox_out_free, memory_values_to_tokens, memory_values_unit)
            bank_free[6] = [(fox.s_lo, 4)]
            bank_free[7] = [(vmem_copied, C)]
            for b in (0, 1, 2):
                bank_free[b] = [(fox.s_exp, 4 * NFOX)]
            for b in (3, 4, 5):
                bank_free[b] = [(fox.s_pt_act, NFOX), (fox.s_pt_dve, 2 * NFOX)]
            def memory_key_sums():
                for hd in range(NX):
                    if hd % 2 == 0:
                        take(4 + hd // 2)
                    for d in range(2):
                        pe.wait_ge(kmem_sq, 2 * hd + d + 1)
                        last = mm(banks[4 + hd // 2][:, hd % 2 * M:(hd % 2 + 1) * M], mean_256, chunk(tmp, 2 * hd + d, M),
                                  start=d == 0, stop=d == 1)
                    last.then_inc(kmem_sum, 1)
                for n in range(2):
                    bank_free[4 + n] = [(kmem_rstd, n + 1)]
            two_units(L["out"].u0, [X, X], (fox.s_lo, -4), fox_first[2])
            dense("out", [X], T, (resid, RESID["out"]), begun=True, hooks={1: memory_key_sums})

            def query_columns(pair):
                take(6 + pair)
                pe.wait_ge(qn_pair, 2 * pair + 2)
                for n in range(2):
                    for q in range(QB):
                        last = mm(banks[6 + pair][:, QB * n + q:QB * n + q + 1],
                                  tmp[:, 2 * n * T + q * P:2 * n * T + (q + 1) * P], mean_256[:, 0:1], start=True, stop=True)
                last.then_inc(qn_sum, 1)
                bank_free[6 + pair] = [(qn_root, pair + 1)]

            def query_spread(pair):
                pe.wait_ge(qn_rstd, pair + 1)
                for hd in (2 * pair, 2 * pair + 1):
                    b = XAT_NORM_BANKS[hd]
                    take(b)
                    for q in range(QB):
                        last = mm(banks[b][:, q * P:(q + 1) * P], qrec[:, 4 * hd + q:4 * hd + q + 1].broadcast_to([P, P]),
                                  ident, start=True, stop=True)
                    last.then_inc(qn_bc, 1)
                    bank_free[b] = [(qn_done, 2 * hd + 2)]
            hooks = spread_hooks("xattn")
            hooks[5] = lambda: query_columns(0)
            hooks[6] = lambda: query_spread(0)
            dense("xq", [Y], T, (sc, SCALED["xq"]), together=((norm_lo, HI_BASE["xattn"]), sum(held(7), [])), hooks=hooks)
            pe.wait_ge(kmem_done, C)
            pe.wait_ge(vmem_copied, C)

            def xat_scores(hd):
                pe.wait_ge(qn_done, 2 * hd + 2)
                for q, b, o, w, _ in XAT_GROUPS:
                    for d in range(2):
                        c = 2 * hd + d
                        last = mm(banks[b][:, o:o + w], xq[:, c * T + q * P:c * T + (q + 1) * P], chunk(kmem, c, M),
                                  start=d == 0, stop=d == 1)
                return last

            def xat_transposes(hd):
                for kb in range(2):
                    for q in range(QB):
                        last = nc.tensor.transpose(banks[3 + kb][:, q * P:(q + 1) * P],
                                                   xat.p[hd % 2][:, q * M + kb * P:q * M + (kb + 1) * P], ident)
                return last

            def xat_values(hd):
                for d in range(2):
                    o = (2 * hd + d) * P
                    for kb in range(2):
                        last = mm(banks[6 + d][:, :], vmem[:, kb * D + o:kb * D + o + P], xat.pt[:, kb * T:(kb + 1) * T],
                                  start=kb == 0, stop=kb == 1)
                return last

            def xat_out_free(hd):
                if hd == 0:
                    pe.wait_ge(qn_root, 2)
                if hd >= 1:
                    pe.wait_ge(xat.s_lo, 2 * hd)

            def later_query_norms(hd):
                if hd == 0:
                    query_columns(1)
                if hd == 1:
                    bank_free[5] = [(qn_done, 4)]
                    query_spread(1)
            bank_free.pop(5)

            xat_first = held(6)

            def first_out_units(hd, half):
                if hd == NX:
                    if half == 0:
                        pe.wait_ge(xat.s_exp, 4 * NX)
                    two_units(L["xo"].u0, [Y, Y], (xat.s_lo, 0), xat_first[half])
            attention(xat, xat_scores, xat_transposes, xat_values, xat_out_free, later_query_norms, first_out_units)
            for b in (0, 1):
                bank_free[b] = [(xat.s_exp, 4 * NX)]
            bank_free[3], bank_free[4] = [(xat.s_pt_act, NX)], [(xat.s_pt_dve, NX)]
            bank_free[6] = bank_free[7] = [(xat.s_lo, 8)]
            two_units(L["xo"].u0, [Y, Y], (xat.s_lo, 0), xat_first[2])
            dense("xo", [Y], T, (resid, RESID["xo"]), begun=True)

            def ada_sums(g):
                for n in range(ADA_B):
                    o = g * ADA_B + n
                    if n == 0:
                        pe.wait_ge(ada_step, 8 * g + 8)
                    dst = banks[7][:, o:o + 1] if isinstance(o, int) else banks[7][:, bass.ds(o, 1)]
                    last = mm(dst, acc[:, n * P:(n + 1) * P], col("one"), start=True, stop=True)
                last.then_inc(ada_sum, 1)
            dense("gu", [X, X], T, (up_scaled, 0), together=((norm_lo, HI_BASE["ffn"]), sum(held(7), [])),
                  hooks=spread_hooks("ffn"),
                  after_second=ada_sums)
            bank_free[7] = [(mods_done, 1)]
            down("down", HALVES["gu"] + FC, (lambda: ada_sums(10), lambda: ada_sums(11)))

            def shifted_norm(name):
                norm_columns(name)
                norm_spread(name, free=(norm_xn, 8 * SHIFTED[name] + C))
            shifted_norm("ffn1_2")
            dense("gu1", [X, X], T, (prod, PROD["gu1"]), together=((norm_lo, HI_BASE["ffn1_2"]), paced))
            down("down1", HALVES["gu1"] + FC)
            shifted_norm("mix_2")
            dense("kv", [X], T, (copied, COPIED["kv"]), together=((norm_lo, HI_BASE["mix_2"]), paced))
            dense("qa", [X], T, (copied, COPIED["qa"]))
            rope(qkv, 0, 2, (copied, COPIED["kv"] + 2))
            for n in range(2):
                take(6 + n)
                if n == 0:
                    pe.wait_ge(copied, COPIED["kv"] + 4)
                for s in range(2):
                    for c in range(2):
                        last = nc.tensor.transpose(banks[6 + n][:, s * 2 * P + c * P:s * 2 * P + (c + 1) * P],
                                                   qkv[:, (2 + c) * T + (2 * n + s) * P:(2 + c) * T + (2 * n + s + 1) * P], ident)
                last.then_inc(vsw_tr, 1)
                bank_free[6 + n] = [(vsw_copied, n + 1)]
            dense("qb", [X], T, (copied, COPIED["qb"]))
            rope(qkv, 4, 4, (copied, COPIED["qa"] + 4))
            dense("cu", [X, X], T, (prod, PROD["cu"]))
            rope(qkv, 8, 4, (copied, COPIED["qb"] + 4))
            dense("b", [X], T, (prod, PROD["b"]))

            pe.wait_ge(kdup_in, 16 * 2 * NKV)
            pe.wait_ge(rope_done, 18)

            def swa_scores(hd):
                r0, g = hd % 2 * HD, hd // (NSW // NKV)
                for q, b, o, w, _ in SWA_GROUPS:
                    qq = (4 + hd // 2) * T + q * P
                    k0 = g * T + (q + 1) * P - w
                    mm(banks[b][:, o:o + w], qkv[r0:r0 + HD, qq:qq + P], kdup[r0:r0 + HD, k0:k0 + w], start=True, stop=False)
                    last = mm(banks[b][:, o:o + w], mask16[:, 0:P], mask16[:, 3 * P - w:3 * P], start=False, stop=True)
                return last

            def swa_transposes(hd):
                for n, (q, kb) in enumerate(SWA_PAIRS):
                    last = nc.tensor.transpose(banks[3 + n // 4][:, n % 4 * P:(n % 4 + 1) * P], swa.p[hd % 2][:, n * P:(n + 1) * P], ident)
                return last

            def swa_values(hd):
                r0, g = hd % 2 * HD, hd // (NSW // NKV)
                bank = banks[6 + hd // 2 % 2]
                for n, (q, kb) in enumerate(SWA_PAIRS):
                    last = mm(bank[r0:r0 + HD, q * P:(q + 1) * P], v_sw[:, kb * 256 + g * HD:kb * 256 + (g + 1) * HD],
                              swa.pt[:, n * P:(n + 1) * P], start=q == 0 or kb < q, stop=kb == q)
                return last

            swa_first = held(7)

            def conv_unit(hd, half):
                if hd == NSW:
                    if half == 0:
                        pe.wait_ge(swa.s_exp, 4 * NSW)
                    two_units(L["az"].u0, [(oh, ol), X], (swa.s_lo, 0), swa_first[half], (0,))
                if hd < NSW:
                    if hd == 0 and half == 0:
                        pe.wait_ge(half_lo, HALVES["b"] + C)
                    if hd >= 2 and half == 0:
                        pe.wait_ge(prod, PROD["cz"] + hd // 2)
                    u = L["cz"].u0 + hd
                    half_unit(u, u % 2, banks[5 if hd % 2 else 2], X if hd % 2 else Y, T, half)
            attention(swa, swa_scores, swa_transposes, swa_values, pair_out_free(swa), fill=conv_unit)
            bank_free[2] = bank_free[5] = [(prod, PROD["cz"] + C)]
            for b in (0, 1):
                bank_free[b] = [(swa.s_exp, 4 * NSW)]
            bank_free[3], bank_free[4] = [(swa.s_pt_act, NSW)], [(swa.s_pt_dve, NSW)]
            bank_free[6] = bank_free[7] = [(swa.s_lo, 8)]
            two_units(L["az"].u0, [(oh, ol), X], (swa.s_lo, 0), swa_first[2], (0,))
            dense("az", [(oh, ol), X], T, (prod, PROD["az"]), begun=True)
            dense("out2", [Y], T, (resid, RESID["out2"]), ready=(half_lo, HALVES["az"]))
            shifted_norm("ffn2_2")
            dense("gu2", [X, X], T, (prod, PROD["gu2"]), together=((norm_lo, HI_BASE["ffn2_2"]), paced))
            down("down2", HALVES["gu2"] + FC)
            norm_columns("final")
            norm_spread("final")


def constants():
    d = np.arange(P)
    rot = np.zeros((P, P), np.float32)
    for m in range(P):
        if m % HD < HD // 2:
            rot[m + HD // 2, m] = -1.0
        else:
            rot[m - HD // 2, m] = 1.0
    same_head = (d[:, None] // HD == d[None, :] // HD)
    row, colm = d[:, None], d[None, :]
    window = np.concatenate([np.where(colm > row, 0.0, NEG), np.where(colm <= row, 0.0, NEG)], 1)
    inv = (10000.0 ** (-np.arange(0, HD, 2, dtype=np.float32) / np.float32(HD))).astype(np.float32)
    ang = (inv[d % (HD // 2)][:, None] * np.arange(T, dtype=np.float32)[None, :]).astype(np.float32)
    tables = np.concatenate([np.eye(P), rot, np.full((P, P), 1.0 / D), same_head / HD, np.full((P, P), 1.0 / 256),
                             np.cos(ang), np.sin(ang), window], 1).astype(np.float32)
    assert tables.shape == (P, NTAB)
    log_g = np.log(np.float32(1.0) - np.float32(2.0) ** (-5.0 - np.arange(NRET, dtype=np.float32))).astype(np.float32)
    s, t = np.arange(P)[:, None], np.arange(T)[None, :]
    seen = t // CHUNK >= s // CHUNK
    decays = np.stack([np.where(seen, np.exp(g * np.abs(t - s)), 0.0) * HD ** -0.5 for g in log_g]).astype(np.float32)
    return tables, decays


def column_units(w):
    return w.reshape(C, P, -1, P).transpose(2, 1, 0, 3).reshape(-1, P, UNIT)


def row_units(w):
    return w.reshape(FC // 2, 2, P, 2, 4, P).transpose(3, 0, 2, 1, 4, 5).reshape(-1, P, UNIT)


def interleave(a, b):
    return np.stack([a, b], 1).reshape(-1, P, UNIT)


def lay_out(i):
    def fm(v):
        return np.asarray(v).reshape(-1, P).T

    def split(w, sizes):
        at, out = 0, []
        for n in sizes:
            out.append(w[:, at:at + n])
            at += n
        return out
    rq, rk, rv, rg, fq, fk, fv, ff = split(i["w_in"][0], [512] * 7 + [8])
    ffp = np.zeros((D, P), np.float32)
    ffp[:, 0:8] = ff
    xk, xv = split(i["w_xkv"][0], [D, D])
    b2, c2, u2, q2, k2, v2, zc, za = split(i["w_in_2"][0], [D, D, D, D, 256, 256, D, D])
    cu_ = column_units
    gate, up = cu_(i["w_gate"][0]), cu_(i["w_up"][0])
    g1, p1 = (cu_(w) for w in split(i["w1_gu_2"][0], [FF, FF]))
    g2, p2 = (cu_(w) for w in split(i["w2_gu_2"][0], [FF, FF]))
    parts = [cu_(w) for w in (fq, fk, rq, rk, rv, rg, fv, ffp, xk, xv, i["w_out"][0], i["w_xq"][0], i["w_xo"][0])]
    parts += [interleave(gate, up), row_units(i["w_down"][0]), interleave(g1, p1), row_units(i["w1_down_2"][0]),
              cu_(k2), cu_(v2), cu_(q2), interleave(cu_(c2), cu_(u2)), cu_(b2),
              interleave(cu_(i["w_conv_proj_2"][0]), cu_(zc)), interleave(cu_(i["w_attn_proj_2"][0]), cu_(za)),
              cu_(i["w_out_2"][0]), interleave(g2, p2), row_units(i["w2_down_2"][0])]
    units = np.concatenate(parts, 0)
    assert units.shape == (UNITS, P, UNIT), units.shape
    head_mask = np.zeros((P, 8), np.float32)
    for r in range(P):
        if r % 32 < 8:
            head_mask[r, r % 32] = 1.0
    bf = np.zeros((P, 1), np.float32)
    bf[0:8, 0] = i["b_forget"][0]
    cols = {"g_mem": fm(i["g_mem"][0]), "g_mix": fm(i["g_mix"][0]), "g_xattn": fm(i["g_xattn"][0]),
            "g_ffn": fm(i["g_ffn"][0]), "g_ffn1_2": fm(i["g_ffn1_2"][0]), "g_mix_2": fm(i["g_mix_2"][0]),
            "g_ffn2_2": fm(i["g_ffn2_2"][0]), "g_final": fm(i["g_final_2"]), "g_ret_out": fm(i["g_ret_out"][0].reshape(-1)),
            "g_fox_q": np.tile(i["g_fox_q"][0], 2)[:, None], "g_fox_k": np.tile(i["g_fox_k"][0], 2)[:, None],
            "g_xq": fm(i["g_xq"][0]), "g_xk": fm(i["g_xk"][0]), "b_forget": bf, "conv": fm(i["conv_w_2"][0].reshape(-1)),
            "c": fm(i["c_2"][0]), "b_ada": fm(i["b_ada_2"][0]), "sinks": np.broadcast_to(i["sinks_2"][0][None, :], (P, NSW)),
            "eps": np.full((P, 1), EPS, np.float32), "one": np.ones((P, 1), np.float32), "head_mask": head_mask}
    vectors = np.concatenate([cols[n] for n in VEC], 1)
    assert vectors.shape == (P, NVEC)
    tables, decays = constants()
    out = {"x_t": i["x"][0].T, "mem_t": i["mem"][0].T, "units": units, "w_ada": i["w_ada_2"][0], "vectors": vectors,
           "tables": tables, "decays": decays}
    return {k: np.ascontiguousarray(v) for k, v in out.items()}


def build(nc, arrays):
    aps = {k: nc.dram_tensor(k, list(v.shape), mybir.dt.float32, kind="ExternalInput").ap() for k, v in arrays.items()}
    out_t = nc.dram_tensor("out_t", [D, T], mybir.dt.float32, kind="ExternalOutput").ap()
    two_block_kernel(nc, *[aps[k] for k in ("x_t", "mem_t", "units", "w_ada", "vectors", "tables", "decays")], out_t)


def kernel(**inputs):
    import concourse.bacc as bacc
    from concourse.bass_utils import run_bass_kernel_spmd

    arrays = lay_out({k: np.asarray(v) for k, v in inputs.items()})
    nc = bacc.Bacc("TRN2", target_bir_lowering=False, num_devices=1)
    build(nc, arrays)
    r = run_bass_kernel_spmd(nc, [arrays], core_ids=[0])
    return r.results[0]["out_t"].T[None]
```
